# Optimizing a Trainium2 kernel written in Bass

```python
import math
import jax, jax.numpy as jnp
from jax import lax
import numpy as np

D_MODEL = 1024
BATCH = 1
SEQ = 128
DEPTH = 2
DEC_BATCH = 1
DEC_SEQ = 256
PAST_LEN = 128

GRID_W = 64
MIX_W = 512
HG_HEADS = 4
HG_DK = 128
HG_DV = MIX_W // HG_HEADS
HG_CHUNK = 16
ML_HEADS = 4
ML_DK = 128
ML_DV = MIX_W // ML_HEADS
ML_CHUNK = 64
MB_HEADS = 8
MB_HEADDIM = MIX_W // MB_HEADS
MB_DINNER = MIX_W
MB_GROUPS = 2
MB_DSTATE = 64
MB_CONV = 3
MB_XBC = MB_DINNER + 2 * MB_GROUPS * MB_DSTATE
MB_CHUNK = 64
D_FF = 2816
N_BRANCH = 3
N_MOD = 9
ALPHA = (2 * DEPTH) ** 0.25
BETA = (8 * DEPTH) ** -0.25
LN_EPS = 1e-5
RMS_EPS = 1e-6
IN_SIZES = (HG_HEADS * HG_DK, HG_HEADS * HG_DV, HG_HEADS * HG_DV, 2 * HG_HEADS * HG_DK,
            ML_HEADS * ML_DK, ML_HEADS * ML_DK, ML_HEADS * ML_DV, ML_HEADS * ML_DV, 2 * ML_HEADS, 2 * ML_HEADS,
            MB_DINNER, MB_XBC, 2 * MB_HEADS, N_BRANCH * D_MODEL)
D_IN = sum(IN_SIZES)

kernel_name = 'hybrid_diffusion_prefix_trunk'

def _split_points():
    pts, acc = [], 0
    for s in IN_SIZES[:-1]:
        acc += s
        pts.append(acc)
    return pts

def _causal(t):
    return jnp.tril(jnp.ones((t, t), dtype=bool))

def _layernorm(x, g, b):
    xf = x.astype(jnp.float32)
    mu = jnp.mean(xf, -1, keepdims=True)
    var = jnp.mean(jnp.square(xf - mu), -1, keepdims=True)
    return ((xf - mu) * lax.rsqrt(var + LN_EPS) * g + b).astype(x.dtype)

def _head_rms(x, g):
    xf = x.astype(jnp.float32)
    y = xf * lax.rsqrt(jnp.mean(xf * xf, -1, keepdims=True) + RMS_EPS)
    return y.reshape(x.shape[0], x.shape[1], -1) * g

def _modulate(x, shift, scale):
    return x * (1 + scale) + shift

def _swiglu(x, w_gu, w_down):
    a, b = jnp.split(jnp.einsum('bld,df->blf', x, w_gu), 2, axis=-1)
    return jnp.einsum('blf,fd->bld', jax.nn.silu(a) * b, w_down)

def _dwconv(x, w, b):
    out = lax.conv_general_dilated(x, w[:, None, :], window_strides=(1,), padding='SAME',
                                   dimension_numbers=('NWC', 'WIO', 'NWC'),
                                   feature_group_count=x.shape[-1])
    return out + b

def _state_scan(decay, contrib, s0):
    def step(s, dc):
        d, cn = dc
        return d * s + cn, s
    s_fin, s_in = lax.scan(step, s0, (jnp.moveaxis(decay, 1, 0), jnp.moveaxis(contrib, 1, 0)))
    return jnp.moveaxis(s_in, 0, 1), s_fin

def _bidir(scan_fn, args_f, args_b, state):
    y_f, s_f = scan_fn(*args_f, tuple(s[:, 0] for s in state))
    y_b, s_b = scan_fn(*(jnp.flip(a, 1) for a in args_b), tuple(s[:, 1] for s in state))
    return y_f + jnp.flip(y_b, 1), tuple(jnp.stack([a, b], axis=1) for a, b in zip(s_f, s_b))

def _hgrn2_scan(q, k, v, logf, state):
    (s0,) = state
    bsz, seq, h, dk = q.shape
    t = HG_CHUNK
    n = seq // t
    q, k, logf = [a.astype(jnp.float32).reshape(bsz, n, t, h, dk) for a in (q, k, logf)]
    v = v.astype(jnp.float32).reshape(bsz, n, t, h, HG_DV)
    b = jnp.cumsum(logf, axis=2)
    b_last = b[:, :, -1]
    e = b[:, :, :, None] - b[:, :, None, :]
    e = jnp.where(_causal(t)[:, :, None, None], e, -jnp.inf)
    att = jnp.einsum('bnthk,bnshk,bntshk->bntsh', q, k, jnp.exp(e))
    o = jnp.einsum('bntsh,bnshv->bnthv', att, v)
    contrib = jnp.einsum('bnshk,bnshv->bnhkv', k * jnp.exp(b_last[:, :, None] - b), v)
    s_in, s_fin = _state_scan(jnp.exp(b_last)[..., None], contrib, s0.astype(jnp.float32))
    o = o + jnp.einsum('bnthk,bnhkv->bnthv', q * jnp.exp(b), s_in)
    return o.reshape(bsz, seq, h, HG_DV), (s_fin,)

def _mlstm_scan(q, k, v, ig, logf, state):
    c0, n0, m0 = state
    bsz, seq, h, dk = q.shape
    t = ML_CHUNK
    n = seq // t
    q, k = [a.astype(jnp.float32).reshape(bsz, n, t, h, dk) for a in (q, k)]
    v = v.astype(jnp.float32).reshape(bsz, n, t, h, ML_DV)
    ig, logf = [a.astype(jnp.float32).reshape(bsz, n, t, h) for a in (ig, logf)]
    b = jnp.cumsum(logf, axis=2)
    b_last = b[:, :, -1]
    g = b_last[:, :, None] - b + ig
    g_max = jnp.max(g, axis=2)
    wg = jnp.exp(g - g_max[:, :, None])
    c_loc = jnp.einsum('bnsh,bnshk,bnshv->bnhkv', wg, k, v)
    n_loc = jnp.einsum('bnsh,bnshk->bnhk', wg, k)

    def step(carry, inp):
        cm, nm, mm = carry
        bl, gm, cl, nl = inp
        m_new = jnp.maximum(bl + mm, gm)
        a = jnp.exp(bl + mm - m_new)
        s = jnp.exp(gm - m_new)
        return (a[..., None, None] * cm + s[..., None, None] * cl, a[..., None] * nm + s[..., None] * nl, m_new), (cm, nm, mm)

    xs = tuple(jnp.moveaxis(a, 1, 0) for a in (b_last, g_max, c_loc, n_loc))
    init = (c0.astype(jnp.float32), n0.astype(jnp.float32), m0.astype(jnp.float32))
    (c_f, n_f, m_f), (c_in, n_in, m_in) = lax.scan(step, init, xs)
    c_in, n_in, m_in = [jnp.moveaxis(a, 0, 1) for a in (c_in, n_in, m_in)]
    bt = jnp.swapaxes(b, 2, 3)
    it = jnp.swapaxes(ig, 2, 3)
    dlog = jnp.where(_causal(t), bt[..., :, None] - bt[..., None, :] + it[..., None, :], -jnp.inf)
    m_inter = bt + m_in[..., None]
    m_t = jnp.maximum(m_inter, jnp.max(dlog, -1))
    s = jnp.exp(dlog - m_t[..., None]) * jnp.einsum('bnthk,bnshk->bnhts', q, k)
    w_inter = jnp.exp(m_inter - m_t)
    num = (jnp.einsum('bnhts,bnshv->bnthv', s, v)
           + jnp.swapaxes(w_inter, 2, 3)[..., None] * jnp.einsum('bnthk,bnhkv->bnthv', q, c_in))
    den = jnp.sum(s, -1) + w_inter * jnp.einsum('bnthk,bnhk->bnht', q, n_in)
    den = jnp.maximum(jnp.abs(den), jnp.exp(-m_t))
    hout = num / jnp.swapaxes(den, 2, 3)[..., None]
    return hout.reshape(bsz, seq, h, ML_DV), (c_f, n_f, m_f)

def _ssd_scan(x, dt, la, bm, cm, state):
    (h0,) = state
    bsz, seq, h, p = x.shape
    t = MB_CHUNK
    n = seq // t
    x = x.astype(jnp.float32).reshape(bsz, n, t, h, p)
    dt = dt.reshape(bsz, n, t, h)
    bm = bm.astype(jnp.float32).reshape(bsz, n, t, h, MB_DSTATE)
    cm = cm.astype(jnp.float32).reshape(bsz, n, t, h, MB_DSTATE)
    a = jnp.cumsum(la.reshape(bsz, n, t, h), axis=2)
    a_last = a[:, :, -1]
    at = jnp.swapaxes(a, 2, 3)
    seg = jnp.where(_causal(t), at[..., :, None] - at[..., None, :], -jnp.inf)
    xdt = x * dt[..., None]
    cb = jnp.einsum('bnthd,bnshd->bnhts', cm, bm)
    y = jnp.einsum('bnhts,bnshp->bnthp', jnp.exp(seg) * cb, xdt)
    contrib = jnp.einsum('bnshd,bnshp->bnhpd', bm * jnp.exp(a_last[:, :, None] - a)[..., None], xdt)
    h_in, h_fin = _state_scan(jnp.exp(a_last)[..., None, None], contrib, h0.astype(jnp.float32))
    y = y + jnp.einsum('bnthd,bnhpd->bnthp', cm * jnp.exp(a)[..., None], h_in)
    return y.reshape(bsz, seq, h, p), (h_fin,)

def _token_mixer(hin, p, states):
    bsz, seq = hin.shape[0], hin.shape[1]
    u = jnp.einsum('bld,de->ble', hin, p['w_in'])
    (hq, hi, hg, hf, mq, mk, mv, mo, mi, mf, mz, mxbc, mdt, bg) = jnp.split(u, _split_points(), axis=-1)
    hg_s, ml_c, ml_n, ml_m, mb_s = states

    lb = p['hg_lb']
    q = jax.nn.silu(hq).reshape(bsz, seq, HG_HEADS, HG_DK)
    iv = hi.reshape(bsz, seq, HG_HEADS, HG_DV)
    fpre = hf.astype(jnp.float32).reshape(bsz, seq, 2, HG_HEADS, HG_DK)
    logf = jnp.logaddexp(jnp.log(lb), jnp.log1p(-lb) + jax.nn.log_sigmoid(fpre))
    kk = (1.0 - lb) * jax.nn.sigmoid(-fpre)
    o_hg, hg_new = _bidir(_hgrn2_scan, (q, kk[:, :, 0], iv, logf[:, :, 0]),
                          (q, kk[:, :, 1], iv, logf[:, :, 1]), (hg_s,))
    y_hg = _head_rms(o_hg, p['hg_norm_g']) * jax.nn.silu(hg.astype(jnp.float32))

    qm = mq.reshape(bsz, seq, ML_HEADS, ML_DK)
    km = mk.reshape(bsz, seq, ML_HEADS, ML_DK) * (ML_DK ** -0.5)
    vm = mv.reshape(bsz, seq, ML_HEADS, ML_DV)
    gb = p['ml_gate_b']
    ig = mi.astype(jnp.float32).reshape(bsz, seq, 2, ML_HEADS) + gb[0]
    lf = jax.nn.log_sigmoid(mf.astype(jnp.float32).reshape(bsz, seq, 2, ML_HEADS) + gb[1])
    h_ml, ml_new = _bidir(_mlstm_scan, (qm, km, vm, ig[:, :, 0], lf[:, :, 0]),
                          (qm, km, vm, ig[:, :, 1], lf[:, :, 1]), (ml_c, ml_n, ml_m))
    y_ml = _head_rms(h_ml, p['ml_norm_g']) * jax.nn.sigmoid(mo.astype(jnp.float32))

    xbc = jax.nn.silu(_dwconv(mxbc, p['mb_conv_w'], p['mb_conv_b']))
    mx, mb_b, mb_c = jnp.split(xbc, [MB_DINNER, MB_DINNER + MB_GROUPS * MB_DSTATE], axis=-1)
    mx = mx.reshape(bsz, seq, MB_HEADS, MB_HEADDIM)
    rep = MB_HEADS // MB_GROUPS
    mb_b = jnp.repeat(mb_b.reshape(bsz, seq, MB_GROUPS, MB_DSTATE), rep, axis=2)
    mb_c = jnp.repeat(mb_c.reshape(bsz, seq, MB_GROUPS, MB_DSTATE), rep, axis=2)
    dt = jax.nn.softplus(mdt.astype(jnp.float32).reshape(bsz, seq, 2, MB_HEADS) + p['mb_dt_bias'])
    la = dt * -jnp.exp(p['mb_a_log'].astype(jnp.float32))
    y_mb, mb_new = _bidir(_ssd_scan, (mx, dt[:, :, 0], la[:, :, 0], mb_b, mb_c),
                          (mx, dt[:, :, 1], la[:, :, 1], mb_b, mb_c), (mb_s,))
    y_mb = y_mb + p['mb_d'][:, None] * mx
    y_mb = _head_rms((y_mb.reshape(bsz, seq, MB_DINNER) * jax.nn.silu(mz.astype(jnp.float32)))[:, :, None], p['mb_norm_g'])

    br = jnp.stack([y_hg, y_ml, y_mb], axis=2).astype(hin.dtype)
    proj = jnp.einsum('blcr,crd->blcd', br, p['w_branch'])
    gates = jax.nn.sigmoid(bg.reshape(bsz, seq, N_BRANCH, D_MODEL))
    y = jnp.einsum('blcd,de->ble', gates * proj, p['w_out'])
    return y, (hg_new[0], ml_new[0], ml_new[1], ml_new[2], mb_new[0])

def _layer(x, mod, p, states):
    sh1, sc1, g1, sh2, sc2, g2, sh3, sc3, g3 = jnp.split(mod, N_MOD, axis=-1)
    x = _layernorm(ALPHA * x + 0.5 * g1 * _swiglu(_modulate(x, sh1, sc1), p['ffn_w_gu'][0], p['ffn_w_down'][0]),
                   p['ln_g'][0], p['ln_b'][0])
    y, new_states = _token_mixer(_modulate(x, sh2, sc2), p, states)
    x = _layernorm(ALPHA * x + g2 * y, p['ln_g'][1], p['ln_b'][1])
    x = _layernorm(ALPHA * x + 0.5 * g3 * _swiglu(_modulate(x, sh3, sc3), p['ffn_w_gu'][1], p['ffn_w_down'][1]),
                   p['ln_g'][2], p['ln_b'][2])
    return x, new_states

def _grid_pos_embed(n_tok):
    rows = n_tok // GRID_W
    r, cidx = jnp.meshgrid(jnp.arange(rows, dtype=jnp.float32), jnp.arange(GRID_W, dtype=jnp.float32), indexing='ij')
    quarter = D_MODEL // 4
    freq = jnp.exp(-math.log(10000.0) * jnp.arange(quarter, dtype=jnp.float32) / quarter)
    ar = r.reshape(-1, 1) * freq
    ac = cidx.reshape(-1, 1) * freq
    return jnp.concatenate([jnp.sin(ar), jnp.cos(ar), jnp.sin(ac), jnp.cos(ac)], axis=-1)

def _zero_states(bsz):
    z = lambda *s: jnp.zeros((bsz, 2) + s, jnp.float32)
    return (z(HG_HEADS, HG_DK, HG_DV), z(ML_HEADS, ML_DK, ML_DV), z(ML_HEADS, ML_DK), z(ML_HEADS),
            z(MB_HEADS, MB_HEADDIM, MB_DSTATE))

def setup_inputs(seed: int = 0) -> dict:
    key = jax.random.key(seed)
    ks = iter(jax.random.split(key, 40))
    nrm = lambda shape, s=1.0: s * jax.random.normal(next(ks), shape, jnp.float32)
    unif = lambda shape, lo, hi: jax.random.uniform(next(ks), shape, jnp.float32, lo, hi)
    d = D_MODEL
    st = (DEC_BATCH, DEPTH, 2)
    dt0 = jnp.exp(unif((DEPTH, 2, MB_HEADS), math.log(1e-3), math.log(1e-1)))
    return {
        'x_prompt': nrm((BATCH, SEQ, d)),
        'x_sample': nrm((DEC_BATCH, DEC_SEQ, d)),
        'state_hgrn': nrm(st + (HG_HEADS, HG_DK, HG_DV), 0.5),
        'state_mlstm_C': nrm(st + (ML_HEADS, ML_DK, ML_DV), 0.3),
        'state_mlstm_n': nrm(st + (ML_HEADS, ML_DK), 0.3),
        'state_mlstm_m': nrm(st + (ML_HEADS,), 1.0),
        'state_ssd': nrm(st + (MB_HEADS, MB_HEADDIM, MB_DSTATE), 0.5),
        'c': nrm((DEC_BATCH, d)),
        'c_ctx': nrm((d,)),
        'w_mod': nrm((DEPTH, d, N_MOD * d), 0.5 * d ** -0.5),
        'b_mod': nrm((DEPTH, N_MOD * d), 0.02),
        'ln_g': 1.0 + nrm((DEPTH, 3, d), 0.02),
        'ln_b': nrm((DEPTH, 3, d), 0.02),
        'ffn_w_gu': nrm((DEPTH, 2, d, 2 * D_FF), d ** -0.5),
        'ffn_w_down': nrm((DEPTH, 2, D_FF, d), BETA * D_FF ** -0.5),
        'w_in': nrm((DEPTH, d, D_IN), d ** -0.5),
        'hg_lb': nrm((DEPTH, 2, HG_HEADS * HG_DK)),
        'hg_norm_g': 1.0 + nrm((DEPTH, HG_HEADS * HG_DV), 0.02),
        'ml_gate_b': jnp.stack([nrm((DEPTH, 2, ML_HEADS), 0.1), unif((DEPTH, 2, ML_HEADS), 3.0, 6.0)], axis=1),
        'ml_norm_g': 1.0 + nrm((DEPTH, ML_HEADS * ML_DV), 0.02),
        'mb_conv_w': nrm((DEPTH, MB_CONV, MB_XBC), MB_CONV ** -0.5),
        'mb_conv_b': nrm((DEPTH, MB_XBC), 0.02),
        'mb_dt_bias': dt0 + jnp.log(-jnp.expm1(-dt0)),
        'mb_a_log': jnp.log(unif((DEPTH, 2, MB_HEADS), 1.0, 16.0)),
        'mb_d': 1.0 + nrm((DEPTH, MB_HEADS), 0.02),
        'mb_norm_g': 1.0 + nrm((DEPTH, MB_DINNER), 0.02),
        'w_branch': nrm((DEPTH, N_BRANCH, MIX_W, d), MIX_W ** -0.5),
        'w_out': nrm((DEPTH, d, d), BETA * d ** -0.5),
    }

def reference(x_prompt, x_sample, state_hgrn, state_mlstm_C, state_mlstm_n, state_mlstm_m, state_ssd, c, c_ctx,
              w_mod, b_mod, ln_g, ln_b, ffn_w_gu, ffn_w_down, w_in, hg_lb, hg_norm_g, ml_gate_b, ml_norm_g,
              mb_conv_w, mb_conv_b, mb_dt_bias, mb_a_log, mb_d, mb_norm_g, w_branch, w_out):
    lbs = jnp.cumsum(jax.nn.softmax(hg_lb.astype(jnp.float32), axis=0), axis=0)
    lbs = (lbs - lbs[0]).reshape(DEPTH, 2, HG_HEADS, HG_DK)
    params = [{'w_in': w_in[l], 'hg_lb': lbs[l], 'hg_norm_g': hg_norm_g[l], 'ml_gate_b': ml_gate_b[l],
               'ml_norm_g': ml_norm_g[l], 'mb_conv_w': mb_conv_w[l], 'mb_conv_b': mb_conv_b[l],
               'mb_dt_bias': mb_dt_bias[l], 'mb_a_log': mb_a_log[l], 'mb_d': mb_d[l], 'mb_norm_g': mb_norm_g[l],
               'w_branch': w_branch[l], 'w_out': w_out[l], 'ln_g': ln_g[l], 'ln_b': ln_b[l],
               'ffn_w_gu': ffn_w_gu[l], 'ffn_w_down': ffn_w_down[l]} for l in range(DEPTH)]
    mod_ctx = jnp.einsum('d,lde->le', jax.nn.silu(c_ctx), w_mod) + b_mod
    mod_lat = jnp.einsum('bd,lde->lbe', jax.nn.silu(c), w_mod) + b_mod[:, None]

    xc = x_prompt
    collected = ([], [], [], [], [])
    for l in range(DEPTH):
        xc, st = _layer(xc, mod_ctx[l][None, None], params[l], _zero_states(x_prompt.shape[0]))
        for lst, s in zip(collected, st):
            lst.append(s)
    y_prompt = xc
    new_state_hgrn = jnp.stack(collected[0], axis=1)
    new_state_mlstm_C = jnp.stack(collected[1], axis=1)
    new_state_mlstm_n = jnp.stack(collected[2], axis=1)
    new_state_mlstm_m = jnp.stack(collected[3], axis=1)
    new_state_ssd = jnp.stack(collected[4], axis=1)

    xs = x_sample + _grid_pos_embed(x_sample.shape[1]).astype(x_sample.dtype)[None]
    for l in range(DEPTH):
        st = (state_hgrn[:, l], state_mlstm_C[:, l], state_mlstm_n[:, l], state_mlstm_m[:, l], state_ssd[:, l])
        xs, _ = _layer(xs, mod_lat[l][:, None], params[l], st)
    y_sample = xs
    return (y_prompt, y_sample, new_state_hgrn, new_state_mlstm_C, new_state_mlstm_n, new_state_mlstm_m, new_state_ssd)


_drawn_inputs = setup_inputs


def setup_inputs(seed=0):
    import zlib

    import numpy as np

    out = dict(_drawn_inputs(seed))
    spreads = {}
    factors = {'state_hgrn': 8.0,
     'state_mlstm_C': 4.53,
     'state_mlstm_n': 8.0,
     'state_mlstm_m': 8.0,
     'hg_norm_g': 56.72,
     'ml_norm_g': 64.0,
     'mb_d': 29.614,
     'mb_norm_g': 34.914}
    for name, (base, spread) in spreads.items():
        noise = np.random.default_rng([zlib.crc32(name.encode()), seed]).standard_normal(out[name].shape)
        drawn = base * np.exp(spread * noise) if base else spread * noise
        out[name] = __import__('jax').numpy.asarray(drawn.astype(out[name].dtype))
    for name, factor in factors.items():
        out[name] = (out[name] * factor).astype(out[name].dtype)
    return out
```

```python
import math
from contextlib import ExitStack

import numpy as np

import concourse.bass as bass
from concourse import mybir

F32 = mybir.dt.float32
F32R = mybir.dt.float32r
U8 = mybir.dt.uint8
ALU = mybir.AluOpType
ACT = mybir.ActivationFunctionType
AX = mybir.AxisListType

P = 128
D = 1024
L = 2
NC_TOK, NL_TOK = 128, 256
T = NC_TOK + NL_TOK
NT = T // P
KC = D // P
DFF = 2816
NF = DFF // P
MIX = 512
NH = MIX // P
SH, SP_ = 8, 64
ALPHA = (2 * L) ** 0.25
LN_EPS, RMS_EPS = 1e-5, 1e-6
NEG = -1e30
GROUPS = ((0, NC_TOK), (NC_TOK, T))
C1 = P + 1

U_MOD = 9 * KC
U_GU, U_DOWN = 2 * NF, 2 * KC
U_FFN = U_GU + U_DOWN
U_IN = 72
U_BR, U_OUT = 12, KC
U_MIX = U_IN + U_BR + U_OUT
U_SPLIT = 2 * U_FFN + U_MIX
NRAW, NSPLIT = 4, 2
UW = (NF // 2) * P
assert U_MOD % NRAW == 0 and U_SPLIT % NRAW == 0 and U_FFN % NRAW == 0

PAR, _n = {}, 0
for _name, _w in (("bmod", 72), ("ln", 48), ("normg", 12), ("convw", 18), ("convb", 6), ("row", 4),
                  ("mbd", 8)):
    PAR[_name] = _n
    _n += _w
NPAR = _n

HG_STEPS = ((0, 0), (1, 0), (0, 1), (1, 2), (0, 2), (1, 1))
LEVELS = (64, 32, 16, 8, 4, 2, 1)


def hg_plan():
    ops = []
    for s, (d, t) in enumerate(HG_STEPS):
        for h in LEVELS:
            ops.append((s, d, t, "level", h))
        ops.append((s, d, t, "diag", 0))
        if t:
            ops.append((s, d, t, "inter", 0))
        if s < 4:
            ops.append((s, d, t, "state", 0))
    return ops


class Signal:

    def __init__(self, sem):
        self.sem, self.n = sem, 0

    def on(self, ins):
        self.n += 1
        return ins.then_inc(self.sem, 1)


def build(nc, ins, outs):
    ctx = ExitStack()
    with ctx:
        end = {"at": (nc.sbuf_base + 31) // 32 * 32}

        def at(name, shape, offset, dt=F32):
            size = int(np.prod(shape[1:])) * (1 if dt == U8 else 4)
            return nc.alloc_sbuf_tensor_at(name, shape, dt, offset=offset), offset + (size + 31) // 32 * 32

        def sb(name, shape, dt=F32):
            t, end["at"] = at(name, shape, end["at"], dt)
            return t

        raw = [sb(f"raw{i}", [P, UW]) for i in range(NRAW)]
        whi = [sb(f"whi{i}", [P, UW], F32R) for i in range(NSPLIT)]
        wlo = [sb(f"wlo{i}", [P, UW], F32R) for i in range(NSPLIT)]
        x = sb("x", [P, KC, T])
        h_hi = sb("h_hi", [P, KC, T], F32R)
        h_lo = sb("h_lo", [P, KC, T], F32R)
        ident = sb("ident", [P, P])
        mean_w = sb("mean_w", [P, P])
        neg = sb("neg", [P, 2, P])
        hmask = sb("hmask", [P, 2, len(LEVELS) + 1, P], U8)
        sgn = sb("sgn", [P, 1])
        keep = sb("keep", [P, NT * C1])
        par = sb("par", [P, NPAR])
        mod = sb("mod", [P, 72, 2])
        cond = sb("cond", [P, KC, 2])
        cond_t = sb("cond_t", [P, KC, 2])
        lb_in = sb("lb_in", [P, 2, 8])
        lb_w = sb("lb_w", [P, 4, 8])
        lbs = sb("lbs", [P, 2, 8])
        lb = sb("lb", [P, 8])
        om = sb("om", [P, 8])
        eps = sb("eps", [P, 2])
        arena = end["at"]

        def region(start, *parts):
            made = []
            for part in parts:
                t, start = at(part[0], part[1], start, part[2] if len(part) > 2 else F32)
                made.append(t)
            return made, start

        (act_hi, act_lo, tb0, tb1, sb0, sb1, vb0, vb1, sq0, sq1, std, rstd, ht0, ht1), e0 = region(
            arena, ("act_hi", [P, NF, T], F32R), ("act_lo", [P, NF, T], F32R),
            *[(n, [P, T]) for n in ("tb0", "tb1", "sb0", "sb1", "vb0", "vb1", "sq0", "sq1", "std", "rstd",
                                    "ht0", "ht1")])
        tb, sbf, vb, sq, ht = (tb0, tb1), (sb0, sb1), (vb0, vb1), (sq0, sq1), (ht0, ht1)
        (pos, hmask_in), _ = region(arena, ("pos", [P, KC, NL_TOK]), ("hmask_in", [P, 2, len(LEVELS) + 1, P]))
        (gates, y_hg, nsq, nyn, nsm), mix0 = region(
            arena, ("gates", [P, 24, T]), ("y_hg", [P, NH, T]), ("nsq", [P, NH, P]), ("nyn", [P, NH, P]),
            ("nsm", [P, 3, NH]))
        (q, v, hgate, kk, cc, ea0, ea1, qe0, qe1, ke0, ke1, att0, att1, hs, kT, so0, so1, etot), e1 = region(
            mix0, ("q", [P, NH, T]), ("v", [P, NT, MIX]), ("hgate", [P, NT, MIX]), ("kk", [P, 2, NH, T]),
            ("cc", [P, 2, NH, NT, C1]), *[(n, [P, NH, P]) for n in ("ea0", "ea1", "qe0", "qe1", "ke0", "ke1",
                                                                      "att0", "att1")],
            ("hs", [P, 2, NH, P]), ("kT", [P, NH, P]), ("so0", [P, NH, P]), ("so1", [P, NH, P]), ("etot", [P, 2, NH]))
        ea, qe, ke, att, so = (ea0, ea1), (qe0, qe1), (ke0, ke1), (att0, att1), (so0, so1)
        (y_ml, t_1, t_2, t_3, t_4, x_5, wb), rows0 = region(
            mix0, ("y_ml", [P, NH, T]), *[(f"t_{i}", [P, NT, P]) for i in (1, 2, 3, 4)], ("x_5", [P, T]),
            ("wb", [P, P]))
        (ga, gb, r_w, r_e, r_u, r_n, cr, x_1, x_2, x_3, x_4, r_N, minit, coef, lastw, dlast, mout), e2 = region(
            rows0, *[(n, [P, T]) for n in ("ga", "gb", "r_w", "r_e", "r_u", "r_n")], ("cr", [P, NT, C1]),
            *[(n, [P, T]) for n in ("x_1", "x_2", "x_3", "x_4", "r_N")], ("minit", [P, NT]), ("coef", [P, 1]),
            ("lastw", [P, 1]), ("dlast", [P, P]), ("mout", [P, 1]))
        (pt0, pt1, pr0, pr1, st0, st1, kw0, kw1, tmpa, tmpb, den, co0, co1), e3 = region(
            rows0, *[(n, [P, T]) for n in ("pt0", "pt1", "pr0", "pr1", "st0", "st1")], ("kw0", [P, 2, P]),
            ("kw1", [P, 2, P]), ("tmpa", [P, NT, C1]), ("tmpb", [P, NT, C1]), ("den", [P, 2, NT]),
            ("co0", [P, C1]), ("co1", [P, C1]))
        assert e3 <= e2
        pt, pr, st, kw, co = (pt0, pt1), (pr0, pr1), (st0, st1), (kw0, kw1), (co0, co1)
        (mq, mk, mkt, va, mo, cs, hout), e4 = region(
            e2, ("mq", [P, NH, T]), ("mk", [P, NH, T]), ("mkt", [P, NT, MIX]), ("va", [P, NT, NH, C1]),
            ("mo", [P, NT, MIX]), ("cs", [P, 2, NH, C1]), ("hout", [P, NT, MIX]))
        (xpad, xs, cth, cbuf, mz, yx, ht_s, xw, ho0, ho1), e5 = region(
            e2, ("xpad", [P, 6, 388]), ("xs", [P, 6, T]), ("cth", [P, 388]), ("cbuf", [P, 388]),
            ("mz", [P, NT, MIX]), ("yx", [P, 2, MIX]), ("ht_s", [P, 2, 4, SP_]), ("xw", [P, MIX]),
            ("ho0", [P, 4, SP_]), ("ho1", [P, 4, SP_]))
        (xt, bt), _ = region(e2, ("xt", [P, NT, MIX]), ("bt", [P, NT, P]))
        zth, _ = at("zth", [P, MIX], e2 + 9312 + 9216)
        y_mb, _ = at("y_mb", [P, NH, T], e2 + 9312 + 9216 + 2 * 1568 + 6144)
        (y_hi, y_lo, zt0, zt1), e7 = region(rows0, ("y_hi", [P, 3, NH, T], F32R), ("y_lo", [P, 3, NH, T], F32R),
                                  ("zt0", [P, 2, T]), ("zt1", [P, 2, T]))
        ps = [ctx.enter_context(nc.psum_tensor(f"ps{i}", [P, 512], F32)) for i in range(8)]

        def sem(name):
            return ctx.enter_context(nc.semaphore(name))

        raw_loaded = [sem(f"raw_loaded{i}") for i in range(NRAW)]
        mod_used = sem("mod_used")
        w_hi = sem("w_hi")
        w_split = sem("w_split")
        w_used = sem("w_used")
        layer_end = sem("layer_end")
        start_loads = sem("start_loads")
        par_loaded = sem("par_loaded")
        stored = sem("stored")
        sp_turn = sem("sp_turn")
        ready = sem("ready")

        OWN = {"pe": {}, "act": {}, "dve": {}}

        def signal(owner, name):
            OWN[owner][name] = sem(name)
            return OWN[owner][name]

        met = signal("dve", "met")
        dve_step = signal("dve", "dve_step")
        act_step = signal("act", "act_step")
        st_loaded = signal("act", "st_loaded")
        gate_t = signal("act", "gate_t")
        gated = signal("dve", "gated")
        down_ev = signal("act", "down_ev")
        resid = signal("dve", "resid")
        ln_mean = signal("pe", "ln_mean")
        ln_cent = signal("dve", "ln_cent")
        ln_sq = signal("act", "ln_sq")
        ln_acc = signal("pe", "ln_acc")
        ln_std = signal("act", "ln_std")
        ln_out = signal("dve", "ln_out")
        md_t = signal("dve", "md_t")
        md_hi = signal("act", "md_hi")
        md_lo = signal("dve", "md_lo")
        evac = signal("act", "evac")
        post = signal("dve", "post")
        hg_ln = signal("act", "hg_ln")
        hg_a = signal("dve", "hg_a")
        hg_e = signal("act", "hg_e")
        hg_b = signal("dve", "hg_b")
        hg_m = signal("pe", "hg_m")
        hg_c = signal("dve", "hg_c")
        hg_m2 = signal("pe", "hg_m2")
        hg_c2 = signal("dve", "hg_c2")
        hg_o = signal("pe", "hg_o")
        nm_sq = signal("act", "nm_sq")
        nm_ms = signal("dve", "nm_ms")
        nm_sd = signal("act", "nm_sd")
        nm_y = signal("dve", "nm_y")
        nm_tr = signal("pe", "nm_tr")
        nm_out = signal("act", "nm_out")
        row_d = signal("dve", "row_d")
        row_a = signal("act", "row_a")
        row_p = signal("pe", "row_p")
        tr_pe = signal("pe", "tr_pe")
        tr_act = signal("act", "tr_act")
        pr_bc = signal("pe", "pr_bc")
        pr_x = signal("dve", "pr_x")
        pr_e = signal("act", "pr_e")
        pr_qk = signal("pe", "pr_qk")
        pr_s = signal("dve", "pr_s")
        pr_n = signal("pe", "pr_n")
        ml_kw = signal("dve", "ml_kw")
        ml_it = signal("pe", "ml_it")
        ml_cu = signal("dve", "ml_cu")
        ml_i2 = signal("pe", "ml_i2")
        ml_iw = signal("act", "ml_iw")
        ml_h = signal("dve", "ml_h")
        sd_w = signal("dve", "sd_w")
        sd_p = signal("pe", "sd_p")
        sd_o = signal("dve", "sd_o")
        br_z = signal("dve", "br_z")
        br_hi = signal("dve", "br_hi")

        ln_x = signal("act", "ln_x")
        hg_lnd = signal("dve", "hg_lnd")
        br_a = signal("act", "br_a")
        br_y = signal("dve", "br_y")
        br_z2 = signal("dve", "br_z2")
        start_v = sem("start_v")
        co_stored = [sem(f"co_stored{i}") for i in range(2)]
        MEET = {k: n + 1 for n, k in enumerate((
            ("ffn", 0), ("down", 0), ("ln", 0), ("hg_in", 0), ("hg", 0), ("ml_in", 0), ("rows", 0), ("ml", 0),
            ("mln", 0), ("ssd_in", 0), ("ssd_c", 0), ("ssd_x", 0), ("ssd", 0), ("br_in", 0), ("out", 0),
            ("ffn", 1), ("down", 1), ("end", 0)))}
        STORES = 6
        ROW_W, ROW_T, ROW_TA = 3, 4, 5
        POST_MZ, POST_SSD = 15, 18

        def down_unit(k):
            return UF1 + U_GU <= k < UM or k >= UF2 + U_GU

        class Steps:

            def __init__(self, eng, s):
                self.eng, self.sem, self.n, self.off = eng, s, 0, 0

            def __call__(self, ins):
                self.n += 1
                ins.then_inc(self.sem, 1)
                return ins

            def done(self):
                self.eng.wait_ge(self.sem, self.off + self.n)

        plan = []
        for b in range(8):
            plan.append(("fm", b, (b % 2,), ("hf", b)))
        for b in range(4):
            plan.append(("fm", 8 + b, (b % 2,), ("hq", b)))
        plan.append(("tm", 12, (2, 3, 4), ("hi", 0)))
        plan.append(("tm", 16, (5, 6, 7), ("hg", 0)))
        for b in range(24):
            plan.append(("fm", 20 + b, (b % 2,), ("bg", b)))
        for b in range(4):
            plan.append(("fm", 44 + b, (b % 2,), ("mq", b)))
        for b in range(4):
            plan.append(("fm", 48 + b, (b % 2,), ("mk", b)))
        for b in range(2):
            plan.append(("fm", 52 + b, (b % 2,), ("gr", b)))
        plan.append(("tm", 54, (2, 3, 4), ("mv", 0)))
        plan.append(("tm", 58, (5, 6, 7), ("mo", 0)))
        for b in range(6):
            plan.append(("fm", 62 + b, (b % 2,), ("xbc", b)))
        plan.append(("tm", 68, (2, 3, 4), ("mz", 0)))
        first_evac, bank_last, n = {}, {}, 0
        bank_before = {}
        for item in plan:
            first_evac[item[3]] = n
            for bank in item[2]:
                bank_before[(item[3], bank)] = bank_last.get(bank, 0)
                n += 1
                bank_last[bank] = n
        N_EVAC = n

        def items(*names):
            return [it for it in plan if it[3][0] in names]

        ops = hg_plan()
        cnt = {}
        for kind in "abcem":
            n = 0
            for o, (s, d, t, what, hh) in enumerate(ops):
                if kind == "m" or (kind == "c" and what != "inter") or (kind in "abe" and what != "diag"):
                    n += 1
                cnt[kind, o] = n
        n2 = 0
        for o, op in enumerate(ops):
            if op[3] == "state":
                n2 += 1
            cnt["s", o] = n2

        UF1, UM, UF2 = 0, U_FFN, U_FFN + U_MIX
        PER = (U_MOD + U_SPLIT) // NRAW

        def raw_ready(eng, l, k4, m):
            eng.wait_ge(raw_loaded[m], (k4 + (l * PER + U_MOD // NRAW + 1)) * 16)

        def unit_split(pe, l, k):
            pe.wait_ge(w_split, k + (l * U_SPLIT + 1 + NRAW))

        def unit_done(eng, l, k):
            eng.wait_ge(w_used, k + (l * U_SPLIT + 1 + NSPLIT))

        def slots_free(eng, l, k):
            eng.wait_ge(w_used, k + (l * U_SPLIT + 1))

        block = ctx.enter_context(nc.Block())

        def meet(eng, n):
            eng.drain().then_inc(met, 1)
            eng.wait_ge(met, 3 * n)

        def layer_over(eng, l, owner):
            eng.drain().then_inc(layer_end, 1)
            eng.wait_ge(layer_end, l * 9 + 3)
            eng.sem_inc(layer_end, 1)
            for s in OWN[owner].values():
                eng.sem_clear(s)
            eng.drain().then_inc(layer_end, 1)
            eng.wait_ge(layer_end, l * 9 + 9)

        @block.sync
        def _(sp):
            for dst, src in ((cond, ins["cond"]), (x, ins["x"]), (lb_in, ins["hg_lb"]), (ident, ins["ident"]),
                             (mean_w, ins["mean_w"]), (neg, ins["neg"]), (hmask_in, ins["hmask"]),
                             (keep, ins["keep"]), (sgn, ins["sgn"]), (pos, ins["pos"])):
                sp.dma_start(dst[tuple(slice(None) for _ in dst.shape)], src).then_inc(start_loads, 16)
            with sp.Fori(0, L) as l:
                with sp.Fori(0, U_MOD // NRAW) as i:
                    for m in range(NRAW):
                        sp.wait_ge(w_split, l * U_SPLIT + (m + 1))
                        sp.sem_inc(sp_turn, 1)
                        sp.wait_ge(mod_used, l * U_MOD + i * NRAW + (m + 1))
                        sp.dma_start(raw[m][:, 0:KC * P], ins["w_mod"][l, i * NRAW + m]).then_inc(raw_loaded[m], 16)

                def stream(part, first, count, width, src, first_of_split=False):
                    with sp.Fori(0, count // NRAW) as i:
                        for m in range(NRAW):
                            sp.wait_ge(w_split, l * U_SPLIT + i * NRAW + (first + m + 1))
                            if first_of_split:
                                sp.sem_inc(sp_turn, 1)
                                sp.wait_ge(mod_used, l * U_MOD + (U_MOD + m + 1))
                            sp.dma_start(raw[m][:, 0:width], src(i * NRAW + m)).then_inc(raw_loaded[m], 16)

                stream("gu", UF1, U_GU, KC * P, lambda k: ins["w_gu"][l, 0, k], True)
                stream("down", UF1 + U_GU, U_DOWN, UW, lambda k: ins["w_down"][l, 0, k])
                stream("in", UM, U_IN, KC * P, lambda k: ins["w_in"][l, k])
                stream("branch", UM + U_IN, U_BR, KC * P, lambda k: ins["w_branch"][l, k])
                stream("out", UM + U_IN + U_BR, U_OUT, KC * P, lambda k: ins["w_out"][l, k])
                stream("gu", UF2, U_GU, KC * P, lambda k: ins["w_gu"][l, 1, k])
                stream("down", UF2 + U_GU, U_DOWN, UW, lambda k: ins["w_down"][l, 1, k])
            sp.wait_ge(layer_end, 9 * L)
            sp.dma_start(outs["y"], x[:, :, :]).then_inc(stored, 16)
            sp.wait_ge(stored, 16 * (STORES * L + 1))

        @block.gpsimd
        def _(pool):
            for _ in range(NRAW):
                pool.sem_inc(w_split, 1)
            with pool.Fori(0, L) as l:
                for first, count, width in ((UF1, U_GU, KC * P), (UF1 + U_GU, U_DOWN, UW), (UM, U_MIX, KC * P),
                                            (UF2, U_GU, KC * P), (UF2 + U_GU, U_DOWN, UW)):
                    with pool.Fori(0, count // NRAW) as i:
                        for m in range(NRAW):
                            s = m % NSPLIT
                            pool.wait_ge(w_hi, l * U_SPLIT + i * NRAW + (first + m + 1))
                            nc.gpsimd.tensor_tensor(wlo[s][:, 0:width], raw[m][:, 0:width],
                                                    whi[s][:, 0:width].bitcast(F32),
                                                    ALU.subtract).then_inc(w_split, 1)

        @block.tensor
        def _(pe):
            mm = nc.tensor.matmul
            for _ in range(NRAW):
                pe.sem_inc(mod_used, 1)
            for _ in range(NSPLIT):
                pe.sem_inc(w_used, 1)
            pe.wait_ge(start_loads, 16 * 10)
            pe.wait_ge(ready, 3)

            def block_product(out, m, xh, xl, chunks, start, stop, w0=0):
                s = m % NSPLIT
                chunks = list(chunks)
                for n, (wc, xc) in enumerate(chunks):
                    hi_, lo_ = (w[s][:, w0 + wc * P:w0 + (wc + 1) * P] for w in (whi, wlo))
                    mm(out, hi_, xh[:, xc, :], start=start and n == 0, stop=False)
                    mm(out, hi_, xl[:, xc, :], start=False, stop=False)
                    last = mm(out, lo_, xh[:, xc, :], start=False, stop=stop and n == len(chunks) - 1)
                return last

            def layer_norm(j):
                for n in range(KC):
                    last = mm(ps[4][:, 0:T], mean_w[:, :], x[:, n, :], start=(n == 0), stop=(n == KC - 1))
                last.then_inc(ln_mean, 1)
                for n in range(KC):
                    pe.wait_ge(ln_sq, KC * j + n + 1)
                    mm(ps[5][:, 0:T], mean_w[:, :], sq[n % 2][:, :], start=(n == 0),
                       stop=(n == KC - 1)).then_inc(ln_acc, 1)

            def ffn(l, j, u0):
                pe.wait_ge(md_lo, KC * (2 * j + 1))
                with pe.Fori(0, U_GU // 4) as i:
                    for m in range(4):
                        unit_split(pe, l, i * 4 + (u0 + m))
                        if m % 2 == 0:
                            pe.wait_ge(gated, i * 2 + (NF * j + m // 2 + 1))
                        block_product(ps[m][:, 0:T], m, h_hi, h_lo, [(c, c) for c in range(KC)], True,
                                      True).then_inc(w_used, 1)
                meet(pe, MEET["ffn", j])
                with pe.Fori(0, U_DOWN // 4) as i:
                    for m in range(4):
                        unit_split(pe, l, i * 4 + (u0 + U_GU + m))
                        if m % 2 == 0:
                            pe.wait_ge(resid, i * 2 + ((0, KC * 2)[j] + m // 2 + 1))
                        half = m % 2
                        block_product(ps[m // 2][:, 0:T], m, act_hi, act_lo,
                                      [(c, half * (NF // 2) + c) for c in range(NF // 2)], half == 0,
                                      half == 1).then_inc(w_used, 1)
                meet(pe, MEET["down", j])

            def project(l, item):
                kind, u, banks, what = item
                for bank in banks:
                    if bank_before[what, bank]:
                        pe.wait_ge(evac, bank_before[what, bank])
                if kind == "fm":
                    unit_split(pe, l, UM + u)
                    block_product(ps[banks[0]][:, 0:T], u, h_hi, h_lo, [(c, c) for c in range(KC)], True,
                                  True).then_inc(w_used, 1)
                    return
                for m in range(4):
                    unit_split(pe, l, UM + u + m)
                    s = m % NSPLIT
                    for c2 in range(2):
                        c = 2 * m + c2
                        for t in range(NT):
                            out = ps[banks[t]][:, :]
                            xh, xl = (a[:, c, t * P:(t + 1) * P] for a in (h_hi, h_lo))
                            wh, wl = (w[s][:, c2 * MIX:(c2 + 1) * MIX] for w in (whi, wlo))
                            mm(out, xh, wh, start=(c == 0), stop=False)
                            mm(out, xl, wh, start=False, stop=False)
                            last = mm(out, xh, wl, start=False, stop=(c == KC - 1))
                    last.then_inc(w_used, 1)

            def normed(b):
                for t in range(NT):
                    n = b * NT + t
                    pe.wait_ge(nm_y, n + 1)
                    if t:
                        pe.wait_ge(nm_out, n)
                    for g in range(NH):
                        last = nc.tensor.transpose(ps[0][:, g * P:(g + 1) * P], nyn[:, g, :], ident[:, :])
                    last.then_inc(nm_tr, 1)
                pe.wait_ge(nm_out, (b + 1) * NT)

            def hgrn(l):
                bgs = items("bg")
                first = set()

                def o_flag(t):
                    f = t not in first
                    first.add(t)
                    return f

                waiting = []
                seen_att = {}
                bg = 0
                for o, (s, d, t, what, hh) in enumerate(ops):
                    S, b = ps[2 + o % 2], o % 2
                    if what != "diag":
                        pe.wait_ge(hg_b, cnt["b", o])
                    if o >= 2:
                        pe.wait_ge(hg_c, cnt["c", o - 2])
                    cols = slice(t * P, (t + 1) * P)
                    for g in range(NH):
                        out = S[:, g * P:(g + 1) * P]
                        if what == "level":
                            last = mm(out, ke[b][:, g, :], qe[b][:, g, :], start=True, stop=True)
                        elif what == "diag":
                            last = mm(out, kk[:, d, g, cols], q[:, g, cols], start=True, stop=True)
                        elif what == "inter":
                            if g == 0:
                                pe.wait_ge(st_loaded, 16)
                                if s >= 4:
                                    pe.wait_ge(hg_c2, s - 1)
                            last = mm(ps[4 + t][:, g * P:(g + 1) * P], qe[b][:, g, :], hs[:, d, g, :],
                                      start=o_flag(t), stop=True, skip_group_check=True)
                        else:
                            last = nc.tensor.transpose(out, ke[b][:, g, :], ident[:, :])
                    last.then_inc(hg_m, 1)
                    for o2, (s2, d2, t2, _, _) in waiting:
                        pe.wait_ge(hg_c, cnt["c", o2])
                        if s2:
                            pe.wait_ge(hg_c2, s2)
                        for g in range(NH):
                            last = mm(ps[7][:, g * P:(g + 1) * P], kT[:, g, :], v[:, t2, g * P:(g + 1) * P],
                                      start=True, stop=True)
                        last.then_inc(hg_m2, 1)
                    waiting = [(o, ops[o])] if what == "state" else []
                    if what == "level" and hh == 64 and s:
                        out_step(s - 1, o_flag)
                    if o % 2 and bg < len(bgs):
                        project(l, bgs[bg])
                        bg += 1
                for it in bgs[bg:]:
                    project(l, it)
                out_step(5, o_flag)

            def out_step(s, o_flag):
                d, t = HG_STEPS[s]
                diag = [o for o, op in enumerate(ops) if op[0] == s and op[3] == "diag"][0]
                pe.wait_ge(hg_c, cnt["c", diag])
                for g in range(NH):
                    last = mm(ps[4 + t][:, g * P:(g + 1) * P], att[d][:, g, :], v[:, t, g * P:(g + 1) * P],
                              start=o_flag(t), stop=True, skip_group_check=True)
                last.then_inc(hg_o, 1)

            def rows():
                pe.wait_ge(row_d, ROW_T)
                pe.wait_ge(row_a, ROW_TA)
                for i, xi in enumerate((x_1, x_2, x_3, x_4)):
                    if i >= 2:
                        pe.wait_ge(tr_act, i - 1)
                    for t in range(NT):
                        last = nc.tensor.transpose(ps[i % 2][:, t * P:(t + 1) * P], xi[:, t * P:(t + 1) * P],
                                                   ident[:, :])
                    last.then_inc(tr_pe, 1)
                mm(ps[2][:, 0:P], mean_w[:, :], dlast[:, :], start=True, stop=True).then_inc(row_p, 1)

            def keys_turned():
                for t in range(NT):
                    if t >= 2:
                        pe.wait_ge(tr_act, 4 + t - 1)
                    elif t == 0:
                        pe.wait_ge(tr_act, 4)
                    for g in range(NH):
                        last = nc.tensor.transpose(ps[3 + t % 2][:, g * P:(g + 1) * P],
                                                   mk[:, g, t * P:(t + 1) * P], ident[:, :])
                    last.then_inc(tr_pe, 1)

            def spread(r, rr):
                if r >= 2:
                    pe.wait_ge(pr_x, r - 1)
                mm(ps[r % 2][:, 0:T], ident[:, rr:rr + 1].to_broadcast([P, P]), x_5[:, :], start=True,
                   stop=True).then_inc(pr_bc, 1)

            def mlstm():
                def head(h):
                    if h >= 2:
                        pe.wait_ge(pr_s, 2 * h - 2)
                    for t in range(NT):
                        c = slice(t * P, (t + 1) * P)
                        last = mm(ps[2 + h % 2][:, c], mk[:, h, c], mq[:, h, c], start=True, stop=True)
                    last.then_inc(pr_qk, 1)

                def second(r):
                    h, d = r // 2, r % 2
                    pe.wait_ge(ml_cu, r + 1)
                    t2 = 2 - d
                    mm(ps[6 + r % 2][:, C1:2 * C1], mq[:, h, t2 * P:(t2 + 1) * P], cs[:, d, h, :], start=True,
                       stop=True).then_inc(ml_i2, 1)

                spread(0, 0)
                head(0)
                pe.wait_ge(st_loaded, 32)
                for r in range(8):
                    h, d = r // 2, r % 2
                    if r < 7:
                        spread(r + 1, 32 * (1 - d) + (r + 1) // 2)
                        if d == 1:
                            head(h + 1)
                    pe.wait_ge(pr_s, r + 1)
                    if r >= 2:
                        pe.wait_ge(ml_h, r - 1)
                    for t in range(NT):
                        last = mm(ps[4 + r % 2][:, t * C1:(t + 1) * C1], st[r % 2][:, t * P:(t + 1) * P],
                                  va[:, t, h, :], start=True, stop=True)
                    last.then_inc(pr_n, 1)
                    pe.wait_ge(ml_kw, r + 1)
                    it, t1 = ps[6 + r % 2], 1 + d
                    mm(it[:, C1:2 * C1], kw[r % 2][:, 0, :], va[:, 0, h, :], start=True, stop=True)
                    mm(it[:, 2 * C1:3 * C1], kw[r % 2][:, 1, :], va[:, t1, h, :], start=True, stop=True)
                    mm(it[:, 0:C1], mq[:, h, t1 * P:(t1 + 1) * P], cs[:, d, h, :], start=True,
                       stop=True).then_inc(ml_it, 1)
                    if r:
                        second(r - 1)
                second(7)

            def ssd():
                meet(pe, MEET["ssd_c", 0])
                for t in range(NT):
                    c = slice(t * P, (t + 1) * P)
                    if t:
                        pe.wait_ge(tr_act, 7 + 2 * t)
                    for g in range(4):
                        last = nc.tensor.transpose(ps[5][:, g * P:(g + 1) * P], xs[:, g, c], ident[:, :])
                    last.then_inc(tr_pe, 1)
                    last = nc.tensor.transpose(ps[6][:, 0:P], xs[:, 4, c], ident[:, :])
                    last.then_inc(tr_pe, 1)
                meet(pe, MEET["ssd_x", 0])
                n = w = 0
                for d in range(2):
                    for step, t in enumerate((0, 1 + d, 2 - d)):
                        c = slice(t * P, (t + 1) * P)
                        if step:
                            pe.wait_ge(st_loaded, 48)
                            pe.wait_ge(sd_o, n)
                            for g in range(2):
                                gp = slice(64 * g, 64 * g + 64)
                                last = mm(ps[(7, 2)[g]][:, 0:256], xs[gp, 5, c],
                                          ht_s[gp, d, :, :].rearrange("p h e -> p (h e)"), start=True, stop=True)
                            last.then_inc(sd_p, 1)
                            n += 1
                        if step < 2:
                            w += 1
                            pe.wait_ge(sd_w, 6 + w)
                            pe.wait_ge(sd_o, n)
                            mm(ps[3][:, :], bt[:, t, :], xw[:, :], start=True, stop=True).then_inc(sd_p, 1)
                            n += 1
                pe.wait_ge(sd_o, n)

                def group(g):
                    if g:
                        pe.wait_ge(pr_s, 8 + 8 * g)
                    gp = slice(64 * g, 64 * g + 64)
                    for t in range(NT):
                        c = slice(t * P, (t + 1) * P)
                        last = mm(ps[2][:, c], xs[gp, 4, c], xs[gp, 5, c], start=True, stop=True)
                    last.then_inc(pr_qk, 1)

                spread(8, 64)
                group(0)
                for r in range(16):
                    head, d = r // 2, r % 2
                    if r < 15:
                        spread(9 + r, 64 + 32 * (1 - d) + (r + 1) // 2)
                    if r == 8:
                        group(1)
                    pe.wait_ge(pr_s, 9 + r)
                    for t in range(NT):
                        last = mm(ps[4 + t][:, head * SP_:(head + 1) * SP_], st[r % 2][:, t * P:(t + 1) * P],
                                  xt[:, t, head * SP_:(head + 1) * SP_], start=(r == 0), stop=True,
                                  skip_group_check=True)
                    last.then_inc(pr_n, 1)

            def branches(l):
                pe.wait_ge(br_y, 3)
                n = 0
                for mblk in range(4):
                    for c in range(3):
                        u = UM + U_IN + 3 * mblk + c
                        unit_split(pe, l, u)
                        b2 = n % 2
                        if n >= 2:
                            pe.wait_ge(br_z, n - 1)
                        for j in range(2):
                            s = u % NSPLIT
                            out = ps[2 * b2 + j][:, 0:T]
                            for k in range(4):
                                wsl = slice(k * 2 * P + j * P, k * 2 * P + (j + 1) * P)
                                mm(out, whi[s][:, wsl], y_hi[:, c, k, :], start=(k == 0), stop=False)
                                mm(out, whi[s][:, wsl], y_lo[:, c, k, :], start=False, stop=False)
                                last = mm(out, wlo[s][:, wsl], y_hi[:, c, k, :], start=False, stop=(k == 3))
                        last.then_inc(w_used, 1)
                        n += 1

            def out_proj(l):
                pe.wait_ge(br_hi, KC)
                with pe.Fori(0, U_OUT // 4) as i:
                    for m in range(4):
                        unit_split(pe, l, i * 4 + (UM + U_IN + U_BR + m))
                        pe.wait_ge(resid, i * 4 + (KC + m + 1))
                        block_product(ps[m % 2][:, 0:T], m, h_hi, h_lo, [(c, c) for c in range(KC)], True,
                                      True).then_inc(w_used, 1)
                meet(pe, MEET["out", 0])

            with pe.Fori(0, L) as l:
                with pe.Fori(0, U_MOD // 4) as i:
                    for m in range(4):
                        pe.wait_ge(raw_loaded[m], (l * PER + i + 1) * 16)
                        for c in range(KC):
                            last = mm(ps[7][:, bass.ds(i * 8 + 2 * m, 2)], raw[m][:, c * P:(c + 1) * P],
                                      cond[:, c, :], start=(c == 0), stop=(c == KC - 1))
                        last.then_inc(mod_used, 1)
                ffn(l, 0, UF1)
                layer_norm(0)
                meet(pe, MEET["ln", 0])
                for it in items("hf", "hq", "hi", "hg"):
                    project(l, it)
                meet(pe, MEET["hg_in", 0])
                hgrn(l)
                meet(pe, MEET["hg", 0])
                normed(0)
                for it in items("mq", "mk", "gr", "mv", "mo"):
                    project(l, it)
                meet(pe, MEET["ml_in", 0])
                rows()
                keys_turned()
                meet(pe, MEET["rows", 0])
                mlstm()
                meet(pe, MEET["ml", 0])
                normed(1)
                meet(pe, MEET["mln", 0])
                for it in items("xbc", "mz"):
                    project(l, it)
                meet(pe, MEET["ssd_in", 0])
                ssd()
                meet(pe, MEET["ssd", 0])
                normed(2)
                meet(pe, MEET["br_in", 0])
                branches(l)
                out_proj(l)
                layer_norm(1)
                ffn(l, 1, UF2)
                layer_norm(2)
                meet(pe, MEET["end", 0])
                layer_over(pe, l, "pe")

        @block.scalar
        def _(act):
            af = nc.scalar.activation
            step = Steps(act, act_step)

            def hi(l, k4, m, width=KC * P):
                raw_ready(act, l, k4, m)
                slots_free(act, l, k4 * 4 + m)
                act.copy(whi[m % NSPLIT][:, 0:width], raw[m][:, 0:width]).then_inc(w_hi, 1)

            def hi_next(l, u):
                k = u + 1
                if k < U_SPLIT:
                    hi(l, k // 4, k % 4, UW if down_unit(k) else KC * P)

            act.wait_ge(start_loads, 16 * 10)
            af(cond_t[:, :, :], cond[:, :, :], ACT.Tanh, scale=0.5).then_inc(ready, 1)
            act.wait_ge(ready, 4)
            af(lb_w[:, 0:2, :], lb_w[:, 0:2, :], ACT.Exp).then_inc(ready, 1)

            def modulate(j):
                for n in range(KC):
                    k = KC * j + n
                    act.wait_ge(md_t, k + 1)
                    act.copy(h_hi[:, n, :], ht[n % 2][:, :]).then_inc(md_hi, 1)

            def layer_norm(j):
                for n in range(KC):
                    k = KC * j + n
                    act.wait_ge(ln_cent, k + 1)
                    if n >= 2:
                        act.wait_ge(ln_acc, k - 1)
                    af(sq[n % 2][:, :], x[:, n, :], ACT.Square).then_inc(ln_sq, 1)
                act.wait_ge(ln_acc, KC * (j + 1))
                af(std[:, :], ps[5][:, 0:T], ACT.Sqrt, bias=eps[:, 0:1]).then_inc(ln_std, 1)
                lnp = PAR["ln"] + 16 * j
                for n in range(KC):
                    act.wait_ge(ln_out, KC * j + n + 1)
                    af(x[:, n, :], x[:, n, :], ACT.Identity, bias=par[:, lnp + 8 + n:lnp + 9 + n],
                       scale=par[:, lnp + n:lnp + n + 1]).then_inc(ln_x, 1)

            def ffn(l, j, u0):
                hi(l, u0 // 4, 0)

                def gu(i, last):
                    for jj in range(2):
                        for part in range(2):
                            m = 2 * jj + part
                            if m < 3:
                                hi(l, i + u0 // 4, m + 1)
                            elif last:
                                hi(l, (u0 + U_GU) // 4, 0, UW)
                            else:
                                hi(l, i + (u0 // 4 + 1), 0)
                        unit_done(act, l, (i * 4) + (u0 + 2 * jj))
                        act.wait_ge(gated, i * 2 + (NF * j + jj + 1))
                        af(tb[jj][:, :], ps[2 * jj][:, 0:T], ACT.Tanh, scale=0.5).then_inc(gate_t, 1)

                with act.Fori(0, U_GU // 4 - 1) as i:
                    gu(i, False)
                gu(U_GU // 4 - 1, True)
                meet(act, MEET["ffn", j])
                gate = 2 if j == 0 else 8

                def down(i, last):
                    for jj in range(2):
                        hi(l, i + (u0 + U_GU) // 4, 2 * jj + 1, UW)
                        if jj == 0:
                            hi(l, i + (u0 + U_GU) // 4, 2, UW)
                        elif not last:
                            hi(l, i + ((u0 + U_GU) // 4 + 1), 0, UW)
                        elif j == 0:
                            hi(l, UM // 4, 0)
                        evac_gated(l, i * 4 + (u0 + U_GU + 2 * jj + 1), ps[jj], gate, i * 2 + jj,
                                   (0, 2 * KC)[j] + jj, i * 2, jj)

                with act.Fori(0, U_DOWN // 4 - 1) as i:
                    down(i, False)
                down(U_DOWN // 4 - 1, True)
                meet(act, MEET["down", j])

            def evac_gated(l, u, bank, gate, n, count, off, jj):
                unit_done(act, l, u)
                act.wait_ge(resid, off + (count + 1))
                for gi, (a, b) in enumerate(GROUPS):
                    col = mod[:, bass.ds(n + gate * KC, 1), gi]
                    last = af(vb[jj][:, a:b], bank[:, a:b], ACT.Copy, scale=col)
                last.then_inc(down_ev, 1)

            def project_out(l, item, body):
                kind, u, banks, what = item
                for m in range(1 if kind == "fm" else 4):
                    hi_next(l, UM + u + m)
                unit_done(act, l, UM + u + (0 if kind == "fm" else 3))
                for n in range(len(banks)):
                    body(n, ps[banks[n]]).then_inc(evac, 1)

            posts = {"n": 0}

            def tmp_free(buf_user):
                if buf_user > 0:
                    act.wait_ge(post, buf_user)

            def normed(b, src, groups, width):
                lnp = PAR["normg"] + 4 * b
                for t in range(NT):
                    n = b * NT + t
                    if t:
                        act.wait_ge(nm_ms, n)
                    af(nsq[:, :, :].rearrange("p a b -> p (a b)"), src(t), ACT.Square).then_inc(nm_sq, 1)
                    act.wait_ge(nm_ms, n + 1)
                    af(nsm[:, 1, 0:groups], nsm[:, 0, 0:groups], ACT.Sqrt, scale=1.0 / width,
                       bias=eps[:, 1:2]).then_inc(nm_sd, 1)
                    act.wait_ge(nm_tr, n + 1)
                    dst = (y_hg, y_ml, y_mb)[b]
                    for g in range(NH):
                        last = af(dst[:, g, t * P:(t + 1) * P], ps[0][:, g * P:(g + 1) * P], ACT.Copy,
                                  scale=par[:, lnp + g:lnp + g + 1])
                    last.then_inc(nm_out, 1)

            def hgrn(l):
                bgs = items("bg")
                bg = 0

                def bgout(item):
                    b = item[3][1]
                    project_out(l, item, lambda n, bank: af(gates[:, b, :], bank[:, 0:T], ACT.Tanh, scale=0.5))

                for o, (s, d, t, what, hh) in enumerate(ops):
                    if what != "diag":
                        act.wait_ge(hg_a, cnt["a", o])
                        if what == "state" and t:
                            af(etot[:, d, :], cc[:, d, :, t, P:C1].rearrange("p a b -> p (a b)"), ACT.Exp)
                        af(ea[o % 2][:, :, :], ea[o % 2][:, :, :], ACT.Exp).then_inc(hg_e, 1)
                    if o % 2 and bg < len(bgs):
                        bgout(bgs[bg])
                        bg += 1
                    if what == "level" and hh == 32 and s in (1, 2):
                        act.wait_ge(hg_c2, s)
                        act.dma_start(outs["hgrn"][l, s - 1], so[s - 1][:, :, :]).then_inc(stored, 16)
                for it in bgs[bg:]:
                    bgout(it)

            def rows():
                act.wait_ge(row_d, 1)
                af(r_e[:, :], r_w[:, :], ACT.Abs).then_inc(row_a, 1)
                act.wait_ge(row_a, 1)
                af(r_e[:, :], r_e[:, :], ACT.Exp, scale=-1.0).then_inc(row_a, 1)
                af(coef[:, :], par[:, PAR["row"] + 1:PAR["row"] + 2], ACT.Exp).then_inc(row_a, 1)
                act.wait_ge(row_d, 2)
                af(r_u[:, :], r_u[:, :], ACT.Ln).then_inc(row_a, 1)
                act.wait_ge(row_d, ROW_W)
                for t in range(NT):
                    last = af(x_2[0:64, t * P:(t + 1) * P], r_N[0:64, t * P:(t + 1) * P], ACT.Exp, scale=-1.0,
                              bias=minit[0:64, t:t + 1])
                af(x_3[:, :], x_3[:, :], ACT.Exp)
                af(x_4[:, :], x_4[:, :], ACT.Exp).then_inc(row_a, 1)
                for i, ti in enumerate((t_1, t_2, t_3, t_4)):
                    act.wait_ge(tr_pe, i + 1)
                    act.copy(ti[:, :, :].rearrange("p a b -> p (a b)"), ps[i % 2][:, 0:T]).then_inc(tr_act, 1)
                act.wait_ge(row_p, 1)
                act.mul(wb[:, :], ps[2][:, 0:P], float(D)).then_inc(row_a, 1)
                for t in range(NT):
                    act.wait_ge(tr_pe, 4 + t + 1)
                    act.copy(mkt[:, t, :], ps[3 + t % 2][:, :]).then_inc(tr_act, 1)

            def pair(r, rr):
                act.wait_ge(pr_x, r + 1)
                if r >= 2:
                    act.wait_ge(pr_s, r - 1)
                    if r <= 9:
                        act.wait_ge(ml_kw, min(r - 1, 8))
                for t in range(NT):
                    c = slice(t * P, (t + 1) * P)
                    last = af(pr[r % 2][:, c], pt[r % 2][:, c], ACT.Exp, bias=t_1[:, t, rr:rr + 1])
                last.then_inc(pr_e, 1)

            def mlstm(l):
                def weigh(r):
                    d, h = r % 2, r // 2
                    it, rr = ps[6 + r % 2], 32 * d + h
                    act.wait_ge(ml_i2, r + 1)
                    if r:
                        act.wait_ge(ml_h, r)
                    af(tmpa[:, 1 + d, :], it[:, 0:C1], ACT.Copy, scale=t_2[:, 1 + d, rr:rr + 1])
                    af(tmpa[:, 2 - d, :], it[:, C1:2 * C1], ACT.Copy,
                       scale=t_2[:, 2 - d, rr:rr + 1]).then_inc(ml_iw, 1)
                    act.dma_start(outs["mlstm"][l, d, h], co[r % 2][:, :]).then_inc(co_stored[r % 2], 16)

                pair(0, 0)
                for r in range(8):
                    if r < 7:
                        pair(r + 1, 32 * ((r + 1) % 2) + (r + 1) // 2)
                    weigh(r)

            def ssd(l):
                for b in range(6):
                    act.wait_ge(sd_w, b + 1)
                    if b:
                        act.wait_ge(post, POST_SSD + b)
                    af(cth[:, 0:386], cbuf[:, 0:386], ACT.Tanh, scale=0.5).then_inc(row_a, 1)
                meet(act, MEET["ssd_c", 0])
                for t in range(NT):
                    act.wait_ge(tr_pe, 7 + 2 * t + 1)
                    act.copy(xt[:, t, :], ps[5][:, :]).then_inc(tr_act, 1)
                    act.wait_ge(tr_pe, 7 + 2 * t + 2)
                    act.copy(bt[:, t, :], ps[6][:, 0:P]).then_inc(tr_act, 1)
                meet(act, MEET["ssd_x", 0])
                for d in range(2):
                    act.wait_ge(sd_o, (1, 5)[d])
                    act.dma_start(outs["ssd"][l, d], (ho0, ho1)[d][:, :, :]).then_inc(stored, 16)
                for r in range(16):
                    pair(8 + r, 64 + 32 * (r % 2) + r // 2)

            def branches(l):
                n = 0
                for b, yb in enumerate((y_hg, y_ml, y_mb)):
                    act.copy(y_hi[:, b, :, :], yb[:, :, :]).then_inc(br_a, 1)
                for mblk in range(4):
                    for c in range(3):
                        hi_next(l, UM + U_IN + 3 * mblk + c)

            def out_proj(l):
                u0 = UM + U_IN + U_BR

                def one(i, last):
                    for m in range(4):
                        if m < 3:
                            hi(l, i + u0 // 4, m + 1)
                        elif not last:
                            hi(l, i + (u0 // 4 + 1), 0)
                        evac_gated(l, i * 4 + (u0 + m), ps[m % 2], 5, i * 4 + m, KC + m, i * 4, m % 2)

                with act.Fori(0, U_OUT // 4 - 1) as i:
                    one(i, False)
                one(U_OUT // 4 - 1, True)
                meet(act, MEET["out", 0])

            with act.Fori(0, L) as l:
                step.n = 0
                act.dma_start(par[:, :], ins["par"][l]).then_inc(par_loaded, 16)
                modulate(0)
                ffn(l, 0, UF1)
                layer_norm(0)
                modulate(1)
                meet(act, MEET["ln", 0])
                act.dma_start(hs[:, :, :, :], ins["hgrn"][l]).then_inc(st_loaded, 16)
                nsil = 0
                for item in items("hf", "hq", "hi", "hg"):
                    what, b = item[3]
                    if what == "hf":
                        d, h = b // NH, b % NH

                        def body(n, bank):
                            af(cc[:, d, h, :, 1:C1], bank[:, 0:T].rearrange("p (a b) -> p a b", b=P), ACT.Copy)
                            return af(kk[:, d, h, :], bank[:, 0:T], ACT.Tanh, scale=-0.5)
                    elif what == "hq":
                        def body(n, bank):
                            nonlocal nsil
                            tmp_free(8 + nsil - 1 if nsil >= 2 else 0)
                            af(q[:, b, :], bank[:, 0:T], ACT.Copy, scale=0.5)
                            ins_ = af(ke[nsil % 2][:, 0:3, :].rearrange("p a b -> p (a b)"), bank[:, 0:T], ACT.Tanh,
                                      scale=0.5)
                            nsil += 1
                            return ins_
                    elif what == "hi":
                        def body(n, bank):
                            return act.copy(v[:, n, :], bank[:, :])
                    else:
                        def body(n, bank):
                            nonlocal nsil
                            tmp_free(8 + nsil - 1)
                            af(hgate[:, n, :], bank[:, :], ACT.Copy, scale=0.5)
                            ins_ = af(ke[nsil % 2][:, :, :].rearrange("p a b -> p (a b)"), bank[:, :], ACT.Tanh,
                                      scale=0.5)
                            nsil += 1
                            return ins_
                    project_out(l, item, body)
                for b in range(8):
                    act.wait_ge(post, b + 1)
                    dst = cc[:, b // NH, b % NH, :, 1:C1]
                    step(af(dst, dst, ACT.Exp, scale=-1.0))
                step.done()
                for b in range(8):
                    if b >= 2:
                        act.wait_ge(hg_lnd, b - 1)
                    dst = cc[:, b // NH, b % NH, :, 1:C1]
                    af(ea[b % 2][:, 0:3, :], dst, ACT.Ln, bias=1.0, scale=lb[:, b:b + 1])
                    af(dst, dst, ACT.Ln, bias=1.0).then_inc(hg_ln, 1)
                meet(act, MEET["hg_in", 0])
                hgrn(l)
                meet(act, MEET["hg", 0])
                normed(0, lambda t: ps[4 + t][:, :], NH, P)
                act.wait_ge(stored, l * (16 * STORES) + 32)
                act.dma_start(cs[:, :, :, :], ins["mlstm"][l]).then_inc(st_loaded, 16)
                for item in items("mq", "mk", "gr", "mv", "mo"):
                    what, b = item[3]
                    if what == "mq":
                        body = lambda n, bank: af(mq[:, b, :], bank[:, 0:T], ACT.Copy)
                    elif what == "mk":
                        body = lambda n, bank: af(mk[:, b, :], bank[:, 0:T], ACT.Copy, scale=P ** -0.5)
                    elif what == "gr":
                        body = lambda n, bank: act.copy((ga, gb)[b][:, :], bank[:, 0:T])
                    elif what == "mv":
                        body = lambda n, bank: act.copy(va[:, n, :, 0:P],
                                                        bank[:, :].rearrange("p (a b) -> p a b", b=P))
                    else:
                        body = lambda n, bank: af(mo[:, n, :], bank[:, :], ACT.Tanh, scale=0.5)
                    project_out(l, item, body)
                meet(act, MEET["ml_in", 0])
                rows()
                for d in range(2):
                    act.dma_start(outs["m"][l, d], mout[32 * d:32 * d + NH, :]).then_inc(stored, 16)
                meet(act, MEET["rows", 0])
                mlstm(l)
                meet(act, MEET["ml", 0])
                normed(1, lambda t: hout[:, t, :], NH, P)
                meet(act, MEET["mln", 0])
                act.dma_start(ht_s[:, :, :, :], ins["ssd"][l]).then_inc(st_loaded, 16)
                nmz = 0
                for item in items("xbc", "mz"):
                    what, b = item[3]
                    if what == "xbc":
                        def body(n, bank):
                            af(xpad[:, b, 1:1 + P], bank[:, 0:P], ACT.Copy)
                            return af(xpad[:, b, P + 3:3 + T], bank[:, P:T], ACT.Copy)
                    else:
                        def body(n, bank):
                            tmp_free(POST_MZ + n if n else 0)
                            af(mz[:, n, :], bank[:, :], ACT.Copy, scale=0.5)
                            return af(zth[:, :], bank[:, :], ACT.Tanh, scale=0.5)
                    project_out(l, item, body)
                meet(act, MEET["ssd_in", 0])
                ssd(l)
                meet(act, MEET["ssd", 0])
                act.wait_ge(stored, l * (16 * STORES) + 16 * STORES)
                for p_ in range(2):
                    act.wait_ge(co_stored[p_], (l + 1) * 64)
                normed(2, lambda t: mz[:, t, :], 1, MIX)
                meet(act, MEET["br_in", 0])
                branches(l)
                out_proj(l)
                layer_norm(1)
                modulate(2)
                ffn(l, 1, UF2)
                layer_norm(2)
                meet(act, MEET["end", 0])
                layer_over(act, l, "act")

        @block.vector
        def _(dve):
            tt, ts, stt = nc.vector.tensor_tensor, nc.vector.tensor_scalar, nc.vector.scalar_tensor_tensor
            cp = nc.vector.tensor_copy
            step = Steps(dve, dve_step)

            nc.vector.memset(eps[:, 0:1], LN_EPS)
            nc.vector.memset(eps[:, 1:2], RMS_EPS)
            dve.wait_ge(start_loads, 16 * 10)
            dve.wait_ge(ready, 1)
            stt(cond_t[:, :, :], cond_t[:, :, :], 1.0, cond[:, :, :], ALU.add, ALU.mult).then_inc(ready, 1)
            dve.wait_ge(ready, 2)
            ts(cond[:, :, :], cond_t[:, :, :], 0.5, None, ALU.mult).then_inc(ready, 1)
            tt(x[:, :, P:T], x[:, :, P:T], pos[:, :, :], ALU.add)
            cp(hmask[:, :, :, :], hmask_in[:, :, :, :]).then_inc(start_v, 1)
            tt(lb_w[:, 2, :], lb_in[:, 0, :], lb_in[:, 1, :], ALU.max).then_inc(start_v, 1)
            dve.wait_ge(start_v, 2)
            tt(lb_w[:, 0:2, :], lb_in[:, :, :], lb_w[:, 2:3, :].to_broadcast([P, 2, 8]),
               ALU.subtract).then_inc(ready, 1)
            nc.vector.memset(lbs[:, 0, :], 0.0)
            dve.wait_ge(ready, 5)
            tt(lb_w[:, 2, :], lb_w[:, 0, :], lb_w[:, 1, :], ALU.add).then_inc(start_v, 1)
            dve.wait_ge(start_v, 3)
            nc.vector.reciprocal(lb_w[:, 3, :], lb_w[:, 2, :]).then_inc(start_v, 1)
            dve.wait_ge(start_v, 4)
            tt(lbs[:, 1, :], lb_w[:, 1, :], lb_w[:, 3, :], ALU.mult).then_inc(start_v, 1)
            dve.wait_ge(start_v, 5)

            def modulate(j):
                def low(n):
                    dve.wait_ge(md_hi, KC * j + n + 1)
                    tt(h_lo[:, n, :], ht[n % 2][:, :], h_hi[:, n, :].bitcast(F32),
                       ALU.subtract).then_inc(md_lo, 1)

                sh, sc = 3 * j * KC, (3 * j + 1) * KC
                for n in range(KC):
                    if j:
                        dve.wait_ge(ln_x, KC * (j - 1) + n + 1)
                    if n >= 2:
                        dve.wait_ge(md_lo, KC * j + n - 1)
                    for gi, (a, b) in enumerate(GROUPS):
                        last = ts(ht[n % 2][:, a:b], x[:, n, a:b], mod[:, sc + n, gi:gi + 1],
                                  mod[:, sh + n, gi:gi + 1], ALU.mult, ALU.add)
                    last.then_inc(md_t, 1)
                    if n:
                        low(n - 1)
                low(KC - 1)

            def layer_norm(j):
                dve.wait_ge(ln_mean, j + 1)
                for n in range(KC):
                    tt(x[:, n, :], x[:, n, :], ps[4][:, 0:T], ALU.subtract).then_inc(ln_cent, 1)
                dve.wait_ge(ln_std, j + 1)
                step(nc.vector.reciprocal(rstd[:, :], std[:, :]))
                step.done()
                for n in range(KC):
                    tt(x[:, n, :], x[:, n, :], rstd[:, :], ALU.mult).then_inc(ln_out, 1)

            def ffn(l, j, u0):
                n0 = step.n
                with dve.Fori(0, U_GU // 4) as i:
                    step.off = i * 6
                    for jj in range(2):
                        dve.wait_ge(gate_t, i * 2 + (NF * j + jj + 1))
                        step(stt(sbf[jj][:, :], tb[jj][:, :], 1.0, ps[2 * jj][:, 0:T], ALU.add, ALU.mult))
                        unit_done(dve, l, i * 4 + (u0 + 2 * jj + 1))
                        step.done()
                        stt(vb[jj][:, :], sbf[jj][:, :], 0.5, ps[2 * jj + 1][:, 0:T], ALU.mult,
                            ALU.mult).then_inc(gated, 1)
                        dve.wait_ge(gated, i * 2 + (NF * j + jj + 3))
                        f = i * 2 + jj
                        step(cp(act_hi[:, bass.ds(f, 1), :], vb[jj][:, :].unsqueeze(1)))
                        step.done()
                        step(tt(act_lo[:, bass.ds(f, 1), :], vb[jj][:, :].unsqueeze(1),
                                act_hi[:, bass.ds(f, 1), :].bitcast(F32), ALU.subtract))
                assert step.n - n0 == 6
                step.off, step.n = 0, n0 + 6 * (U_GU // 4)
                meet(dve, MEET["ffn", j])
                down(l, 2 * KC * j, U_DOWN // 4, 2)
                meet(dve, MEET["down", j])

            def down(l, c0, iters, per):
                with dve.Fori(0, iters) as i:
                    for jj in range(per):
                        dve.wait_ge(down_ev, i * per + (c0 + jj + 1))
                        xb = x[:, bass.ds(i * per + jj, 1), :]
                        stt(xb, xb, ALPHA, vb[jj % 2][:, :].unsqueeze(1), ALU.mult, ALU.add).then_inc(resid, 1)

            def normed(b, src, gate, groups, width):
                for t in range(NT):
                    n = b * NT + t
                    dve.wait_ge(nm_sq, n + 1)
                    nc.vector.reduce_sum(nsm[:, 0, 0:groups],
                                         nsq[:, :, :].rearrange("p a b -> p (a b)").rearrange(
                                             "p (g e) -> p g e", g=groups), axis=AX.X).then_inc(nm_ms, 1)
                    dve.wait_ge(nm_sd, n + 1)
                    step(nc.vector.reciprocal(nsm[:, 2, 0:groups], nsm[:, 1, 0:groups]))
                    step.done()
                    if t:
                        dve.wait_ge(nm_tr, n)
                    out = nyn[:, :, :]
                    if groups == 1:
                        ts(out.rearrange("p a b -> p (a b)"), src(t), nsm[:, 2, 0:1], None,
                           ALU.mult).then_inc(nm_y, 1)
                        continue
                    step(tt(out, src(t).rearrange("p (a b) -> p a b", b=P),
                            nsm[:, 2, :].unsqueeze(2).to_broadcast([P, NH, P]), ALU.mult))
                    step.done()
                    flat = out.rearrange("p a b -> p (a b)")
                    tt(flat, flat, gate[:, t, :], ALU.mult).then_inc(nm_y, 1)

            def hgrn_in():
                for item in items("hf", "hq", "hi", "hg"):
                    what, b = item[3]
                    e = first_evac[item[3]]
                    if what == "hf":
                        dve.wait_ge(evac, e + 1)
                        dst = cc[:, b // NH, b % NH, :, 1:C1]
                        ts(dst, dst, -44.0, None, ALU.max)
                        kb = kk[:, b // NH, b % NH, :]
                        ts(kb, kb, 1.0, om[:, b:b + 1], ALU.add, ALU.mult).then_inc(post, 1)
                    elif what == "hq":
                        dve.wait_ge(evac, e + 1)
                        stt(q[:, b, :], ke[b % 2][:, 0:3, :].rearrange("p a b -> p (a b)"), 1.0, q[:, b, :],
                            ALU.add, ALU.mult).then_inc(post, 1)
                    elif what == "hg":
                        for n in range(NT):
                            dve.wait_ge(evac, e + n + 1)
                            stt(hgate[:, n, :], ke[n % 2][:, :, :].rearrange("p a b -> p (a b)"), 1.0,
                                hgate[:, n, :], ALU.add, ALU.mult).then_inc(post, 1)
                for b in range(8):
                    dve.wait_ge(hg_ln, b + 1)
                    dst = cc[:, b // NH, b % NH, :, 1:C1]
                    tt(dst, ea[b % 2][:, 0:3, :], dst, ALU.subtract).then_inc(hg_lnd, 1)
                dve.wait_ge(hg_lnd, 8)
                step(nc.vector.memset(cc[:, :, :, :, 0:1].rearrange("p a b c d -> p (a b c d)"), 0.0))
                step.done()
                for b in range(8):
                    row = cc[:, b // NH, b % NH, :, :].rearrange("p a b -> p (a b)")
                    step(nc.vector.tensor_tensor_scan(row, keep[:, :], row, 0.0, ALU.mult, ALU.add))
                for a in (*qe, *ke, *att):
                    step(nc.vector.memset(a[:, :, :], 0.0))
                step.done()

            def hgrn():
                ph = lambda a, hh: a.rearrange("p g (b two h) -> p g b two h", two=2, h=hh)

                def exponents(o):
                    s, d, t, what, hh = ops[o]
                    if what == "diag":
                        return
                    e, ct = ea[o % 2], cc[:, d, :, t, :]
                    v_ = ct[:, :, 1 - d:C1 - d]
                    tot = ct[:, :, P:C1].to_broadcast([P, NH, P])
                    if o >= 2:
                        dve.wait_ge(hg_b, cnt["b", o - 2])
                    if what == "level":
                        nb = P // (2 * hh)
                        ev, vv = ph(e[:, :, :], hh), ph(v_, hh)
                        mid = ct[:, :, hh:C1:2 * hh].unsqueeze(3).to_broadcast([P, NH, nb, hh])
                        tt(ev[:, :, :, 0, :], mid, vv[:, :, :, 0, :], ALU.subtract)
                        tt(ev[:, :, :, 1, :], vv[:, :, :, 1, :], mid, ALU.subtract).then_inc(hg_a, 1)
                    elif (what == "inter") == (d == 0):
                        cp(e[:, :, :], v_).then_inc(hg_a, 1)
                    else:
                        tt(e[:, :, :], tot, v_, ALU.subtract).then_inc(hg_a, 1)

                def products(o):
                    s, d, t, what, hh = ops[o]
                    if what == "diag":
                        return
                    c = slice(t * P, (t + 1) * P)
                    b, qv, kv = o % 2, q[:, :, c], kk[:, d, :, c]
                    dve.wait_ge(hg_e, cnt["e", o])
                    if o >= 2:
                        dve.wait_ge(hg_m, o - 1)
                    if what == "level":
                        ev = ph(ea[b][:, :, :], hh)
                        qs, ks = 1 - d, d
                        tt(ph(qe[b][:, :, :], hh)[:, :, :, qs, :], ph(qv, hh)[:, :, :, qs, :],
                           ev[:, :, :, qs, :], ALU.mult)
                        tt(ph(ke[b][:, :, :], hh)[:, :, :, ks, :], ph(kv, hh)[:, :, :, ks, :],
                           ev[:, :, :, ks, :], ALU.mult).then_inc(hg_b, 1)
                    elif what == "inter":
                        tt(qe[b][:, :, :], qv, ea[b][:, :, :], ALU.mult).then_inc(hg_b, 1)
                    else:
                        tt(ke[b][:, :, :], kv, ea[b][:, :, :], ALU.mult).then_inc(hg_b, 1)

                def take(o):
                    s, d, t, what, hh = ops[o]
                    if what == "inter":
                        return
                    S = ps[2 + o % 2][:, :].rearrange("p (a b) -> p a b", b=P)
                    dve.wait_ge(hg_m, o + 1)
                    if o:
                        dve.wait_ge(hg_c, cnt["c", o] - 1)
                    if what == "state":
                        if s:
                            dve.wait_ge(hg_m2, s)
                        cp(kT[:, :, :], S).then_inc(hg_c, 1)
                        return
                    lev = LEVELS.index(hh) if what == "level" else len(LEVELS)
                    if lev == 0 and s >= 2:
                        dve.wait_ge(hg_o, s - 1)
                    nc.vector.copy_predicated(att[d][:, :, :], hmask[:, d, lev:lev + 1, :].to_broadcast(
                        [P, NH, P]), S).then_inc(hg_c, 1)

                def states(o):
                    s, d, t, what, hh = ops[o]
                    if what != "state":
                        return
                    dve.wait_ge(hg_m2, s + 1)
                    if t == 0:
                        cp(so[d][:, :, :], ps[7][:, :].rearrange("p (a b) -> p a b", b=P)).then_inc(hg_c2, 1)
                        return
                    dve.wait_ge(st_loaded, 16)
                    for g in range(NH):
                        last = stt(hs[:, d, g, :], hs[:, d, g, :], etot[:, d, g:g + 1],
                                   ps[7][:, g * P:(g + 1) * P], ALU.mult, ALU.add)
                    last.then_inc(hg_c2, 1)

                exponents(0)
                for o in range(len(ops)):
                    if o + 1 < len(ops):
                        exponents(o + 1)
                    products(o)
                    if o:
                        take(o - 1)
                    if o >= 2:
                        states(o - 2)
                take(len(ops) - 1)

            def rows():
                pr_ = PAR["row"]
                col = lambda i: par[:, pr_ + i:pr_ + i + 1]
                fw, bw, f64, b96 = slice(0, 32), slice(32, 64), slice(64, 96), slice(96, 128)
                inc_ = cr[:, :, 1:C1]
                exc = cr[:, :, 0:P]
                v3 = lambda a: a[:, :].rearrange("p (a b) -> p a b", b=P)

                def s_(ins):
                    step(ins)
                    step.done()

                ts(r_w[:, :], ga[:, :], col(0), sgn[:, :], ALU.add, ALU.mult).then_inc(row_d, 1)
                dve.wait_ge(row_d, 1)
                dve.wait_ge(row_a, 2)
                s_(ts(r_u[:, :], r_e[:, :], 1.0, None, ALU.add))
                stt(r_n[:, :], r_u[:, :], -1.0, r_e[:, :], ALU.add, ALU.subtract).then_inc(row_d, 1)
                dve.wait_ge(row_d, 2)
                dve.wait_ge(row_a, 4)
                s_(tt(r_u[:, :], r_u[:, :], r_n[:, :], ALU.subtract))
                s_(stt(r_w[:, :], r_w[:, :], 0.0, r_u[:, :], ALU.max, ALU.add))
                s_(nc.vector.memset(cr[:, :, 0:1].rearrange("p a b -> p (a b)"), 0.0))
                s_(ts(inc_, v3(r_w), coef[:, :], -1.0, ALU.mult, ALU.mult))
                flat = cr[:, :, :].rearrange("p a b -> p (a b)")
                s_(nc.vector.tensor_tensor_scan(flat, keep[:, :], flat, 0.0, ALU.mult, ALU.add))
                s_(ts(gb[:, :], gb[:, :], col(2), None, ALU.add))
                step(tt(v3(x_1)[fw], v3(gb)[fw], inc_[fw], ALU.subtract))
                step(tt(v3(x_1)[bw], v3(gb)[bw], exc[bw], ALU.add))
                step(ts(v3(x_1)[f64], inc_[f64], -1.0, None, ALU.mult))
                step(cp(v3(x_1)[b96], exc[b96]))
                step(cp(v3(x_5)[f64], inc_[f64]))
                step(ts(v3(x_5)[b96], exc[b96], -1.0, None, ALU.mult))
                step(cp(x_2[64:128, :], r_w[64:128, :]))
                step(nc.vector.memset(minit[:, 0:1], 0.0))
                step.done()
                s_(cp(minit[fw, 1:2], par[fw, pr_ + 3:pr_ + 4]))
                s_(cp(minit[bw, 0:1], cr[bw, 0, P:C1]))
                s_(tt(minit[bw, 2:3], par[bw, pr_ + 3:pr_ + 4], cr[bw, 2, P:C1], ALU.add))

                def running(t, back):
                    r = bw if back else fw
                    c = slice(t * P, (t + 1) * P)
                    a, n_ = x_1[r, c], r_N[r, c]
                    if back:
                        a, n_ = a[:, ::-1], n_[:, ::-1]
                    s_(nc.vector.tensor_tensor_scan(n_, a, a, minit[r, t:t + 1], ALU.max, ALU.max))

                running(0, False)
                running(0, True)
                running(1, False)
                running(2, True)
                s_(tt(minit[fw, 2:3], r_N[fw, 2 * P - 1:2 * P], cr[fw, 1, P:C1], ALU.add))
                s_(tt(minit[bw, 1:2], r_N[bw, 2 * P:2 * P + 1], cr[bw, 1, P:C1], ALU.add))
                running(2, False)
                running(1, True)
                step(tt(mout[fw, :], r_N[fw, P - 1:P], cr[fw, 0, P:C1], ALU.add))
                step(cp(mout[bw, :], r_N[bw, 0:1]))
                step(ts(x_5[0:64, :], r_N[0:64, :], -1.0, None, ALU.mult))
                step(stt(v3(x_3)[fw], inc_[fw], -1.0, v3(r_N)[fw], ALU.mult, ALU.subtract))
                step(tt(v3(x_3)[bw], exc[bw], v3(r_N)[bw], ALU.subtract))
                step(cp(v3(x_3)[f64], inc_[f64]))
                tot = cr[:, :, P:C1].to_broadcast([P, NT, P])
                step(tt(v3(x_3)[b96], tot[b96], exc[b96], ALU.subtract))
                step(nc.vector.memset(x_4[0:64, :], 0.0))
                step(tt(v3(x_4)[f64], tot[f64], inc_[f64], ALU.subtract))
                cp(v3(x_4)[b96], exc[b96]).then_inc(row_d, 1)
                dve.wait_ge(row_d, 3)
                dve.wait_ge(row_a, 5)
                step(cp(lastw[fw, :], x_2[fw, 2 * P - 1:2 * P]))
                step(cp(lastw[bw, :], x_2[bw, 2 * P:2 * P + 1]))
                step(cp(lastw[f64, :], x_3[f64, 2 * P - 1:2 * P]))
                s_(cp(lastw[b96, :], x_3[b96, 2 * P:2 * P + 1]))
                ts(dlast[:, :], ident[:, :], lastw[:, :], None, ALU.mult).then_inc(row_d, 1)
                dve.wait_ge(row_d, 4)
                step(nc.vector.memset(va[:, :, :, P:C1].rearrange("p a b c -> p (a b c)"), 1.0))
                s_(ts(mo[:, :, :], mo[:, :, :], 0.5, 0.5, ALU.mult, ALU.add))

            def exps(r, d):
                dve.wait_ge(pr_bc, r + 1)
                if r >= 2:
                    dve.wait_ge(pr_e, r - 1)
                tt(pt[r % 2][:, :].rearrange("p (a b) -> p a b", b=P),
                   neg[:, d:d + 1, :].to_broadcast([P, NT, P]),
                   ps[r % 2][:, 0:T].rearrange("p (a b) -> p a b", b=P), ALU.add).then_inc(pr_x, 1)

            def scores(r, bank, nqk, rr=None):
                dve.wait_ge(pr_e, r + 1)
                dve.wait_ge(pr_qk, nqk)
                if r >= 2:
                    dve.wait_ge(pr_n, r - 1)
                if rr is None:
                    tt(st[r % 2][:, :], pr[r % 2][:, :], bank[:, 0:T], ALU.mult).then_inc(pr_s, 1)
                    return
                for t in range(NT):
                    c = slice(t * P, (t + 1) * P)
                    last = stt(st[r % 2][:, c], pr[r % 2][:, c], t_2[:, t, rr:rr + 1], bank[:, c], ALU.mult, ALU.mult)
                last.then_inc(pr_s, 1)

            def mlstm(l):
                def weights(r):
                    h, d = r // 2, r % 2
                    if r >= 2:
                        dve.wait_ge(ml_it, r - 1)
                    for n, t in enumerate((0, 1 + d)):
                        lastc = t * P + (P - 1 if d == 0 else 0)
                        last = ts(kw[r % 2][:, n, :], mkt[:, t, h * P:(h + 1) * P],
                                  pr[r % 2][:, lastc:lastc + 1], None, ALU.mult)
                    last.then_inc(ml_kw, 1)

                def carry(r):
                    h, d = r // 2, r % 2
                    dve.wait_ge(ml_it, r + 1)
                    if r >= 2:
                        dve.wait_ge(co_stored[r % 2], l * 64 + 16 * (r // 2))
                    it = ps[6 + r % 2]
                    cp(co[r % 2][:, :], it[:, C1:2 * C1])
                    rr = 32 * d + h
                    stt(cs[:, d, h, :], cs[:, d, h, :], wb[:, rr:rr + 1], it[:, 2 * C1:3 * C1], ALU.mult,
                        ALU.add).then_inc(ml_cu, 1)

                def heads(r):
                    h, d = r // 2, r % 2
                    rr = 32 * d + h
                    dve.wait_ge(pr_n, r + 1)
                    dve.wait_ge(ml_iw, r + 1)
                    nm = ps[4 + r % 2][:, 0:3 * C1].rearrange("p (a b) -> p a b", b=C1)
                    step(cp(tmpb[:, 0, :], nm[:, 0, :]))
                    step(tt(tmpb[:, 1:3, :], tmpa[:, 1:3, :], nm[:, 1:3, :], ALU.add))
                    step.done()
                    dn = tmpb[:, :, P:C1].rearrange("p a b -> p (a b)")
                    step(stt(den[:, 0, :], dn, -1.0, dn, ALU.mult, ALU.max))
                    step.done()
                    step(tt(den[:, 0, :], den[:, 0, :], t_3[:, :, rr], ALU.max))
                    step.done()
                    step(nc.vector.reciprocal(den[:, 1, :], den[:, 0, :]))
                    step.done()
                    for t in range(NT):
                        dst = hout[:, t, h * P:(h + 1) * P]
                        if d == 0:
                            last = ts(dst, tmpb[:, t, 0:P], den[:, 1, t:t + 1], None, ALU.mult)
                        else:
                            last = stt(dst, tmpb[:, t, 0:P], den[:, 1, t:t + 1], dst, ALU.mult, ALU.add)
                    last.then_inc(ml_h, 1)

                exps(0, 0)
                for r in range(8):
                    if r < 7:
                        exps(r + 1, (r + 1) % 2)
                    scores(r, ps[2 + r // 2 % 2], r // 2 + 1)
                    weights(r)
                    if r:
                        heads(r - 1)
                    carry(r)
                heads(7)

            def ssd():
                for b in range(6):
                    w0 = PAR["convw"] + 3 * b
                    tap = lambda j: par[:, w0 + j:w0 + j + 1]
                    bias = par[:, PAR["convb"] + b:PAR["convb"] + b + 1]
                    if b:
                        dve.wait_ge(post, POST_SSD + b)
                    step(ts(cbuf[:, 0:386], xpad[:, b, 1:387], tap(1), bias, ALU.mult, ALU.add))
                    step.done()
                    step(stt(cbuf[:, 0:386], xpad[:, b, 0:386], tap(0), cbuf[:, 0:386], ALU.mult, ALU.add))
                    step.done()
                    stt(cbuf[:, 0:386], xpad[:, b, 2:388], tap(2), cbuf[:, 0:386], ALU.mult,
                        ALU.add).then_inc(sd_w, 1)
                    dve.wait_ge(row_a, 7 + b)
                    step(ts(cth[:, 0:386], cth[:, 0:386], 0.5, 0.5, ALU.mult, ALU.add))
                    step.done()
                    step(tt(xs[:, b, 0:P], cth[:, 0:P], cbuf[:, 0:P], ALU.mult))
                    tt(xs[:, b, P:T], cth[:, P + 2:T + 2], cbuf[:, P + 2:T + 2], ALU.mult).then_inc(post, 1)
                meet(dve, MEET["ssd_c", 0])
                meet(dve, MEET["ssd_x", 0])
                v8 = lambda a: a.rearrange("p (h e) -> p h e", e=SP_)
                rows8 = lambda a, t, d: a[:, t, 64 + 32 * d:72 + 32 * d].unsqueeze(2).to_broadcast([P, SH, SP_])
                n = 0
                for d in range(2):
                    def weigh(t):
                        step(tt(v8(xw[:, :]), v8(xt[:, t, :]), rows8(t_2, t, d), ALU.mult))
                        step.done()
                        tt(v8(xw[:, :]), v8(xw[:, :]), rows8(t_4, t, d), ALU.mult).then_inc(sd_w, 1)

                    weigh(0)
                    for stp, t in enumerate((0, 1 + d, 2 - d)):
                        if stp:
                            dve.wait_ge(sd_p, n + 1)
                            dst = yx[:, t - 1, :]
                            for g in range(2):
                                half = slice(256 * g, 256 * g + 256)
                                last = tt(v8((dst, zth)[d][:, half]), v8(ps[(7, 2)[g]][:, 0:256]),
                                          rows8(t_3, t, d)[:, 4 * g:4 * g + 4, :], ALU.mult)
                            if d == 0:
                                last.then_inc(sd_o, 1)
                            else:
                                step(last)
                                step.done()
                                tt(dst, dst, zth[:, :], ALU.add).then_inc(sd_o, 1)
                                dve.wait_ge(sd_o, n + 1)
                            n += 1
                        if stp < 2:
                            dve.wait_ge(sd_p, n + 1)
                            for g in range(2):
                                gp = slice(64 * g, 64 * g + 64)
                                src = ps[3][gp, 256 * g:256 * g + 256].rearrange("p (h e) -> p h e", e=SP_)
                                if stp == 0:
                                    last = cp((ho0, ho1)[d][gp, :, :], src)
                                else:
                                    h0 = 64 + 32 * d + 4 * g
                                    step(tt(ht_s[gp, d, :, :], ht_s[gp, d, :, :],
                                            wb[gp, h0:h0 + 4].unsqueeze(2).to_broadcast([64, 4, SP_]), ALU.mult))
                                    step.done()
                                    last = tt(ht_s[gp, d, :, :], ht_s[gp, d, :, :], src, ALU.add)
                            last.then_inc(sd_o, 1)
                            n += 1
                            if stp == 0:
                                weigh(1 + d)
                exps(8, 0)
                for r in range(16):
                    if r < 15:
                        exps(9 + r, (r + 1) % 2)
                    scores(8 + r, ps[2], 5 + r // 8, 64 + 32 * (r % 2) + r // 2)
                dve.wait_ge(pr_n, 24)
                for t in range(NT):
                    y = xt[:, t, :]
                    md = par[:, PAR["mbd"]:PAR["mbd"] + 8].unsqueeze(2).to_broadcast([P, SH, SP_])
                    step(tt(v8(y), v8(y), md, ALU.mult))
                    step.done()
                    step(tt(y, y, ps[4 + t][:, :], ALU.add))
                    step.done()
                    if t:
                        step(tt(y, y, yx[:, t - 1, :], ALU.add))
                        step.done()
                    step(tt(mz[:, t, :], mz[:, t, :], y, ALU.mult))

            def branches(l):
                for b, yb in enumerate((y_hg, y_ml, y_mb)):
                    dve.wait_ge(br_a, b + 1)
                    tt(y_lo[:, b, :, :], yb[:, :, :], y_hi[:, b, :, :].bitcast(F32),
                       ALU.subtract).then_inc(br_y, 1)
                n = 0
                for mblk in range(4):
                    z = (zt0, zt1)[mblk % 2]
                    for c in range(3):
                        unit_done(dve, l, UM + U_IN + n)
                        for j in range(2):
                            bank = ps[2 * (n % 2) + j][:, 0:T]
                            gt = gates[:, 8 * c + 2 * mblk + j, :]
                            if c == 0:
                                if mblk >= 2:
                                    dve.wait_ge(br_hi, 2 * (mblk - 1))
                                last = stt(z[:, j, :], gt, 1.0, bank, ALU.add, ALU.mult)
                            else:
                                last = stt(gt, gt, 1.0, bank, ALU.add, ALU.mult)
                        last.then_inc(br_z, 1)
                        if c:
                            dve.wait_ge(br_z, n + 1)
                            g2 = gates[:, 8 * c + 2 * mblk:8 * c + 2 * mblk + 2, :]
                            step(tt(z[:, :, :], z[:, :, :], g2, ALU.add))
                            step.done()
                        n += 1
                    step.done()
                    ts(z[:, :, :], z[:, :, :], 0.5, None, ALU.mult).then_inc(br_z2, 1)
                    dve.wait_ge(br_z2, mblk + 1)
                    for j in range(2):
                        k = 2 * mblk + j
                        step(cp(h_hi[:, k, :], z[:, j, :]))
                        step.done()
                        tt(h_lo[:, k, :], z[:, j, :], h_hi[:, k, :].bitcast(F32),
                           ALU.subtract).then_inc(br_hi, 1)

            with dve.Fori(0, L) as l:
                step.n = 0
                for _ in range(2):
                    dve.sem_inc(gated, 1)
                    dve.sem_inc(resid, 1)
                step(cp(lb[:, :], lbs[:, bass.ds(l, 1), :].rearrange("p a b -> p (a b)")))
                step.done()
                step(ts(om[:, :], lb[:, :], -0.5, 0.5, ALU.mult, ALU.add))
                dve.wait_ge(par_loaded, (l + 1) * 16)
                dve.wait_ge(mod_used, l * U_MOD + (U_MOD + NRAW))
                step(tt(mod[:, :, :], ps[7][:, 0:144].rearrange("p (a b) -> p a b", b=2),
                        par[:, PAR["bmod"]:PAR["bmod"] + 72].unsqueeze(2).to_broadcast([P, 72, 2]), ALU.add))
                step.done()
                for j in range(3):
                    sc = mod[:, (3 * j + 1) * KC:(3 * j + 2) * KC, :]
                    step(ts(sc, sc, 1.0, None, ALU.add))
                for j in (2, 8):
                    g = mod[:, j * KC:(j + 1) * KC, :]
                    step(ts(g, g, 0.5, None, ALU.mult))
                step.done()
                modulate(0)
                ffn(l, 0, UF1)
                layer_norm(0)
                modulate(1)
                meet(dve, MEET["ln", 0])
                hgrn_in()
                meet(dve, MEET["hg_in", 0])
                hgrn()
                meet(dve, MEET["hg", 0])
                normed(0, lambda t: ps[4 + t][:, :], hgate, NH, P)
                meet(dve, MEET["ml_in", 0])
                rows()
                meet(dve, MEET["rows", 0])
                mlstm(l)
                meet(dve, MEET["ml", 0])
                normed(1, lambda t: hout[:, t, :], mo, NH, P)
                meet(dve, MEET["mln", 0])
                for c in (0, P + 1, P + 2, T + 3):
                    step(nc.vector.memset(xpad[:, :, c:c + 1].rearrange("p a b -> p (a b)"), 0.0))
                for n in range(NT):
                    dve.wait_ge(evac, first_evac["mz", 0] + n + 1)
                    stt(mz[:, n, :], zth[:, :], 1.0, mz[:, n, :], ALU.add, ALU.mult).then_inc(post, 1)
                meet(dve, MEET["ssd_in", 0])
                ssd()
                meet(dve, MEET["ssd", 0])
                normed(2, lambda t: mz[:, t, :], None, 1, MIX)
                meet(dve, MEET["br_in", 0])
                branches(l)
                down(l, KC, U_OUT // 4, 4)
                meet(dve, MEET["out", 0])
                layer_norm(1)
                modulate(2)
                ffn(l, 1, UF2)
                layer_norm(2)
                meet(dve, MEET["end", 0])
                layer_over(dve, l, "dve")


def cols(m, order):
    return np.concatenate([m[..., a:b] for a, b in order], axis=-1)


def constants():
    i = np.arange(P)
    s, t = i[:, None], i[None, :]
    neg = np.stack([np.where(s <= t, 0.0, NEG), np.where(s >= t, 0.0, NEG)], 1).astype(np.float32)
    hm = np.zeros((P, 2, len(LEVELS) + 1, P), np.float32)
    for n, h in enumerate(LEVELS):
        same = s // (2 * h) == t // (2 * h)
        sf, tf = s % (2 * h) < h, t % (2 * h) < h
        hm[:, 0, n], hm[:, 1, n] = same & sf & ~tf, same & ~sf & tf
    hm[:, 0, -1] = hm[:, 1, -1] = s == t
    keep = np.ones((P, NT, C1), np.float32)
    keep[:, :, 0] = 0.0
    sgn = np.where(i < 64, -1.0, 1.0).astype(np.float32)[:, None]
    width, quarter = 64, D // 4
    n = np.arange(NL_TOK)
    freq = np.exp(-math.log(10000.0) * np.arange(quarter, dtype=np.float32) / quarter).astype(np.float32)
    ar = (n // width).astype(np.float32)[:, None] * freq
    ac = (n % width).astype(np.float32)[:, None] * freq
    pos = np.concatenate([np.sin(ar), np.cos(ar), np.sin(ac), np.cos(ac)], -1).astype(np.float32)
    return {"ident": np.eye(P, dtype=np.float32), "mean_w": np.full((P, P), 1.0 / D, np.float32), "neg": neg,
            "hmask": hm, "keep": keep.reshape(P, -1), "sgn": sgn, "pos": pos.T.reshape(KC, P, NL_TOK)
            .transpose(1, 0, 2).copy()}


def laid_out(a):
    a = {k: np.asarray(v) for k, v in a.items()}
    f = np.ascontiguousarray

    def units(w, n):
        lead = w.shape[:-2]
        K, N = w.shape[-2:]
        w = w.reshape(*lead, K // P, P, N // n, n)
        return np.moveaxis(w, (-2, -3, -4, -1), (-4, -3, -2, -1)).reshape(*lead, N // n, P, K // P * n)

    r = {}
    xt = np.concatenate([a["x_prompt"][0], a["x_sample"][0]], 0).T.reshape(KC, P, T)
    r["x"] = f(xt.transpose(1, 0, 2))
    r["cond"] = f(np.stack([a["c_ctx"], a["c"][0]], -1).reshape(KC, P, 2).transpose(1, 0, 2))
    r["hg_lb"] = f(a["hg_lb"].reshape(L, 8, P).transpose(2, 0, 1))
    r["w_mod"] = f(units(a["w_mod"], P))
    gu = units(a["ffn_w_gu"], P)
    gu = gu.reshape(L, 2, 2, NF, P, KC * P)
    r["w_gu"] = f(gu.transpose(0, 1, 3, 2, 4, 5).reshape(L, 2, U_GU, P, KC * P))
    dn = units(a["ffn_w_down"], P).reshape(L, 2, KC, P, 2, UW)
    r["w_down"] = f(dn.transpose(0, 1, 2, 4, 3, 5).reshape(L, 2, U_DOWN, P, UW))
    w, at, seg = a["w_in"], 0, {}
    for name, size in (("hq", 512), ("hi", 512), ("hg", 512), ("hf", 1024), ("mq", 512), ("mk", 512), ("mv", 512),
                       ("mo", 512), ("mi", 8), ("mf", 8), ("mz", 512), ("xbc", 768), ("dt", 16), ("bg", 3072)):
        seg[name] = w[..., at:at + size]
        at += size
    fm = lambda m: units(m, P)
    tm = lambda m: f(m.reshape(L, 4, 2, P, MIX).transpose(0, 1, 3, 2, 4)).reshape(L, 4, P, KC * P)

    def rows(parts):
        m = np.zeros((L, D, P), w.dtype)
        for at_, p in parts:
            m[..., at_:at_ + p.shape[-1]] = p
        return fm(m)

    mf, mi, dt = seg["mf"], seg["mi"], seg["dt"]
    gr = [rows([(0, mf[..., 0:4]), (32, mf[..., 4:8]), (64, dt[..., 0:8]), (96, dt[..., 8:16])]),
          rows([(0, mi[..., 0:4]), (32, mi[..., 4:8])])]
    r["w_in"] = f(np.concatenate([fm(seg["hf"]), fm(seg["hq"]), tm(seg["hi"]), tm(seg["hg"]), fm(seg["bg"]),
                                  fm(seg["mq"]), fm(seg["mk"]), *gr, tm(seg["mv"]), tm(seg["mo"]),
                                  fm(seg["xbc"]), tm(seg["mz"])], 1))
    br = units(a["w_branch"], 2 * P)
    r["w_branch"] = f(br.transpose(0, 2, 1, 3, 4).reshape(L, U_BR, P, KC * P))
    r["w_out"] = f(units(a["w_out"], P))
    par = np.zeros((L, P, NPAR), np.float32)

    def put(name, m):
        par[:, :, PAR[name]:PAR[name] + m.shape[1]] = m.transpose(0, 2, 1)

    put("bmod", a["b_mod"].reshape(L, 72, P))
    put("ln", np.stack([a["ln_g"], a["ln_b"]], 2).reshape(L, 48, P))
    put("normg", np.stack([a["hg_norm_g"], a["ml_norm_g"], a["mb_norm_g"]], 1).reshape(L, 12, P))
    put("convw", a["mb_conv_w"].reshape(L, 3, 6, P).transpose(0, 2, 1, 3).reshape(L, 18, P))
    put("convb", a["mb_conv_b"].reshape(L, 6, P))
    row = np.zeros((L, 4, P), np.float32)
    gb, sm = a["ml_gate_b"], a["state_mlstm_m"][0]
    for d in range(2):
        row[:, 0, 32 * d:32 * d + 4] = gb[:, 1, d]
        row[:, 0, 64 + 32 * d:72 + 32 * d] = a["mb_dt_bias"][:, d]
        row[:, 1, 64 + 32 * d:72 + 32 * d] = a["mb_a_log"][:, d]
        row[:, 2, 32 * d:32 * d + 4] = gb[:, 0, d]
        row[:, 3, 32 * d:32 * d + 4] = sm[:, d]
    put("row", row)
    par[:, :, PAR["mbd"]:PAR["mbd"] + 8] = a["mb_d"][:, None, :]
    r["par"] = par
    r["hgrn"] = f(a["state_hgrn"][0].transpose(0, 3, 1, 2, 4))
    cn = np.concatenate([a["state_mlstm_C"][0], a["state_mlstm_n"][0][..., None]], -1)
    r["mlstm"] = f(cn.transpose(0, 3, 1, 2, 4))
    ss = a["state_ssd"][0].reshape(L, 2, 2, 4, SP_, 64)
    r["ssd"] = f(ss.transpose(0, 2, 5, 1, 3, 4).reshape(L, P, 2, 4, SP_))
    return r


OUTS = {"y": (P, KC, T), "hgrn": (L, 2, P, NH, P), "mlstm": (L, 2, NH, P, C1), "m": (L, 2, NH, 1),
        "ssd": (L, 2, P, 4, SP_)}


def returned(o):
    y = o["y"].transpose(2, 1, 0).reshape(T, D)
    hg = o["hgrn"].transpose(0, 1, 3, 2, 4)[None]
    ml = o["mlstm"][None]
    ssd = o["ssd"].reshape(L, 2, 2, 64, 4, SP_).transpose(0, 1, 2, 4, 5, 3).reshape(1, L, 2, SH, SP_, 64)
    return (y[None, :NC_TOK], y[None, NC_TOK:], hg, ml[..., :P], ml[..., P], o["m"].reshape(1, L, 2, NH), ssd)


def kernel(**inputs):
    import concourse.bacc as bacc
    from concourse.bass_utils import run_bass_kernel_spmd

    arrays = {**laid_out(inputs), **constants()}
    nc = bacc.Bacc("TRN2", target_bir_lowering=False, num_devices=1)
    ins = {n: nc.dram_tensor(f"in_{n}", a.shape, mybir.dt.from_np(a.dtype), kind="ExternalInput").ap()
           for n, a in arrays.items()}
    outs = {n: nc.dram_tensor(f"out_{n}", s, F32, kind="ExternalOutput").ap() for n, s in OUTS.items()}
    build(nc, ins, outs)
    r = run_bass_kernel_spmd(nc, [{f"in_{n}": a for n, a in arrays.items()}], core_ids=[0])
    got = returned({n: r.results[0][f"out_{n}"] for n in OUTS})
    return tuple(np.ascontiguousarray(g) for g in got)
```

```python
import math
from contextlib import ExitStack

import numpy as np

import concourse.bass as bass
from concourse import mybir

F32 = mybir.dt.float32
F32R = mybir.dt.float32r
U8 = mybir.dt.uint8
ALU = mybir.AluOpType
ACT = mybir.ActivationFunctionType
AX = mybir.AxisListType

P = 128
D = 1024
L = 2
NC_TOK, NL_TOK = 128, 256
T = NC_TOK + NL_TOK
NT = T // P
KC = D // P
DFF = 2816
NF = DFF // P
MIX = 512
NH = MIX // P
SH, SP_ = 8, 64
ALPHA = (2 * L) ** 0.25
LN_EPS, RMS_EPS = 1e-5, 1e-6
NEG = -1e30
GROUPS = ((0, NC_TOK), (NC_TOK, T))
C1 = P + 1

U_MOD = 9 * KC
U_MOD0 = 5 * KC
KTHIRDS = -(-NF // KC)
U_GU, U_DOWN = 2 * NF, KTHIRDS * KC
U_FFN = U_GU + U_DOWN
U_IN = 72 + U_MOD
HG_UNITS = 20
GATE_SEQ = [it for r in range(6) for it in (
    ("bg", 4 * r), ("mod", 3 * r), ("bg", 4 * r + 1), ("turn", 3 * r), ("mod", 3 * r + 1),
    ("bg", 4 * r + 2), ("turn", 3 * r + 1), ("mod", 3 * r + 2), ("bg", 4 * r + 3), ("turn", 3 * r + 2))]
GATE_UNITS = {"bg": 1, "mod": 4, "turn": 0}
HG_ITEMS, ROW_ITEMS = 30, 7
for _n in (HG_ITEMS, HG_ITEMS + ROW_ITEMS):
    assert GATE_SEQ[_n - 1][0] == "turn"
U_BR, U_OUT = 12, KC
U_MIX = U_IN + U_BR + U_OUT
U_SPLIT = 2 * U_FFN + U_MIX
NRAW = NSPLIT = 4
AHEAD = 3
UW = KC * P
DOWN_LAST = (NF - 2 * KC) * P
assert U_MOD0 % NRAW == 0 and U_SPLIT % NRAW == 0 and U_FFN % NRAW == 0 and U_IN % NRAW == 0
MOD_ORDER = (5, 6, 7, 8, 0, 1, 2, 3, 4)
LOW0 = UW * 5 // 16

PAR, _n = {}, 0
for _name, _w in (("bmod", 72), ("ln", 48), ("normg", 12), ("convw", 18), ("convb", 6), ("row", 4),
                  ("mbd", 8)):
    PAR[_name] = _n
    _n += _w
NPAR = _n

HG_STEPS = ((0, 0), (1, 0), (0, 1), (1, 2), (0, 2), (1, 1))
LEVELS = (64, 32, 16, 8, 4, 2, 1)


def hg_plan():
    ops = []
    for s, (d, t) in enumerate(HG_STEPS):
        for h in LEVELS:
            ops.append((s, d, t, "level", h))
        ops.append((s, d, t, "diag", 0))
        if t:
            ops.append((s, d, t, "inter", 0))
        if s < 4:
            ops.append((s, d, t, "state", 0))
    return ops


def build(nc, ins, outs):
    ctx = ExitStack()
    with ctx:
        end = {"at": (nc.sbuf_base + 31) // 32 * 32}

        def at(name, shape, offset, dt=F32):
            size = int(np.prod(shape[1:])) * (1 if dt == U8 else 4)
            return nc.alloc_sbuf_tensor_at(name, shape, dt, offset=offset), offset + (size + 31) // 32 * 32

        def sb(name, shape, dt=F32):
            t, end["at"] = at(name, shape, end["at"], dt)
            return t

        raw = [sb(f"raw{i}", [P, UW]) for i in range(NRAW)]
        whi = [sb(f"whi{i}", [P, UW], F32R) for i in range(NSPLIT)]
        wlo = [sb(f"wlo{i}", [P, UW], F32R) for i in range(NSPLIT)]
        x = sb("x", [P, KC, T])
        h_hi = sb("h_hi", [P, KC, T], F32R)
        h_lo = sb("h_lo", [P, KC, T], F32R)
        ident = sb("ident", [P, P])
        mean_w = sb("mean_w", [P, P])
        neg = sb("neg", [P, 2, P])
        hmask = sb("hmask", [P, 2, len(LEVELS) + 1, P], U8)
        sgn = sb("sgn", [P, 1])
        keep = sb("keep", [P, NT * C1])
        par = sb("par", [P, NPAR])
        mod = sb("mod", [P, 72, 2])
        cond = sb("cond", [P, KC, 2])
        cond_t = sb("cond_t", [P, KC, 2])
        cond_s = sb("cond_s", [P, KC, 4], F32R)
        pick = sb("pick", [P, 2])
        bmod0 = sb("bmod0", [P, U_MOD0])
        lb_in = sb("lb_in", [P, 2, 8])
        lb_w = sb("lb_w", [P, 4, 8])
        lbs = sb("lbs", [P, 2, 8])
        lb = sb("lb", [P, 8])
        om = sb("om", [P, 8])
        eps = sb("eps", [P, 2])
        mout = sb("mout", [P, 1])
        modr = sb("modr", [P, U_MOD, 2])
        arena = end["at"]

        def region(start, *parts):
            made = []
            for part in parts:
                t, start = at(part[0], part[1], start, part[2] if len(part) > 2 else F32)
                made.append(t)
            return made, start

        (act_hi, act_lo, tb0, tb1, sb0, sb1, vb0, vb1, sq0, sq1, std, rstd, ht0, ht1), e0 = region(
            arena, ("act_hi", [P, NF, T], F32R), ("act_lo", [P, NF, T], F32R),
            *[(n, [P, T]) for n in ("tb0", "tb1", "sb0", "sb1", "vb0", "vb1", "sq0", "sq1", "std", "rstd",
                                    "ht0", "ht1")])
        tb, sbf, vb, sq, ht = (tb0, tb1), (sb0, sb1), (vb0, vb1), (sq0, sq1), (ht0, ht1)
        (pos, hmask_in), _ = region(arena, ("pos", [P, KC, NL_TOK]), ("hmask_in", [P, 2, len(LEVELS) + 1, P]))
        (gates, y_hg, nsq, nyn, nsm), mix0 = region(
            arena, ("gates", [P, 24, T]), ("y_hg", [P, NH, T]), ("nsq", [P, NH, P]), ("nyn", [P, NH, P]),
            ("nsm", [P, 3, NH]))
        modrow, _ = at("modrow", [P, MIX], mix0 - 2 * 2048 - 64)
        (q, v, hgate, kk, cc, ea0, ea1, qe0, qe1, ke0, ke1, att0, att1, hs, kT, so0, so1, etot), e1 = region(
            mix0, ("q", [P, NH, T]), ("v", [P, NT, MIX]), ("hgate", [P, NT, MIX]), ("kk", [P, 2, NH, T]),
            ("cc", [P, 2, NH, NT, C1]), *[(n, [P, NH, P]) for n in ("ea0", "ea1", "qe0", "qe1", "ke0", "ke1",
                                                                      "att0", "att1")],
            ("hs", [P, 2, NH, P]), ("kT", [P, NH, P]), ("so0", [P, NH, P]), ("so1", [P, NH, P]), ("etot", [P, 2, NH]))
        ea2, _ = at("ea2", [P, NH, P], mix0 - 2048 - 64)
        ea, qe, ke, att, so = (ea0, ea1, ea2), (qe0, qe1), (ke0, ke1), (att0, att1), (so0, so1)
        (y_ml, t_1, t_2, t_3, t_4, x_5, wb), rows0 = region(
            mix0, ("y_ml", [P, NH, T]), *[(f"t_{i}", [P, NT, P]) for i in (1, 2, 3, 4)], ("x_5", [P, T]),
            ("wb", [P, P]))
        (ga, gb, r_w, r_e, r_u, r_n, cr, x_1, x_2, x_3, x_4, r_N, minit, coef, lastw, dlast), e2 = region(
            rows0, *[(n, [P, T]) for n in ("ga", "gb", "r_w", "r_e", "r_u", "r_n")], ("cr", [P, NT, C1]),
            *[(n, [P, T]) for n in ("x_1", "x_2", "x_3", "x_4", "r_N")], ("minit", [P, NT]), ("coef", [P, 1]),
            ("lastw", [P, 1]), ("dlast", [P, P]))
        (pt0, pt1, pr0, pr1, st0, st1, kw0, kw1, tmpa, tmpb, den, co0, co1, cs), e3 = region(
            rows0, *[(n, [P, T]) for n in ("pt0", "pt1", "pr0", "pr1", "st0", "st1")], ("kw0", [P, 2, P]),
            ("kw1", [P, 2, P]), ("tmpa", [P, NT, C1]), ("tmpb", [P, NT, C1]), ("den", [P, 2, NT]),
            ("co0", [P, C1]), ("co1", [P, C1]), ("cs", [P, 2, NH, C1]))
        e2 = max(e2, e3)
        pt, pr, st, kw, co = (pt0, pt1), (pr0, pr1), (st0, st1), (kw0, kw1), (co0, co1)
        (mq, mk, mkt, va, mo, hout), e4 = region(
            e2, ("mq", [P, NH, T]), ("mk", [P, NH, T]), ("mkt", [P, NT, MIX]), ("va", [P, NT, NH, C1]),
            ("mo", [P, NT, MIX]), ("hout", [P, NT, MIX]))
        es = e3 - 2 * NH * C1 * 4
        (xpad, xs, cth, cbuf, mz, yx, ht_s, xw, ho0, ho1), e5 = region(
            es, ("xpad", [P, 6, 388]), ("xs", [P, 6, T]), ("cth", [P, 388]), ("cbuf", [P, 388]),
            ("mz", [P, NT, MIX]), ("yx", [P, 2, MIX]), ("ht_s", [P, 2, 4, SP_]), ("xw", [P, MIX]),
            ("ho0", [P, 4, SP_]), ("ho1", [P, 4, SP_]))
        (xt, bt), _ = region(es, ("xt", [P, NT, MIX]), ("bt", [P, NT, P]))
        zth, _ = at("zth", [P, MIX], es + 9312 + 9216)
        y_mb, _ = at("y_mb", [P, NH, T], es + 9312 + 9216 + 2 * 1568 + 6144)
        (y_hi, y_lo, zt0, zt1), e7 = region(rows0, ("y_hi", [P, 3, NH, T], F32R), ("y_lo", [P, 3, NH, T], F32R),
                                  ("zt0", [P, 2, T]), ("zt1", [P, 2, T]))
        ps = [ctx.enter_context(nc.psum_tensor(f"ps{i}", [P, 512], F32)) for i in range(8)]

        def sem(name):
            return ctx.enter_context(nc.semaphore(name))

        raw_loaded = [sem(f"raw_loaded{i}") for i in range(NRAW)]
        w_hi = sem("w_hi")
        w_split = sem("w_split")
        w_used = sem("w_used")
        layer_end = sem("layer_end")
        cond_loaded = sem("cond_loaded")
        start_loads = sem("start_loads")
        par_loaded = sem("par_loaded")
        stored = sem("stored")
        ready = sem("ready")
        rows0_out = sem("rows0_out")
        low0 = sem("low0")
        turned0 = sem("turned0")

        OWN = {"pe": {}, "act": {}, "dve": {}}

        def signal(owner, name):
            OWN[owner][name] = sem(name)
            return OWN[owner][name]

        met = signal("dve", "met")
        dve_step = signal("dve", "dve_step")
        act_step = signal("act", "act_step")
        st_loaded = signal("act", "st_loaded")
        gate_t = signal("act", "gate_t")
        gated = signal("dve", "gated")
        down_ev = signal("act", "down_ev")
        resid = signal("dve", "resid")
        ln_mean = signal("pe", "ln_mean")
        ln_cent = signal("dve", "ln_cent")
        ln_sq = signal("act", "ln_sq")
        ln_acc = signal("pe", "ln_acc")
        ln_std = signal("act", "ln_std")
        ln_out = signal("dve", "ln_out")
        md_t = signal("dve", "md_t")
        md_hi = signal("act", "md_hi")
        md_lo = signal("dve", "md_lo")
        evac = signal("act", "evac")
        post = signal("dve", "post")
        hg_ln = signal("act", "hg_ln")
        hg_a = signal("dve", "hg_a")
        hg_e = signal("act", "hg_e")
        hg_b = signal("dve", "hg_b")
        hg_m = signal("pe", "hg_m")
        hg_c = signal("dve", "hg_c")
        hg_m2 = signal("pe", "hg_m2")
        hg_c2 = signal("dve", "hg_c2")
        hg_o = signal("pe", "hg_o")
        nm_sq = signal("act", "nm_sq")
        nm_ms = signal("dve", "nm_ms")
        nm_sd = signal("act", "nm_sd")
        nm_y = signal("dve", "nm_y")
        nm_tr = signal("pe", "nm_tr")
        nm_out = signal("act", "nm_out")
        row_d = signal("dve", "row_d")
        row_a = signal("act", "row_a")
        row_p = signal("pe", "row_p")
        tr_pe = signal("pe", "tr_pe")
        tr_act = signal("act", "tr_act")
        pr_bc = signal("pe", "pr_bc")
        pr_x = signal("dve", "pr_x")
        pr_e = signal("act", "pr_e")
        pr_qk = signal("pe", "pr_qk")
        pr_s = signal("dve", "pr_s")
        pr_n = signal("pe", "pr_n")
        ml_kw = signal("dve", "ml_kw")
        ml_it = signal("pe", "ml_it")
        ml_cu = signal("dve", "ml_cu")
        ml_i2 = signal("pe", "ml_i2")
        ml_iw = signal("act", "ml_iw")
        ml_h = signal("dve", "ml_h")
        sd_w = signal("dve", "sd_w")
        sd_p = signal("pe", "sd_p")
        sd_o = signal("dve", "sd_o")
        br_z = signal("dve", "br_z")
        br_hi = signal("dve", "br_hi")

        ln_x = signal("act", "ln_x")
        turned = signal("pe", "turned")
        hg_lnd = signal("dve", "hg_lnd")
        br_a = signal("act", "br_a")
        br_y = signal("dve", "br_y")
        br_z2 = signal("dve", "br_z2")
        start_v = sem("start_v")
        co_stored = [sem(f"co_stored{i}") for i in range(2)]
        MEET = {k: n + 1 for n, k in enumerate((
            ("ffn", 0), ("down", 0), ("ln", 0), ("hg_in", 0), ("hg", 0), ("ml_in", 0), ("rows", 0), ("ml", 0),
            ("mln", 0), ("ssd_in", 0), ("ssd_c", 0), ("ssd_x", 0), ("ssd", 0), ("br_in", 0), ("out", 0),
            ("ffn", 1), ("down", 1), ("end", 0)))}
        STORES = 6
        ROW_W, ROW_T, ROW_TA = 3, 4, 5
        POST_MZ, POST_SSD = 15, 18

        def width(k):
            for first in (UF1 + U_GU, UF2 + U_GU):
                if first <= k < first + U_DOWN and (k - first) % KTHIRDS == KTHIRDS - 1:
                    return DOWN_LAST
            return UW

        class Steps:

            def __init__(self, eng, s):
                self.eng, self.sem, self.n, self.off = eng, s, 0, 0

            def __call__(self, ins):
                self.n += 1
                ins.then_inc(self.sem, 1)
                return ins

            def done(self):
                self.eng.wait_ge(self.sem, self.off + self.n)

        UF1, UM, UF2 = 0, U_FFN, U_FFN + U_MIX
        plan = []
        for b in range(8):
            plan.append(("fm", b, (b % 2,), ("hf", b)))
        for b in range(4):
            plan.append(("fm", 8 + b, (b % 2,), ("hq", b)))
        plan.append(("tm", 12, (2, 3, 4), ("hi", 0)))
        plan.append(("tm", 16, (5, 6, 7), ("hg", 0)))
        def gate_items(u, a, b, banks):
            for n, what in enumerate(GATE_SEQ[a:b]):
                plan.append((what[0] if what[0] != "bg" else "fm", u, (banks(n),), what))
                u += GATE_UNITS[what[0]]
            return u

        u1 = gate_items(HG_UNITS, 0, HG_ITEMS, lambda n: n % 2)
        for b in range(4):
            plan.append(("fm", u1 + b, (b % 2,), ("mq", b)))
        for b in range(4):
            plan.append(("fm", u1 + 4 + b, (b % 2,), ("mk", b)))
        for b in range(2):
            plan.append(("fm", u1 + 8 + b, (b % 2,), ("gr", b)))
        plan.append(("tm", u1 + 10, (2, 3, 4), ("mv", 0)))
        plan.append(("tm", u1 + 14, (5, 6, 7), ("mo", 0)))
        u2 = gate_items(u1 + 18, HG_ITEMS, HG_ITEMS + ROW_ITEMS, lambda n: 6 + n % 2)
        for b in range(6):
            plan.append(("fm", u2 + b, (b % 2,), ("xbc", b)))
        plan.append(("tm", u2 + 6, (2, 3, 4), ("mz", 0)))
        u3 = gate_items(u2 + 10, HG_ITEMS + ROW_ITEMS, None, lambda n: n % 2 if n < 12 else (3, 7)[n % 2])
        assert u3 == U_IN
        first_evac, bank_last, n = {}, {}, 0
        bank_before = {}
        for item in plan:
            first_evac[item[3]] = n
            for bank in item[2]:
                bank_before[(item[3], bank)] = bank_last.get(bank, 0)
                n += 1
                bank_last[bank] = n
        N_EVAC = n

        def items(*names):
            return [it for it in plan if it[3][0] in names]

        ops = hg_plan()
        cnt = {}
        for kind in "abcem":
            n = 0
            for o, (s, d, t, what, hh) in enumerate(ops):
                if kind == "m" or (kind == "c" and what != "inter") or (kind in "abe" and what != "diag"):
                    n += 1
                cnt[kind, o] = n
        n2 = 0
        for o, op in enumerate(ops):
            if op[3] == "state":
                n2 += 1
            cnt["s", o] = n2


        def hg_items(o):
            a, b = (-(-HG_ITEMS * n // len(ops)) for n in (o, o + 1))
            return items("bg", "mod", "turn")[a:b]

        def row_items():
            return items("bg", "mod", "turn")[HG_ITEMS:HG_ITEMS + ROW_ITEMS]

        def sd_items(slot):
            pairs = slot - 12
            first = HG_ITEMS + ROW_ITEMS
            left = len(GATE_SEQ) - first - 12
            a, b = (slot, slot + 1) if pairs < 0 else (12 + -(-left * n // 16) for n in (pairs, pairs + 1))
            return items("bg", "mod", "turn")[first + a:first + b]

        def glob(l, k):
            return k + (l * U_SPLIT + U_MOD0)

        def unit_split(pe, l, k):
            pe.wait_ge(w_split, glob(l, k + (1 + NRAW)))

        def unit_done(eng, l, k):
            eng.wait_ge(w_used, glob(l, k + (1 + NSPLIT)))

        block = ctx.enter_context(nc.Block())

        def meet(eng, n):
            eng.drain().then_inc(met, 1)
            eng.wait_ge(met, 3 * n)

        def layer_over(eng, l, owner):
            eng.drain().then_inc(layer_end, 1)
            eng.wait_ge(layer_end, l * 9 + 3)
            eng.sem_inc(layer_end, 1)
            for s in OWN[owner].values():
                eng.sem_clear(s)
            eng.drain().then_inc(layer_end, 1)
            eng.wait_ge(layer_end, l * 9 + 9)

        @block.sync
        def _(sp):
            for dst, src in ((cond, ins["cond"]), (lb_in, ins["hg_lb"]), (bmod0, ins["bmod0"]),
                             (pick, ins["pick"])):
                sp.dma_start(dst[tuple(slice(None) for _ in dst.shape)], src).then_inc(cond_loaded, 16)
            with sp.Fori(0, U_MOD0 // NRAW) as i:
                for m in range(NRAW):
                    sp.wait_ge(w_split, i * NRAW + (m + 1))
                    sp.dma_start(raw[m][:, :], ins["w_mod"][i * NRAW + m]).then_inc(raw_loaded[m], 16)
            with sp.Fori(0, L) as l:

                def stream(first, count, per, src):
                    with sp.Fori(0, count // per) as i:
                        for m in range(per):
                            w = width(first + m)
                            sp.wait_ge(w_split, glob(l, i * per + (first + m + 1)))
                            sp.dma_start(raw[m % NRAW][:, 0:w],
                                         src(i * per + m)[:, 0:w]).then_inc(raw_loaded[m % NRAW], 16)

                stream(UF1, U_GU, NRAW, lambda k: ins["w_gu"][l, 0, k])
                stream(UF1 + U_GU, U_DOWN, 12, lambda k: ins["w_down"][l, 0, k])
                stream(UM, U_IN, NRAW, lambda k: ins["w_in"][l, k])
                stream(UM + U_IN, U_BR, NRAW, lambda k: ins["w_branch"][l, k])
                stream(UM + U_IN + U_BR, U_OUT, NRAW, lambda k: ins["w_out"][l, k])
                stream(UF2, U_GU, NRAW, lambda k: ins["w_gu"][l, 1, k])
                stream(UF2 + U_GU, U_DOWN, 12, lambda k: ins["w_down"][l, 1, k])
            sp.wait_ge(layer_end, 9 * L)
            sp.dma_start(outs["y"], x[:, :, :]).then_inc(stored, 16)
            sp.wait_ge(stored, 16 * (STORES * L + 1))

        @block.gpsimd
        def _(pool):
            for _ in range(NRAW):
                pool.sem_inc(w_split, 1)

            def low(m, w):
                s = m % NRAW
                nc.gpsimd.tensor_tensor(wlo[s][:, 0:w], raw[s][:, 0:w], whi[s][:, 0:w].bitcast(F32),
                                        ALU.subtract).then_inc(w_split, 1)

            with pool.Fori(0, U_MOD0 // NRAW) as i:
                for m in range(NRAW):
                    pool.wait_ge(low0, i * NRAW + (m + 1))
                    low(m, LOW0)
            with pool.Fori(0, L) as l:
                for first, count, per in ((UF1, U_GU, NRAW), (UF1 + U_GU, U_DOWN, 12), (UM, U_MIX, NRAW),
                                          (UF2, U_GU, NRAW), (UF2 + U_GU, U_DOWN, 12)):
                    with pool.Fori(0, count // per) as i:
                        for m in range(per):
                            pool.wait_ge(w_hi, glob(l, i * per + (first + m + 1)))
                            low(m, width(first + m))

        @block.tensor
        def _(pe):
            mm = nc.tensor.matmul
            for _ in range(NSPLIT):
                pe.sem_inc(w_used, 1)
            pe.sem_inc(turned0, 1)
            pe.wait_ge(cond_loaded, 16 * 4)
            pe.wait_ge(start_v, 2)

            def block_product(out, m, xh, xl, chunks, start, stop, made=None):
                s = m % NSPLIT
                chunks = list(chunks)
                for n, (wc, xc) in enumerate(chunks):
                    if made is not None:
                        pe.wait_ge(md_lo, made + xc + 1)
                    hi_, lo_ = (w[s][:, wc * P:(wc + 1) * P] for w in (whi, wlo))
                    mm(out, hi_, xh[:, xc, :], start=start and n == 0, stop=False)
                    mm(out, hi_, xl[:, xc, :], start=False, stop=False)
                    last = mm(out, lo_, xh[:, xc, :], start=False, stop=stop and n == len(chunks) - 1)
                return last

            def mod_product(bank, u, m):
                s = u % NSPLIT
                for c in range(2):
                    for w in (whi, wlo):
                        last = mm(bank[0:4, :], cond_s[:, 2 * m + c, :], w[s][:, c * MIX:(c + 1) * MIX],
                                  start=(m == 0 and c == 0 and w is whi), stop=(m == 3 and c == 1 and w is wlo))
                return last

            def turn(out):
                for b in range(4):
                    last = mm(out[:, 2 * b:2 * b + 2], modrow[0:4, b * P:(b + 1) * P], pick[0:4, :], start=True,
                              stop=True)
                return last

            def layer_norm(j):
                for n in range(KC):
                    last = mm(ps[4][:, 0:T], mean_w[:, :], x[:, n, :], start=(n == 0), stop=(n == KC - 1))
                last.then_inc(ln_mean, 1)
                for n in range(KC):
                    pe.wait_ge(ln_sq, KC * j + n + 1)
                    mm(ps[5][:, 0:T], mean_w[:, :], sq[n % 2][:, :], start=(n == 0),
                       stop=(n == KC - 1)).then_inc(ln_acc, 1)

            def ffn(l, j, u0):
                with pe.Fori(0, U_GU // 4) as i:
                    for m in range(4):
                        unit_split(pe, l, i * 4 + (u0 + m))
                        if m % 2 == 0:
                            pe.wait_ge(gated, i * 2 + (NF * j + m // 2 + 1))
                        block_product(ps[m][:, 0:T], m, h_hi, h_lo, [(c, c) for c in range(KC)], True, True,
                                      made=2 * KC * j if m == 0 else None).then_inc(w_used, 1)
                meet(pe, MEET["ffn", j])
                with pe.Fori(0, U_DOWN // 12) as i:
                    for m in range(12):
                        b, third = m // KTHIRDS, m % KTHIRDS
                        unit_split(pe, l, i * 12 + (u0 + U_GU + m))
                        if third == 0:
                            pe.wait_ge(resid, i * 4 + ((0, KC * 2)[j] + b + 1))
                        block_product(ps[b % 2][:, 0:T], m, act_hi, act_lo,
                                      [(c, third * KC + c) for c in range(width(u0 + U_GU + m) // P)],
                                      third == 0, third == KTHIRDS - 1).then_inc(w_used, 1)
                meet(pe, MEET["down", j])

            def project(l, item):
                kind, u, banks, what = item
                for bank in banks:
                    if bank_before[what, bank]:
                        pe.wait_ge(evac, bank_before[what, bank])
                if kind == "mod":
                    for m in range(4):
                        unit_split(pe, l, UM + u + m)
                        mod_product(ps[banks[0]], u + m, m).then_inc(w_used, 1)
                    return
                if kind == "turn":
                    pe.wait_ge(evac, first_evac["mod", what[1]] + 1)
                    turn(ps[banks[0]][:, 0:8]).then_inc(turned, 1)
                    return
                if kind == "fm":
                    unit_split(pe, l, UM + u)
                    block_product(ps[banks[0]][:, 0:T], u, h_hi, h_lo, [(c, c) for c in range(KC)], True, True,
                                  made=KC if u == 0 else None).then_inc(w_used, 1)
                    return
                for m in range(4):
                    unit_split(pe, l, UM + u + m)
                    s = (u + m) % NSPLIT
                    for c2 in range(2):
                        c = 2 * m + c2
                        for t in range(NT):
                            out = ps[banks[t]][:, :]
                            xh, xl = (a[:, c, t * P:(t + 1) * P] for a in (h_hi, h_lo))
                            wh, wl = (w[s][:, c2 * MIX:(c2 + 1) * MIX] for w in (whi, wlo))
                            mm(out, xh, wh, start=(c == 0), stop=False)
                            mm(out, xl, wh, start=False, stop=False)
                            last = mm(out, xh, wl, start=False, stop=(c == KC - 1))
                    last.then_inc(w_used, 1)

            def normed(b):
                for t in range(NT):
                    n = b * NT + t
                    pe.wait_ge(nm_y, n + 1)
                    if t >= 2:
                        pe.wait_ge(nm_out, n - 1)
                    for g in range(NH):
                        last = nc.tensor.transpose(ps[2 + t % 2][:, g * P:(g + 1) * P], nyn[:, g, :], ident[:, :])
                    last.then_inc(nm_tr, 1)
                pe.wait_ge(nm_out, (b + 1) * NT)

            def hgrn(l):
                first = set()

                def o_flag(t):
                    f = t not in first
                    first.add(t)
                    return f

                waiting = []
                for o, (s, d, t, what, hh) in enumerate(ops):
                    S, b = ps[2 + o % 2], o % 2
                    if what != "diag":
                        pe.wait_ge(hg_b, cnt["b", o])
                    if o >= 2:
                        pe.wait_ge(hg_c, cnt["c", o - 2])
                    cols = slice(t * P, (t + 1) * P)
                    for g in range(NH):
                        out = S[:, g * P:(g + 1) * P]
                        if what == "level":
                            last = mm(out, ke[b][:, g, :], qe[b][:, g, :], start=True, stop=True)
                        elif what == "diag":
                            last = mm(out, kk[:, d, g, cols], q[:, g, cols], start=True, stop=True)
                        elif what == "inter":
                            if g == 0:
                                pe.wait_ge(st_loaded, 16)
                                if s >= 4:
                                    pe.wait_ge(hg_c2, s - 1)
                            last = mm(ps[4 + t][:, g * P:(g + 1) * P], qe[b][:, g, :], hs[:, d, g, :],
                                      start=o_flag(t), stop=True, skip_group_check=True)
                        else:
                            last = nc.tensor.transpose(out, ke[b][:, g, :], ident[:, :])
                    last.then_inc(hg_m, 1)
                    for o2, (s2, d2, t2, _, _) in waiting:
                        pe.wait_ge(hg_c, cnt["c", o2])
                        if s2:
                            pe.wait_ge(hg_c2, s2)
                        for g in range(NH):
                            last = mm(ps[7][:, g * P:(g + 1) * P], kT[:, g, :], v[:, t2, g * P:(g + 1) * P],
                                      start=True, stop=True)
                        last.then_inc(hg_m2, 1)
                    waiting = [(o, ops[o])] if what == "state" else []
                    if what == "level" and hh == 64 and s:
                        out_step(s - 1, o_flag)
                    for it in hg_items(o):
                        project(l, it)
                out_step(5, o_flag)

            def out_step(s, o_flag):
                d, t = HG_STEPS[s]
                diag = [o for o, op in enumerate(ops) if op[0] == s and op[3] == "diag"][0]
                pe.wait_ge(hg_c, cnt["c", diag])
                for g in range(NH):
                    last = mm(ps[4 + t][:, g * P:(g + 1) * P], att[d][:, g, :], v[:, t, g * P:(g + 1) * P],
                              start=o_flag(t), stop=True, skip_group_check=True)
                last.then_inc(hg_o, 1)

            def rows(l):
                for it in row_items():
                    project(l, it)
                pe.wait_ge(row_d, ROW_T)
                pe.wait_ge(row_a, ROW_TA)
                for i, xi in enumerate((x_1, x_2, x_3, x_4)):
                    if i >= 2:
                        pe.wait_ge(tr_act, i - 1)
                    for t in range(NT):
                        last = nc.tensor.transpose(ps[i % 2][:, t * P:(t + 1) * P], xi[:, t * P:(t + 1) * P],
                                                   ident[:, :])
                    last.then_inc(tr_pe, 1)
                mm(ps[2][:, 0:P], mean_w[:, :], dlast[:, :], start=True, stop=True).then_inc(row_p, 1)

            def keys_turned():
                for t in range(NT):
                    if t >= 2:
                        pe.wait_ge(tr_act, 4 + t - 1)
                    elif t == 0:
                        pe.wait_ge(tr_act, 4)
                    for g in range(NH):
                        last = nc.tensor.transpose(ps[3 + t % 2][:, g * P:(g + 1) * P],
                                                   mk[:, g, t * P:(t + 1) * P], ident[:, :])
                    last.then_inc(tr_pe, 1)

            def spread(r, rr):
                if r >= 2:
                    pe.wait_ge(pr_x, r - 1)
                mm(ps[r % 2][:, 0:T], ident[:, rr:rr + 1].to_broadcast([P, P]), x_5[:, :], start=True,
                   stop=True).then_inc(pr_bc, 1)

            def mlstm():
                def head(h):
                    if h >= 2:
                        pe.wait_ge(pr_s, 2 * h - 2)
                    for t in range(NT):
                        c = slice(t * P, (t + 1) * P)
                        last = mm(ps[2 + h % 2][:, c], mk[:, h, c], mq[:, h, c], start=True, stop=True)
                    last.then_inc(pr_qk, 1)

                def second(r):
                    h, d = r // 2, r % 2
                    pe.wait_ge(ml_cu, r + 1)
                    t2 = 2 - d
                    mm(ps[6 + r % 2][:, C1:2 * C1], mq[:, h, t2 * P:(t2 + 1) * P], cs[:, d, h, :], start=True,
                       stop=True).then_inc(ml_i2, 1)

                spread(0, 0)
                head(0)
                pe.wait_ge(st_loaded, 32)
                for r in range(8):
                    h, d = r // 2, r % 2
                    if r < 7:
                        spread(r + 1, 32 * (1 - d) + (r + 1) // 2)
                        if d == 1:
                            head(h + 1)
                    if r:
                        second(r - 1)
                    pe.wait_ge(pr_s, r + 1)
                    if r >= 2:
                        pe.wait_ge(ml_h, r - 1)
                    for t in range(NT):
                        last = mm(ps[4 + r % 2][:, t * C1:(t + 1) * C1], st[r % 2][:, t * P:(t + 1) * P],
                                  va[:, t, h, :], start=True, stop=True)
                    last.then_inc(pr_n, 1)
                    pe.wait_ge(ml_kw, r + 1)
                    it, t1 = ps[6 + r % 2], 1 + d
                    mm(it[:, C1:2 * C1], kw[r % 2][:, 0, :], va[:, 0, h, :], start=True, stop=True)
                    mm(it[:, 2 * C1:3 * C1], kw[r % 2][:, 1, :], va[:, t1, h, :], start=True, stop=True)
                    mm(it[:, 0:C1], mq[:, h, t1 * P:(t1 + 1) * P], cs[:, d, h, :], start=True,
                           stop=True).then_inc(ml_it, 1)
                second(7)

            def ssd(l):
                for slot in range(6):
                    for it in sd_items(slot):
                        project(l, it)
                meet(pe, MEET["ssd_c", 0])
                for t in range(NT):
                    c = slice(t * P, (t + 1) * P)
                    if t:
                        pe.wait_ge(tr_act, 7 + 2 * t)
                    for g in range(4):
                        last = nc.tensor.transpose(ps[5][:, g * P:(g + 1) * P], xs[:, g, c], ident[:, :])
                    last.then_inc(tr_pe, 1)
                    last = nc.tensor.transpose(ps[6][:, 0:P], xs[:, 4, c], ident[:, :])
                    last.then_inc(tr_pe, 1)
                meet(pe, MEET["ssd_x", 0])
                n = w = 0
                for d in range(2):
                    for step, t in enumerate((0, 1 + d, 2 - d)):
                        c = slice(t * P, (t + 1) * P)
                        if step:
                            pe.wait_ge(st_loaded, 48)
                            pe.wait_ge(sd_o, n)
                            for g in range(2):
                                gp = slice(64 * g, 64 * g + 64)
                                last = mm(ps[(7, 2)[g]][:, 0:256], xs[gp, 5, c],
                                          ht_s[gp, d, :, :].rearrange("p h e -> p (h e)"), start=True, stop=True)
                            last.then_inc(sd_p, 1)
                            n += 1
                        if step < 2:
                            w += 1
                            pe.wait_ge(sd_w, 6 + w)
                            pe.wait_ge(sd_o, n)
                            mm(ps[3][:, :], bt[:, t, :], xw[:, :], start=True, stop=True).then_inc(sd_p, 1)
                            n += 1
                        for it in sd_items(6 + 3 * d + step):
                            project(l, it)
                pe.wait_ge(sd_o, n)
                pe.wait_ge(evac, first_evac[sd_items(11)[0][3]] + 1)

                def group(g):
                    if g:
                        pe.wait_ge(pr_s, 8 + 8 * g)
                    gp = slice(64 * g, 64 * g + 64)
                    for t in range(NT):
                        c = slice(t * P, (t + 1) * P)
                        last = mm(ps[2][:, c], xs[gp, 4, c], xs[gp, 5, c], start=True, stop=True)
                    last.then_inc(pr_qk, 1)

                spread(8, 64)
                group(0)
                for r in range(16):
                    head, d = r // 2, r % 2
                    if r < 15:
                        spread(9 + r, 64 + 32 * (1 - d) + (r + 1) // 2)
                    if r == 8:
                        group(1)
                    pe.wait_ge(pr_s, 9 + r)
                    for t in range(NT):
                        last = mm(ps[4 + t][:, head * SP_:(head + 1) * SP_], st[r % 2][:, t * P:(t + 1) * P],
                                  xt[:, t, head * SP_:(head + 1) * SP_], start=(r == 0), stop=True,
                                  skip_group_check=True)
                    last.then_inc(pr_n, 1)
                    for it in sd_items(12 + r):
                        project(l, it)

            def branches(l):
                pe.wait_ge(br_y, 3)
                n = 0
                for mblk in range(4):
                    for c in range(3):
                        u = UM + U_IN + 3 * mblk + c
                        unit_split(pe, l, u)
                        b2 = n % 2
                        if n >= 2:
                            pe.wait_ge(br_z, n - 1)
                        for j in range(2):
                            s = u % NSPLIT
                            out = ps[2 * b2 + j][:, 0:T]
                            for k in range(4):
                                wsl = slice(k * 2 * P + j * P, k * 2 * P + (j + 1) * P)
                                mm(out, whi[s][:, wsl], y_hi[:, c, k, :], start=(k == 0), stop=False)
                                mm(out, whi[s][:, wsl], y_lo[:, c, k, :], start=False, stop=False)
                                last = mm(out, wlo[s][:, wsl], y_hi[:, c, k, :], start=False, stop=(k == 3))
                        last.then_inc(w_used, 1)
                        n += 1

            def out_proj(l):
                pe.wait_ge(br_hi, KC)
                with pe.Fori(0, U_OUT // 4) as i:
                    for m in range(4):
                        unit_split(pe, l, i * 4 + (UM + U_IN + U_BR + m))
                        pe.wait_ge(resid, i * 4 + (KC + m + 1))
                        block_product(ps[m % 2][:, 0:T], m, h_hi, h_lo, [(c, c) for c in range(KC)], True,
                                      True).then_inc(w_used, 1)
                meet(pe, MEET["out", 0])

            with pe.Fori(0, U_MOD0 // 4) as i:
                for m in range(4):
                    pe.wait_ge(w_split, i * 4 + (m + 1 + NRAW))
                    mod_product(ps[0], m, m).then_inc(w_used, 1)
                pe.wait_ge(rows0_out, i + 1)
                for b in range(4):
                    last = mm(ps[7][:, bass.ds(i * 8 + 2 * b, 2)], modrow[0:4, b * P:(b + 1) * P], pick[0:4, :],
                              start=True, stop=True)
                last.then_inc(turned0, 1)
            pe.wait_ge(start_loads, 16 * 8)
            with pe.Fori(0, L) as l:
                ffn(l, 0, UF1)
                layer_norm(0)
                pe.drain().then_inc(met, 1)
                for it in items("hf", "hq", "hi", "hg"):
                    project(l, it)
                meet(pe, MEET["hg_in", 0])
                hgrn(l)
                meet(pe, MEET["hg", 0])
                its = items("mq", "mk", "gr", "mv", "mo")
                for it in its[:2]:
                    project(l, it)
                normed(0)
                for it in its[2:]:
                    project(l, it)
                meet(pe, MEET["ml_in", 0])
                rows(l)
                keys_turned()
                meet(pe, MEET["rows", 0])
                mlstm()
                meet(pe, MEET["ml", 0])
                its = items("xbc", "mz")
                for it in its[:2]:
                    project(l, it)
                normed(1)
                meet(pe, MEET["mln", 0])
                for it in its[2:]:
                    project(l, it)
                meet(pe, MEET["ssd_in", 0])
                ssd(l)
                meet(pe, MEET["ssd", 0])
                normed(2)
                meet(pe, MEET["br_in", 0])
                branches(l)
                out_proj(l)
                layer_norm(1)
                ffn(l, 1, UF2)
                layer_norm(2)
                meet(pe, MEET["end", 0])
                layer_over(pe, l, "pe")

        @block.scalar
        def _(act):
            af = nc.scalar.activation
            step = Steps(act, act_step)

            def round_unit(g4, m, w=UW):
                act.wait_ge(raw_loaded[m], (g4 + 1) * 16)
                act.wait_ge(w_used, g4 * 4 + (m + 1))
                act.copy(whi[m][:, 0:w], raw[m][:, 0:w]).then_inc(w_hi, 1)

            def ahead(l, u, off=0):
                k = u + AHEAD
                if k < U_SPLIT:
                    round_unit(off + (l * (U_SPLIT // 4) + (U_MOD0 // 4 + k // 4)), k % 4, width(k))

            for dst, src in ((x, ins["x"]), (pos, ins["pos"]), (hmask_in, ins["hmask"]), (ident, ins["ident"]),
                             (mean_w, ins["mean_w"]), (neg, ins["neg"]), (keep, ins["keep"]), (sgn, ins["sgn"])):
                act.dma_start(dst[tuple(slice(None) for _ in dst.shape)], src).then_inc(start_loads, 16)
            act.wait_ge(cond_loaded, 16 * 4)
            af(cond_t[:, :, :], cond[:, :, :], ACT.Tanh, scale=0.5).then_inc(ready, 1)
            act.wait_ge(ready, 4)
            af(lb_w[:, 0:2, :], lb_w[:, 0:2, :], ACT.Exp).then_inc(ready, 1)
            for m in range(AHEAD):
                round_unit(0, m)

            def rows_out(i):
                act.wait_ge(w_used, i * 4 + (4 + NSPLIT))
                act.wait_ge(turned0, i + 1)
                act.copy(modrow[0:4, :], ps[0][0:4, :]).then_inc(rows0_out, 1)

            with act.Fori(0, U_MOD0 // 4 - 1) as i:
                for m in range(4):
                    k = m + AHEAD
                    round_unit(i + k // 4, k % 4)
                rows_out(i)
            round_unit(U_MOD0 // 4 - 1, AHEAD)
            rows_out(U_MOD0 // 4 - 1)

            def high(j, n):
                act.wait_ge(md_t, KC * j + n + 1)
                act.copy(h_hi[:, n, :], ht[n % 2][:, :]).then_inc(md_hi, 1)

            def layer_norm(j):
                for n in range(KC):
                    k = KC * j + n
                    act.wait_ge(ln_cent, k + 1)
                    if n >= 2:
                        act.wait_ge(ln_acc, k - 1)
                    af(sq[n % 2][:, :], x[:, n, :], ACT.Square).then_inc(ln_sq, 1)
                act.wait_ge(ln_acc, KC * (j + 1))
                af(std[:, :], ps[5][:, 0:T], ACT.Sqrt, bias=eps[:, 0:1]).then_inc(ln_std, 1)
                lnp = PAR["ln"] + 16 * j
                for n in range(KC):
                    act.wait_ge(ln_out, KC * j + n + 1)
                    af(x[:, n, :], x[:, n, :], ACT.Identity, bias=par[:, lnp + 8 + n:lnp + 9 + n],
                       scale=par[:, lnp + n:lnp + n + 1]).then_inc(ln_x, 1)
                    if j < 2 and n:
                        high(j + 1, n - 1)
                if j < 2:
                    high(j + 1, KC - 1)

            def ffn(l, j, u0):
                def gu(i, base):
                    for jj in range(2):
                        ahead(l, base + 2 * jj, i)
                        ahead(l, base + 2 * jj + 1, i)
                        unit_done(act, l, i * 4 + (base + 2 * jj))
                        act.wait_ge(gated, i * 2 + ((base - u0) // 2 + NF * j + jj + 1))
                        af(tb[jj][:, :], ps[2 * jj][:, 0:T], ACT.Tanh, scale=0.5).then_inc(gate_t, 1)

                if j == 0:
                    for k in range(AHEAD):
                        ahead(l, k - AHEAD)
                with act.Fori(0, U_GU // 4 - 1) as i:
                    gu(i, u0)
                gu(0, u0 + U_GU - 4)
                meet(act, MEET["ffn", j])
                for b in range(KC):
                    first = u0 + U_GU + KTHIRDS * b
                    for k in range(KTHIRDS):
                        ahead(l, first + k)
                    evac_gated(l, first + KTHIRDS - 1, ps[b % 2], (2, 8)[j] * KC + b, 2 * KC * j + b, b % 2)
                meet(act, MEET["down", j])

            def evac_gated(l, u, bank, col, count, jj):
                unit_done(act, l, u)
                act.wait_ge(resid, count + 1)
                for gi, (a, b) in enumerate(GROUPS):
                    last = af(vb[jj][:, a:b], bank[:, a:b], ACT.Copy, scale=mod[:, col, gi:gi + 1])
                last.then_inc(down_ev, 1)

            def project_out(l, item, body, rounded=False):
                kind, u, banks, what = item
                if kind == "turn":
                    act.wait_ge(turned, what[1] + 1)
                else:
                    units = 1 if kind == "fm" else 4
                    for m in range(0 if rounded else units):
                        ahead(l, UM + u + m)
                    unit_done(act, l, UM + u + units - 1)
                    if kind == "mod" and what[1]:
                        act.wait_ge(turned, what[1])
                for n in range(len(banks)):
                    body(n, ps[banks[n]]).then_inc(evac, 1)

            def tmp_free(buf_user):
                if buf_user > 0:
                    act.wait_ge(post, buf_user)

            def normed(b, src, groups, width):
                lnp = PAR["normg"] + 4 * b

                def turned_out(t):
                    act.wait_ge(nm_tr, b * NT + t + 1)
                    dst = (y_hg, y_ml, y_mb)[b]
                    for g in range(NH):
                        last = af(dst[:, g, t * P:(t + 1) * P], ps[2 + t % 2][:, g * P:(g + 1) * P], ACT.Copy,
                                  scale=par[:, lnp + g:lnp + g + 1])
                    last.then_inc(nm_out, 1)

                for t in range(NT):
                    n = b * NT + t
                    if t:
                        act.wait_ge(nm_ms, n)
                    af(nsq[:, :, :].rearrange("p a b -> p (a b)"), src(t), ACT.Square).then_inc(nm_sq, 1)
                    act.wait_ge(nm_ms, n + 1)
                    af(nsm[:, 1, 0:groups], nsm[:, 0, 0:groups], ACT.Sqrt, scale=1.0 / width,
                       bias=eps[:, 1:2]).then_inc(nm_sd, 1)
                    if t:
                        turned_out(t - 1)
                turned_out(NT - 1)

            def gate_out(l, item):
                what, b = item[3]
                if what == "bg":
                    project_out(l, item, lambda n, bank: af(gates[:, b, :], bank[:, 0:T], ACT.Tanh, scale=0.5))
                elif what == "mod":
                    project_out(l, item, lambda n, bank: act.copy(modrow[0:4, :], bank[0:4, :]))
                else:
                    project_out(l, item, lambda n, bank: act.copy(
                        modr[:, 4 * b:4 * b + 4, :].rearrange("p a b -> p (a b)"), bank[:, 0:8]))

            def hgrn(l):
                def decays(o):
                    s, d, t, what, hh = ops[o]
                    if what == "diag":
                        return
                    act.wait_ge(hg_a, cnt["a", o])
                    if what == "state" and t:
                        af(etot[:, d, :], cc[:, d, :, t, P:C1].rearrange("p a b -> p (a b)"), ACT.Exp)
                    af(ea[o % 3][:, :, :], ea[o % 3][:, :, :], ACT.Exp).then_inc(hg_e, 1)

                decays(0)
                decays(1)
                for o, (s, d, t, what, hh) in enumerate(ops):
                    if o + 2 < len(ops):
                        decays(o + 2)
                    for it in hg_items(o):
                        gate_out(l, it)
                    if what == "level" and hh == 32 and s in (1, 2):
                        act.wait_ge(hg_c2, s)
                        act.dma_start(outs["hgrn"][l, s - 1], so[s - 1][:, :, :]).then_inc(stored, 16)

            def rows(l):
                act.wait_ge(row_d, 1)
                af(r_e[:, :], r_w[:, :], ACT.Abs).then_inc(row_a, 1)
                act.wait_ge(row_a, 1)
                af(r_e[:, :], r_e[:, :], ACT.Exp, scale=-1.0).then_inc(row_a, 1)
                af(coef[:, :], par[:, PAR["row"] + 1:PAR["row"] + 2], ACT.Exp).then_inc(row_a, 1)
                act.wait_ge(row_d, 2)
                af(r_u[:, :], r_u[:, :], ACT.Ln).then_inc(row_a, 1)
                for it in row_items():
                    gate_out(l, it)
                act.wait_ge(row_d, ROW_W)
                for t in range(NT):
                    last = af(x_2[0:64, t * P:(t + 1) * P], r_N[0:64, t * P:(t + 1) * P], ACT.Exp, scale=-1.0,
                              bias=minit[0:64, t:t + 1])
                af(x_3[:, :], x_3[:, :], ACT.Exp)
                af(x_4[:, :], x_4[:, :], ACT.Exp).then_inc(row_a, 1)
                for i, ti in enumerate((t_1, t_2, t_3, t_4)):
                    act.wait_ge(tr_pe, i + 1)
                    act.copy(ti[:, :, :].rearrange("p a b -> p (a b)"), ps[i % 2][:, 0:T]).then_inc(tr_act, 1)
                act.wait_ge(row_p, 1)
                act.mul(wb[:, :], ps[2][:, 0:P], float(D)).then_inc(row_a, 1)
                for t in range(NT):
                    act.wait_ge(tr_pe, 4 + t + 1)
                    act.copy(mkt[:, t, :], ps[3 + t % 2][:, :]).then_inc(tr_act, 1)

            def pair(r, rr):
                act.wait_ge(pr_x, r + 1)
                if r >= 2:
                    act.wait_ge(pr_s, r - 1)
                    if r <= 9:
                        act.wait_ge(ml_kw, min(r - 1, 8))
                for t in range(NT):
                    c = slice(t * P, (t + 1) * P)
                    last = af(pr[r % 2][:, c], pt[r % 2][:, c], ACT.Exp, bias=t_1[:, t, rr:rr + 1])
                last.then_inc(pr_e, 1)

            def mlstm(l):
                def weigh(r):
                    d, h = r % 2, r // 2
                    it, rr = ps[6 + r % 2], 32 * d + h
                    act.wait_ge(ml_i2, r + 1)
                    if r:
                        act.wait_ge(ml_h, r)
                    af(tmpa[:, 1 + d, :], it[:, 0:C1], ACT.Copy, scale=t_2[:, 1 + d, rr:rr + 1])
                    af(tmpa[:, 2 - d, :], it[:, C1:2 * C1], ACT.Copy,
                       scale=t_2[:, 2 - d, rr:rr + 1]).then_inc(ml_iw, 1)
                    act.dma_start(outs["mlstm"][l, d, h], co[r % 2][:, :]).then_inc(co_stored[r % 2], 16)

                pair(0, 0)
                pair(1, 32)
                for r in range(8):
                    if r < 6:
                        pair(r + 2, 32 * (r % 2) + (r + 2) // 2)
                    weigh(r)

            def ssd(l):
                for b in range(6):
                    act.wait_ge(sd_w, b + 1)
                    if b:
                        act.wait_ge(post, POST_SSD + b)
                    af(cth[:, 0:386], cbuf[:, 0:386], ACT.Tanh, scale=0.5).then_inc(row_a, 1)
                    for it in sd_items(b):
                        gate_out(l, it)
                meet(act, MEET["ssd_c", 0])
                for t in range(NT):
                    act.wait_ge(tr_pe, 7 + 2 * t + 1)
                    act.copy(xt[:, t, :], ps[5][:, :]).then_inc(tr_act, 1)
                    act.wait_ge(tr_pe, 7 + 2 * t + 2)
                    act.copy(bt[:, t, :], ps[6][:, 0:P]).then_inc(tr_act, 1)
                meet(act, MEET["ssd_x", 0])
                for d in range(2):
                    act.wait_ge(sd_o, (1, 5)[d])
                    act.dma_start(outs["ssd"][l, d], (ho0, ho1)[d][:, :, :]).then_inc(stored, 16)
                    for slot in range(6 + 3 * d, 9 + 3 * d):
                        for it in sd_items(slot):
                            gate_out(l, it)
                pair(8, 64)
                for r in range(16):
                    if r < 15:
                        pair(9 + r, 64 + 32 * ((r + 1) % 2) + (r + 1) // 2)
                    for it in sd_items(12 + r):
                        gate_out(l, it)

            def branches(l):
                n = 0
                for b, yb in enumerate((y_hg, y_ml, y_mb)):
                    act.copy(y_hi[:, b, :, :], yb[:, :, :]).then_inc(br_a, 1)
                for mblk in range(4):
                    for c in range(3):
                        ahead(l, UM + U_IN + 3 * mblk + c)

            def out_proj(l):
                for k in range(U_OUT):
                    ahead(l, UM + U_IN + U_BR + k)
                    evac_gated(l, UM + U_IN + U_BR + k, ps[k % 2], 5 * KC + k, KC + k, k % 2)
                meet(act, MEET["out", 0])

            with act.Fori(0, L) as l:
                step.n = 0
                act.dma_start(par[:, :], ins["par"][l]).then_inc(par_loaded, 16)
                for n in range(KC):
                    high(0, n)
                ffn(l, 0, UF1)
                layer_norm(0)
                meet(act, MEET["ln", 0])
                act.dma_start(hs[:, :, :, :], ins["hgrn"][l]).then_inc(st_loaded, 16)
                nsil = 0
                for item in items("hf", "hq", "hi", "hg"):
                    what, b = item[3]
                    if what == "hf":
                        d, h = b // NH, b % NH

                        def body(n, bank):
                            af(cc[:, d, h, :, 1:C1], bank[:, 0:T].rearrange("p (a b) -> p a b", b=P), ACT.Copy)
                            return af(kk[:, d, h, :], bank[:, 0:T], ACT.Tanh, scale=-0.5)
                    elif what == "hq":
                        def body(n, bank):
                            nonlocal nsil
                            tmp_free(8 + nsil - 1 if nsil >= 2 else 0)
                            af(q[:, b, :], bank[:, 0:T], ACT.Copy, scale=0.5)
                            ins_ = af(ke[nsil % 2][:, 0:3, :].rearrange("p a b -> p (a b)"), bank[:, 0:T], ACT.Tanh,
                                      scale=0.5)
                            nsil += 1
                            return ins_
                    elif what == "hi":
                        def body(n, bank):
                            return act.copy(v[:, n, :], bank[:, :])
                    else:
                        def body(n, bank):
                            nonlocal nsil
                            tmp_free(8 + nsil - 1)
                            af(hgate[:, n, :], bank[:, :], ACT.Copy, scale=0.5)
                            ins_ = af(ke[nsil % 2][:, :, :].rearrange("p a b -> p (a b)"), bank[:, :], ACT.Tanh,
                                      scale=0.5)
                            nsil += 1
                            return ins_
                    project_out(l, item, body, what in ("hi", "hg"))
                    if item is not items("hq")[-1]:
                        continue
                    for b in range(8):
                        act.wait_ge(post, b + 1)
                        dst = cc[:, b // NH, b % NH, :, 1:C1]
                        step(af(dst, dst, ACT.Exp, scale=-1.0))
                        if b % 2:
                            ahead(l, UM + 12 + b // 2)
                    step.done()
                    for b in range(8):
                        if b >= 2:
                            act.wait_ge(hg_lnd, b - 1)
                        dst = cc[:, b // NH, b % NH, :, 1:C1]
                        af(ea[b % 2][:, 0:3, :], dst, ACT.Ln, bias=1.0, scale=lb[:, b:b + 1])
                        af(dst, dst, ACT.Ln, bias=1.0).then_inc(hg_ln, 1)
                        if b % 2:
                            ahead(l, UM + 16 + b // 2)
                meet(act, MEET["hg_in", 0])
                hgrn(l)
                meet(act, MEET["hg", 0])
                normed(0, lambda t: ps[4 + t][:, :], NH, P)
                act.wait_ge(stored, l * (16 * STORES) + 32)
                for item in items("mq", "mk", "gr", "mv", "mo"):
                    what, b = item[3]
                    if what == "mq":
                        body = lambda n, bank: af(mq[:, b, :], bank[:, 0:T], ACT.Copy)
                    elif what == "mk":
                        body = lambda n, bank: af(mk[:, b, :], bank[:, 0:T], ACT.Copy, scale=P ** -0.5)
                    elif what == "gr":
                        body = lambda n, bank: act.copy((ga, gb)[b][:, :], bank[:, 0:T])
                    elif what == "mv":
                        body = lambda n, bank: act.copy(va[:, n, :, 0:P],
                                                        bank[:, :].rearrange("p (a b) -> p a b", b=P))
                    else:
                        body = lambda n, bank: af(mo[:, n, :], bank[:, :], ACT.Tanh, scale=0.5)
                    project_out(l, item, body)
                meet(act, MEET["ml_in", 0])
                rows(l)
                for d in range(2):
                    act.dma_start(outs["m"][l, d], mout[32 * d:32 * d + NH, :]).then_inc(stored, 16)
                meet(act, MEET["rows", 0])
                act.dma_start(cs[:, :, :, :], ins["mlstm"][l]).then_inc(st_loaded, 16)
                mlstm(l)
                meet(act, MEET["ml", 0])
                normed(1, lambda t: hout[:, t, :], NH, P)
                meet(act, MEET["mln", 0])
                act.dma_start(ht_s[:, :, :, :], ins["ssd"][l]).then_inc(st_loaded, 16)
                nmz = 0
                for item in items("xbc", "mz"):
                    what, b = item[3]
                    if what == "xbc":
                        def body(n, bank):
                            af(xpad[:, b, 1:1 + P], bank[:, 0:P], ACT.Copy)
                            return af(xpad[:, b, P + 3:3 + T], bank[:, P:T], ACT.Copy)
                    else:
                        def body(n, bank):
                            tmp_free(POST_MZ + n if n else 0)
                            af(mz[:, n, :], bank[:, :], ACT.Copy, scale=0.5)
                            return af(zth[:, :], bank[:, :], ACT.Tanh, scale=0.5)
                    project_out(l, item, body)
                meet(act, MEET["ssd_in", 0])
                ssd(l)
                meet(act, MEET["ssd", 0])
                act.wait_ge(stored, l * (16 * STORES) + 16 * STORES)
                for p_ in range(2):
                    act.wait_ge(co_stored[p_], (l + 1) * 64)
                normed(2, lambda t: mz[:, t, :], 1, MIX)
                meet(act, MEET["br_in", 0])
                branches(l)
                out_proj(l)
                layer_norm(1)
                ffn(l, 1, UF2)
                layer_norm(2)
                meet(act, MEET["end", 0])
                layer_over(act, l, "act")

        @block.vector
        def _(dve):
            tt, ts, stt = nc.vector.tensor_tensor, nc.vector.tensor_scalar, nc.vector.scalar_tensor_tensor
            cp = nc.vector.tensor_copy
            step = Steps(dve, dve_step)

            nc.vector.memset(eps[:, 0:1], LN_EPS)
            nc.vector.memset(eps[:, 1:2], RMS_EPS)
            dve.wait_ge(cond_loaded, 16 * 4)
            dve.wait_ge(ready, 1)
            stt(cond_t[:, :, :], cond_t[:, :, :], 1.0, cond[:, :, :], ALU.add, ALU.mult).then_inc(ready, 1)
            dve.wait_ge(ready, 2)
            ts(cond[:, :, :], cond_t[:, :, :], 0.5, None, ALU.mult).then_inc(ready, 1)
            dve.wait_ge(ready, 3)
            cp(cond_s[:, :, 0:2], cond[:, :, :]).then_inc(start_v, 1)
            dve.wait_ge(start_v, 1)
            tt(cond_s[:, :, 2:4], cond[:, :, :], cond_s[:, :, 0:2].bitcast(F32), ALU.subtract).then_inc(start_v, 1)
            tt(lb_w[:, 2, :], lb_in[:, 0, :], lb_in[:, 1, :], ALU.max).then_inc(start_v, 1)
            dve.wait_ge(start_v, 3)
            tt(lb_w[:, 0:2, :], lb_in[:, :, :], lb_w[:, 2:3, :].to_broadcast([P, 2, 8]),
               ALU.subtract).then_inc(ready, 1)
            with dve.Fori(0, U_MOD0 // NRAW) as i:
                for m in range(NRAW):
                    dve.wait_ge(w_hi, i * NRAW + (m + 1))
                    tt(wlo[m][:, LOW0:UW], raw[m][:, LOW0:UW], whi[m][:, LOW0:UW].bitcast(F32),
                       ALU.subtract).then_inc(low0, 1)
            dve.wait_ge(start_loads, 16 * 8)
            tt(x[:, :, P:T], x[:, :, P:T], pos[:, :, :], ALU.add)
            cp(hmask[:, :, :, :], hmask_in[:, :, :, :])
            nc.vector.memset(lbs[:, 0, :], 0.0)
            dve.wait_ge(ready, 5)
            tt(lb_w[:, 2, :], lb_w[:, 0, :], lb_w[:, 1, :], ALU.add).then_inc(start_v, 1)
            dve.wait_ge(start_v, 4)
            nc.vector.reciprocal(lb_w[:, 3, :], lb_w[:, 2, :]).then_inc(start_v, 1)
            dve.wait_ge(start_v, 5)
            tt(lbs[:, 1, :], lb_w[:, 1, :], lb_w[:, 3, :], ALU.mult).then_inc(start_v, 1)
            dve.wait_ge(start_v, 6)

            def adaln(chunks, src, bias, done):
                a, b = chunks[0] * KC, (chunks[-1] + 1) * KC
                m = mod[:, a:b, :]
                done(tt(m, src, bias.unsqueeze(2).to_broadcast([P, b - a, 2]), ALU.add))
                for j in chunks:
                    c = mod[:, j * KC:(j + 1) * KC, :]
                    if j % 3 == 1:
                        done(ts(c, c, 1.0, None, ALU.add))
                    if j in (2, 8):
                        done(ts(c, c, 0.5, None, ALU.mult))

            marks = {"n": 6}

            def start_done(ins_):
                marks["n"] += 1
                ins_.then_inc(start_v, 1)
                dve.wait_ge(start_v, marks["n"])

            dve.wait_ge(turned0, U_MOD0 // 4 + 1)
            adaln(MOD_ORDER[4:], ps[7][:, 0:2 * U_MOD0].rearrange("p (a b) -> p a b", b=2), bmod0[:, :], start_done)

            def modulated(j, n):
                sh, sc = 3 * j * KC, (3 * j + 1) * KC
                if j:
                    dve.wait_ge(ln_x, KC * (j - 1) + n + 1)
                if n >= 2:
                    dve.wait_ge(md_lo, KC * j + n - 1)
                for gi, (a, b) in enumerate(GROUPS):
                    last = ts(ht[n % 2][:, a:b], x[:, n, a:b], mod[:, sc + n, gi:gi + 1],
                              mod[:, sh + n, gi:gi + 1], ALU.mult, ALU.add)
                last.then_inc(md_t, 1)

            def low(j, n):
                dve.wait_ge(md_hi, KC * j + n + 1)
                tt(h_lo[:, n, :], ht[n % 2][:, :], h_hi[:, n, :].bitcast(F32), ALU.subtract).then_inc(md_lo, 1)

            def layer_norm(j):
                dve.wait_ge(ln_mean, j + 1)
                for n in range(KC):
                    tt(x[:, n, :], x[:, n, :], ps[4][:, 0:T], ALU.subtract).then_inc(ln_cent, 1)
                dve.wait_ge(ln_std, j + 1)
                step(nc.vector.reciprocal(rstd[:, :], std[:, :]))
                step.done()
                for n in range(KC + 2):
                    if n < KC:
                        tt(x[:, n, :], x[:, n, :], rstd[:, :], ALU.mult).then_inc(ln_out, 1)
                    if j < 2 and n:
                        if n >= 2:
                            low(j + 1, n - 2)
                        if n <= KC:
                            modulated(j + 1, n - 1)

            def ffn(l, j, u0):
                n0 = step.n
                with dve.Fori(0, U_GU // 4) as i:
                    step.off = i * 6
                    for jj in range(2):
                        dve.wait_ge(gate_t, i * 2 + (NF * j + jj + 1))
                        step(stt(sbf[jj][:, :], tb[jj][:, :], 1.0, ps[2 * jj][:, 0:T], ALU.add, ALU.mult))
                        unit_done(dve, l, i * 4 + (u0 + 2 * jj + 1))
                        step.done()
                        stt(vb[jj][:, :], sbf[jj][:, :], 0.5, ps[2 * jj + 1][:, 0:T], ALU.mult,
                            ALU.mult).then_inc(gated, 1)
                        dve.wait_ge(gated, i * 2 + (NF * j + jj + 3))
                        f = i * 2 + jj
                        step(cp(act_hi[:, bass.ds(f, 1), :], vb[jj][:, :].unsqueeze(1)))
                        step.done()
                        step(tt(act_lo[:, bass.ds(f, 1), :], vb[jj][:, :].unsqueeze(1),
                                act_hi[:, bass.ds(f, 1), :].bitcast(F32), ALU.subtract))
                assert step.n - n0 == 6
                step.off, step.n = 0, n0 + 6 * (U_GU // 4)
                meet(dve, MEET["ffn", j])
                down(l, 2 * KC * j, 2, 4)
                meet(dve, MEET["down", j])

            def down(l, c0, iters, per):
                with dve.Fori(0, iters) as i:
                    for jj in range(per):
                        dve.wait_ge(down_ev, i * per + (c0 + jj + 1))
                        xb = x[:, bass.ds(i * per + jj, 1), :]
                        stt(xb, xb, ALPHA, vb[jj % 2][:, :].unsqueeze(1), ALU.mult, ALU.add).then_inc(resid, 1)

            def normed(b, src, gate, groups, width):
                def sums(t):
                    dve.wait_ge(nm_sq, b * NT + t + 1)
                    nc.vector.reduce_sum(nsm[:, 0, 0:groups],
                                         nsq[:, :, :].rearrange("p a b -> p (a b)").rearrange(
                                             "p (g e) -> p g e", g=groups), axis=AX.X).then_inc(nm_ms, 1)

                sums(0)
                for t in range(NT):
                    n = b * NT + t
                    dve.wait_ge(nm_sd, n + 1)
                    if t:
                        dve.wait_ge(nm_y, n)
                    step(nc.vector.reciprocal(nsm[:, 2, 0:groups], nsm[:, 1, 0:groups]))
                    if t < NT - 1:
                        sums(t + 1)
                    step.done()
                    if t:
                        dve.wait_ge(nm_tr, n)
                    out = nyn[:, :, :]
                    if groups == 1:
                        ts(out.rearrange("p a b -> p (a b)"), src(t), nsm[:, 2, 0:1], None,
                           ALU.mult).then_inc(nm_y, 1)
                        continue
                    step(tt(out, src(t).rearrange("p (a b) -> p a b", b=P),
                            nsm[:, 2, :].unsqueeze(2).to_broadcast([P, NH, P]), ALU.mult))
                    step.done()
                    flat = out.rearrange("p a b -> p (a b)")
                    tt(flat, flat, gate[:, t, :], ALU.mult).then_inc(nm_y, 1)

            def hgrn_in():
                for item in items("hf", "hq"):
                    what, b = item[3]
                    e = first_evac[item[3]]
                    if what == "hf":
                        dve.wait_ge(evac, e + 1)
                        dst = cc[:, b // NH, b % NH, :, 1:C1]
                        ts(dst, dst, -44.0, None, ALU.max)
                        kb = kk[:, b // NH, b % NH, :]
                        ts(kb, kb, 1.0, om[:, b:b + 1], ALU.add, ALU.mult).then_inc(post, 1)
                    elif what == "hq":
                        dve.wait_ge(evac, e + 1)
                        stt(q[:, b, :], ke[b % 2][:, 0:3, :].rearrange("p a b -> p (a b)"), 1.0, q[:, b, :],
                            ALU.add, ALU.mult).then_inc(post, 1)
                for b in range(8):
                    dve.wait_ge(hg_ln, b + 1)
                    dst = cc[:, b // NH, b % NH, :, 1:C1]
                    tt(dst, ea[b % 2][:, 0:3, :], dst, ALU.subtract).then_inc(hg_lnd, 1)
                dve.wait_ge(hg_lnd, 8)
                step(nc.vector.memset(cc[:, :, :, :, 0:1].rearrange("p a b c d -> p (a b c d)"), 0.0))
                step.done()
                for b in range(8):
                    row = cc[:, b // NH, b % NH, :, :].rearrange("p a b -> p (a b)")
                    step(nc.vector.tensor_tensor_scan(row, keep[:, :], row, 0.0, ALU.mult, ALU.add))
                for a in (*qe, *att):
                    step(nc.vector.memset(a[:, :, :], 0.0))
                for n in range(NT):
                    dve.wait_ge(evac, first_evac["hg", 0] + n + 1)
                    stt(hgate[:, n, :], ke[n % 2][:, :, :].rearrange("p a b -> p (a b)"), 1.0,
                        hgate[:, n, :], ALU.add, ALU.mult).then_inc(post, 1)
                dve.wait_ge(post, 8 + NH + NT)
                for a in ke:
                    step(nc.vector.memset(a[:, :, :], 0.0))
                step.done()

            def hgrn():
                ph = lambda a, hh: a.rearrange("p g (b two h) -> p g b two h", two=2, h=hh)

                def exponents(o):
                    s, d, t, what, hh = ops[o]
                    if what == "diag":
                        return
                    e, ct = ea[o % 3], cc[:, d, :, t, :]
                    v_ = ct[:, :, 1 - d:C1 - d]
                    tot = ct[:, :, P:C1].to_broadcast([P, NH, P])
                    if o >= 3:
                        dve.wait_ge(hg_b, cnt["b", o - 3])
                    if what == "level":
                        nb = P // (2 * hh)
                        ev, vv = ph(e[:, :, :], hh), ph(v_, hh)
                        mid = ct[:, :, hh:C1:2 * hh].unsqueeze(3).to_broadcast([P, NH, nb, hh])
                        tt(ev[:, :, :, 0, :], mid, vv[:, :, :, 0, :], ALU.subtract)
                        tt(ev[:, :, :, 1, :], vv[:, :, :, 1, :], mid, ALU.subtract).then_inc(hg_a, 1)
                    elif (what == "inter") == (d == 0):
                        cp(e[:, :, :], v_).then_inc(hg_a, 1)
                    else:
                        tt(e[:, :, :], tot, v_, ALU.subtract).then_inc(hg_a, 1)

                def products(o):
                    s, d, t, what, hh = ops[o]
                    if what == "diag":
                        return
                    c = slice(t * P, (t + 1) * P)
                    b, qv, kv = o % 2, q[:, :, c], kk[:, d, :, c]
                    dve.wait_ge(hg_e, cnt["e", o])
                    if o >= 2:
                        dve.wait_ge(hg_m, o - 1)
                    if what == "level":
                        ev = ph(ea[o % 3][:, :, :], hh)
                        qs, ks = 1 - d, d
                        tt(ph(qe[b][:, :, :], hh)[:, :, :, qs, :], ph(qv, hh)[:, :, :, qs, :],
                           ev[:, :, :, qs, :], ALU.mult)
                        tt(ph(ke[b][:, :, :], hh)[:, :, :, ks, :], ph(kv, hh)[:, :, :, ks, :],
                           ev[:, :, :, ks, :], ALU.mult).then_inc(hg_b, 1)
                    elif what == "inter":
                        tt(qe[b][:, :, :], qv, ea[o % 3][:, :, :], ALU.mult).then_inc(hg_b, 1)
                    else:
                        tt(ke[b][:, :, :], kv, ea[o % 3][:, :, :], ALU.mult).then_inc(hg_b, 1)

                def take(o):
                    s, d, t, what, hh = ops[o]
                    if what == "inter":
                        return
                    S = ps[2 + o % 2][:, :].rearrange("p (a b) -> p a b", b=P)
                    dve.wait_ge(hg_m, o + 1)
                    if o:
                        dve.wait_ge(hg_c, cnt["c", o] - 1)
                    if what == "state":
                        if s:
                            dve.wait_ge(hg_m2, s)
                        cp(kT[:, :, :], S).then_inc(hg_c, 1)
                        return
                    lev = LEVELS.index(hh) if what == "level" else len(LEVELS)
                    if lev == 0 and s >= 2:
                        dve.wait_ge(hg_o, s - 1)
                    nc.vector.copy_predicated(att[d][:, :, :], hmask[:, d, lev:lev + 1, :].to_broadcast(
                        [P, NH, P]), S).then_inc(hg_c, 1)

                def states(o):
                    s, d, t, what, hh = ops[o]
                    if what != "state":
                        return
                    dve.wait_ge(hg_m2, s + 1)
                    if t == 0:
                        cp(so[d][:, :, :], ps[7][:, :].rearrange("p (a b) -> p a b", b=P)).then_inc(hg_c2, 1)
                        return
                    dve.wait_ge(st_loaded, 16)
                    for g in range(NH):
                        last = stt(hs[:, d, g, :], hs[:, d, g, :], etot[:, d, g:g + 1],
                                   ps[7][:, g * P:(g + 1) * P], ALU.mult, ALU.add)
                    last.then_inc(hg_c2, 1)

                exponents(0)
                exponents(1)
                for o in range(len(ops)):
                    if o + 2 < len(ops):
                        exponents(o + 2)
                    products(o)
                    if o:
                        take(o - 1)
                    if o >= 2:
                        states(o - 2)
                take(len(ops) - 1)

            def rows():
                pr_ = PAR["row"]
                col = lambda i: par[:, pr_ + i:pr_ + i + 1]
                fw, bw, f64, b96 = slice(0, 32), slice(32, 64), slice(64, 96), slice(96, 128)
                inc_ = cr[:, :, 1:C1]
                exc = cr[:, :, 0:P]
                v3 = lambda a: a[:, :].rearrange("p (a b) -> p a b", b=P)

                def s_(ins):
                    step(ins)
                    step.done()

                ts(r_w[:, :], ga[:, :], col(0), sgn[:, :], ALU.add, ALU.mult).then_inc(row_d, 1)
                dve.wait_ge(row_d, 1)
                dve.wait_ge(row_a, 2)
                s_(ts(r_u[:, :], r_e[:, :], 1.0, None, ALU.add))
                stt(r_n[:, :], r_u[:, :], -1.0, r_e[:, :], ALU.add, ALU.subtract).then_inc(row_d, 1)
                dve.wait_ge(row_d, 2)
                dve.wait_ge(row_a, 4)
                s_(tt(r_u[:, :], r_u[:, :], r_n[:, :], ALU.subtract))
                s_(stt(r_w[:, :], r_w[:, :], 0.0, r_u[:, :], ALU.max, ALU.add))
                s_(nc.vector.memset(cr[:, :, 0:1].rearrange("p a b -> p (a b)"), 0.0))
                s_(ts(inc_, v3(r_w), coef[:, :], -1.0, ALU.mult, ALU.mult))
                flat = cr[:, :, :].rearrange("p a b -> p (a b)")
                s_(nc.vector.tensor_tensor_scan(flat, keep[:, :], flat, 0.0, ALU.mult, ALU.add))
                s_(ts(gb[:, :], gb[:, :], col(2), None, ALU.add))
                step(tt(v3(x_1)[fw], v3(gb)[fw], inc_[fw], ALU.subtract))
                step(tt(v3(x_1)[bw], v3(gb)[bw], exc[bw], ALU.add))
                step(ts(v3(x_1)[f64], inc_[f64], -1.0, None, ALU.mult))
                step(cp(v3(x_1)[b96], exc[b96]))
                step(cp(v3(x_5)[f64], inc_[f64]))
                step(ts(v3(x_5)[b96], exc[b96], -1.0, None, ALU.mult))
                step(cp(x_2[64:128, :], r_w[64:128, :]))
                step(nc.vector.memset(minit[:, 0:1], 0.0))
                step.done()
                s_(cp(minit[fw, 1:2], par[fw, pr_ + 3:pr_ + 4]))
                s_(cp(minit[bw, 0:1], cr[bw, 0, P:C1]))
                s_(tt(minit[bw, 2:3], par[bw, pr_ + 3:pr_ + 4], cr[bw, 2, P:C1], ALU.add))

                def running(t, back):
                    r = bw if back else fw
                    c = slice(t * P, (t + 1) * P)
                    a, n_ = x_1[r, c], r_N[r, c]
                    if back:
                        a, n_ = a[:, ::-1], n_[:, ::-1]
                    s_(nc.vector.tensor_tensor_scan(n_, a, a, minit[r, t:t + 1], ALU.max, ALU.max))

                running(0, False)
                running(0, True)
                running(1, False)
                running(2, True)
                s_(tt(minit[fw, 2:3], r_N[fw, 2 * P - 1:2 * P], cr[fw, 1, P:C1], ALU.add))
                s_(tt(minit[bw, 1:2], r_N[bw, 2 * P:2 * P + 1], cr[bw, 1, P:C1], ALU.add))
                running(2, False)
                running(1, True)
                step(tt(mout[fw, :], r_N[fw, P - 1:P], cr[fw, 0, P:C1], ALU.add))
                step(cp(mout[bw, :], r_N[bw, 0:1]))
                step(ts(x_5[0:64, :], r_N[0:64, :], -1.0, None, ALU.mult))
                step(stt(v3(x_3)[fw], inc_[fw], -1.0, v3(r_N)[fw], ALU.mult, ALU.subtract))
                step(tt(v3(x_3)[bw], exc[bw], v3(r_N)[bw], ALU.subtract))
                step(cp(v3(x_3)[f64], inc_[f64]))
                tot = cr[:, :, P:C1].to_broadcast([P, NT, P])
                step(tt(v3(x_3)[b96], tot[b96], exc[b96], ALU.subtract))
                step(nc.vector.memset(x_4[0:64, :], 0.0))
                step(tt(v3(x_4)[f64], tot[f64], inc_[f64], ALU.subtract))
                cp(v3(x_4)[b96], exc[b96]).then_inc(row_d, 1)
                dve.wait_ge(row_d, 3)
                dve.wait_ge(row_a, 5)
                step(cp(lastw[fw, :], x_2[fw, 2 * P - 1:2 * P]))
                step(cp(lastw[bw, :], x_2[bw, 2 * P:2 * P + 1]))
                step(cp(lastw[f64, :], x_3[f64, 2 * P - 1:2 * P]))
                s_(cp(lastw[b96, :], x_3[b96, 2 * P:2 * P + 1]))
                ts(dlast[:, :], ident[:, :], lastw[:, :], None, ALU.mult).then_inc(row_d, 1)
                dve.wait_ge(row_d, 4)
                step(nc.vector.memset(va[:, :, :, P:C1].rearrange("p a b c -> p (a b c)"), 1.0))
                s_(ts(mo[:, :, :], mo[:, :, :], 0.5, 0.5, ALU.mult, ALU.add))

            def exps(r, d):
                dve.wait_ge(pr_bc, r + 1)
                if r >= 2:
                    dve.wait_ge(pr_e, r - 1)
                tt(pt[r % 2][:, :].rearrange("p (a b) -> p a b", b=P),
                   neg[:, d:d + 1, :].to_broadcast([P, NT, P]),
                   ps[r % 2][:, 0:T].rearrange("p (a b) -> p a b", b=P), ALU.add).then_inc(pr_x, 1)

            def scores(r, bank, nqk, rr=None):
                dve.wait_ge(pr_e, r + 1)
                dve.wait_ge(pr_qk, nqk)
                if r >= 2:
                    dve.wait_ge(pr_n, r - 1)
                if rr is None:
                    tt(st[r % 2][:, :], pr[r % 2][:, :], bank[:, 0:T], ALU.mult).then_inc(pr_s, 1)
                    return
                for t in range(NT):
                    c = slice(t * P, (t + 1) * P)
                    last = stt(st[r % 2][:, c], pr[r % 2][:, c], t_2[:, t, rr:rr + 1], bank[:, c], ALU.mult, ALU.mult)
                last.then_inc(pr_s, 1)

            def mlstm(l):
                def weights(r):
                    h, d = r // 2, r % 2
                    if r >= 2:
                        dve.wait_ge(ml_it, r - 1)
                    for n, t in enumerate((0, 1 + d)):
                        lastc = t * P + (P - 1 if d == 0 else 0)
                        last = ts(kw[r % 2][:, n, :], mkt[:, t, h * P:(h + 1) * P],
                                  pr[r % 2][:, lastc:lastc + 1], None, ALU.mult)
                    last.then_inc(ml_kw, 1)

                def carry(r):
                    h, d = r // 2, r % 2
                    dve.wait_ge(ml_it, r + 1)
                    if r >= 2:
                        dve.wait_ge(co_stored[r % 2], l * 64 + 16 * (r // 2))
                    it = ps[6 + r % 2]
                    cp(co[r % 2][:, :], it[:, C1:2 * C1])
                    rr = 32 * d + h
                    stt(cs[:, d, h, :], cs[:, d, h, :], wb[:, rr:rr + 1], it[:, 2 * C1:3 * C1], ALU.mult,
                        ALU.add).then_inc(ml_cu, 1)

                def heads(r):
                    h, d = r // 2, r % 2
                    rr = 32 * d + h
                    dve.wait_ge(pr_n, r + 1)
                    dve.wait_ge(ml_iw, r + 1)
                    nm = ps[4 + r % 2][:, 0:3 * C1].rearrange("p (a b) -> p a b", b=C1)
                    step(cp(tmpb[:, 0, :], nm[:, 0, :]))
                    step(tt(tmpb[:, 1:3, :], tmpa[:, 1:3, :], nm[:, 1:3, :], ALU.add))
                    step.done()
                    dn = tmpb[:, :, P:C1].rearrange("p a b -> p (a b)")
                    step(stt(den[:, 0, :], dn, -1.0, dn, ALU.mult, ALU.max))
                    step.done()
                    step(tt(den[:, 0, :], den[:, 0, :], t_3[:, :, rr], ALU.max))
                    step.done()
                    step(nc.vector.reciprocal(den[:, 1, :], den[:, 0, :]))
                    step.done()
                    for t in range(NT):
                        dst = hout[:, t, h * P:(h + 1) * P]
                        if d == 0:
                            last = ts(dst, tmpb[:, t, 0:P], den[:, 1, t:t + 1], None, ALU.mult)
                        else:
                            last = stt(dst, tmpb[:, t, 0:P], den[:, 1, t:t + 1], dst, ALU.mult, ALU.add)
                    last.then_inc(ml_h, 1)

                exps(0, 0)
                for r in range(8):
                    if r < 7:
                        exps(r + 1, (r + 1) % 2)
                    scores(r, ps[2 + r // 2 % 2], r // 2 + 1)
                    weights(r)
                    if r:
                        heads(r - 1)
                    carry(r)
                heads(7)

            def ssd():
                for b in range(6):
                    w0 = PAR["convw"] + 3 * b
                    tap = lambda j: par[:, w0 + j:w0 + j + 1]
                    bias = par[:, PAR["convb"] + b:PAR["convb"] + b + 1]
                    if b:
                        dve.wait_ge(post, POST_SSD + b)
                    step(ts(cbuf[:, 0:386], xpad[:, b, 1:387], tap(1), bias, ALU.mult, ALU.add))
                    step.done()
                    step(stt(cbuf[:, 0:386], xpad[:, b, 0:386], tap(0), cbuf[:, 0:386], ALU.mult, ALU.add))
                    step.done()
                    stt(cbuf[:, 0:386], xpad[:, b, 2:388], tap(2), cbuf[:, 0:386], ALU.mult,
                        ALU.add).then_inc(sd_w, 1)
                    dve.wait_ge(row_a, 7 + b)
                    step(ts(cth[:, 0:386], cth[:, 0:386], 0.5, 0.5, ALU.mult, ALU.add))
                    step.done()
                    step(tt(xs[:, b, 0:P], cth[:, 0:P], cbuf[:, 0:P], ALU.mult))
                    tt(xs[:, b, P:T], cth[:, P + 2:T + 2], cbuf[:, P + 2:T + 2], ALU.mult).then_inc(post, 1)
                meet(dve, MEET["ssd_c", 0])
                meet(dve, MEET["ssd_x", 0])
                v8 = lambda a: a.rearrange("p (h e) -> p h e", e=SP_)
                rows8 = lambda a, t, d: a[:, t, 64 + 32 * d:72 + 32 * d].unsqueeze(2).to_broadcast([P, SH, SP_])
                n = 0
                for d in range(2):
                    def weigh(t):
                        step(tt(v8(xw[:, :]), v8(xt[:, t, :]), rows8(t_2, t, d), ALU.mult))
                        step.done()
                        tt(v8(xw[:, :]), v8(xw[:, :]), rows8(t_4, t, d), ALU.mult).then_inc(sd_w, 1)

                    weigh(0)
                    for stp, t in enumerate((0, 1 + d, 2 - d)):
                        if stp:
                            dve.wait_ge(sd_p, n + 1)
                            dst = yx[:, t - 1, :]
                            for g in range(2):
                                half = slice(256 * g, 256 * g + 256)
                                last = tt(v8((dst, zth)[d][:, half]), v8(ps[(7, 2)[g]][:, 0:256]),
                                          rows8(t_3, t, d)[:, 4 * g:4 * g + 4, :], ALU.mult)
                            if d == 0:
                                last.then_inc(sd_o, 1)
                            else:
                                step(last)
                                step.done()
                                tt(dst, dst, zth[:, :], ALU.add).then_inc(sd_o, 1)
                                dve.wait_ge(sd_o, n + 1)
                            n += 1
                        if stp < 2:
                            dve.wait_ge(sd_p, n + 1)
                            for g in range(2):
                                gp = slice(64 * g, 64 * g + 64)
                                src = ps[3][gp, 256 * g:256 * g + 256].rearrange("p (h e) -> p h e", e=SP_)
                                if stp == 0:
                                    last = cp((ho0, ho1)[d][gp, :, :], src)
                                else:
                                    h0 = 64 + 32 * d + 4 * g
                                    step(tt(ht_s[gp, d, :, :], ht_s[gp, d, :, :],
                                            wb[gp, h0:h0 + 4].unsqueeze(2).to_broadcast([64, 4, SP_]), ALU.mult))
                                    step.done()
                                    last = tt(ht_s[gp, d, :, :], ht_s[gp, d, :, :], src, ALU.add)
                            last.then_inc(sd_o, 1)
                            n += 1
                            if stp == 0:
                                weigh(1 + d)
                exps(8, 0)
                for r in range(16):
                    if r < 15:
                        exps(9 + r, (r + 1) % 2)
                    scores(8 + r, ps[2], 5 + r // 8, 64 + 32 * (r % 2) + r // 2)
                def done(ins_):
                    step(ins_)
                    step.done()

                dve.wait_ge(evac, first_evac["turn", U_MOD // 4 - 1] + 1)
                b0 = PAR["bmod"]
                adaln(MOD_ORDER[:4], modr[:, 0:32, :], par[:, b0:b0 + 32], done)
                adaln(MOD_ORDER[4:], modr[:, 32:72, :], par[:, b0 + 32:b0 + 72], done)
                dve.wait_ge(pr_n, 24)
                for t in range(NT):
                    y = xt[:, t, :]
                    md = par[:, PAR["mbd"]:PAR["mbd"] + 8].unsqueeze(2).to_broadcast([P, SH, SP_])
                    step(tt(v8(y), v8(y), md, ALU.mult))
                    step.done()
                    step(tt(y, y, ps[4 + t][:, :], ALU.add))
                    step.done()
                    if t:
                        step(tt(y, y, yx[:, t - 1, :], ALU.add))
                        step.done()
                    step(tt(mz[:, t, :], mz[:, t, :], y, ALU.mult))

            def branches(l):
                for b, yb in enumerate((y_hg, y_ml, y_mb)):
                    dve.wait_ge(br_a, b + 1)
                    tt(y_lo[:, b, :, :], yb[:, :, :], y_hi[:, b, :, :].bitcast(F32),
                       ALU.subtract).then_inc(br_y, 1)
                n = 0
                for mblk in range(4):
                    z = (zt0, zt1)[mblk % 2]
                    for c in range(3):
                        unit_done(dve, l, UM + U_IN + n)
                        for j in range(2):
                            bank = ps[2 * (n % 2) + j][:, 0:T]
                            gt = gates[:, 8 * c + 2 * mblk + j, :]
                            if c == 0:
                                if mblk >= 2:
                                    dve.wait_ge(br_hi, 2 * (mblk - 1))
                                last = stt(z[:, j, :], gt, 1.0, bank, ALU.add, ALU.mult)
                            else:
                                last = stt(gt, gt, 1.0, bank, ALU.add, ALU.mult)
                        last.then_inc(br_z, 1)
                        if c:
                            dve.wait_ge(br_z, n + 1)
                            g2 = gates[:, 8 * c + 2 * mblk:8 * c + 2 * mblk + 2, :]
                            step(tt(z[:, :, :], z[:, :, :], g2, ALU.add))
                            step.done()
                        n += 1
                    step.done()
                    ts(z[:, :, :], z[:, :, :], 0.5, None, ALU.mult).then_inc(br_z2, 1)
                    dve.wait_ge(br_z2, mblk + 1)
                    for j in range(2):
                        k = 2 * mblk + j
                        step(cp(h_hi[:, k, :], z[:, j, :]))
                        step.done()
                        tt(h_lo[:, k, :], z[:, j, :], h_hi[:, k, :].bitcast(F32),
                           ALU.subtract).then_inc(br_hi, 1)

            with dve.Fori(0, L) as l:
                step.n = 0
                for _ in range(2):
                    dve.sem_inc(gated, 1)
                    dve.sem_inc(resid, 1)
                step(cp(lb[:, :], lbs[:, bass.ds(l, 1), :].rearrange("p a b -> p (a b)")))
                step.done()
                step(ts(om[:, :], lb[:, :], -0.5, 0.5, ALU.mult, ALU.add))
                dve.wait_ge(par_loaded, (l + 1) * 16)
                step.done()
                for n in range(KC + 1):
                    if n < KC:
                        modulated(0, n)
                    if n:
                        low(0, n - 1)
                ffn(l, 0, UF1)
                layer_norm(0)
                meet(dve, MEET["ln", 0])
                hgrn_in()
                meet(dve, MEET["hg_in", 0])
                hgrn()
                meet(dve, MEET["hg", 0])
                normed(0, lambda t: ps[4 + t][:, :], hgate, NH, P)
                meet(dve, MEET["ml_in", 0])
                rows()
                meet(dve, MEET["rows", 0])
                mlstm(l)
                meet(dve, MEET["ml", 0])
                normed(1, lambda t: hout[:, t, :], mo, NH, P)
                meet(dve, MEET["mln", 0])
                for c in (0, P + 1, P + 2, T + 3):
                    step(nc.vector.memset(xpad[:, :, c:c + 1].rearrange("p a b -> p (a b)"), 0.0))
                for n in range(NT):
                    dve.wait_ge(evac, first_evac["mz", 0] + n + 1)
                    stt(mz[:, n, :], zth[:, :], 1.0, mz[:, n, :], ALU.add, ALU.mult).then_inc(post, 1)
                meet(dve, MEET["ssd_in", 0])
                ssd()
                meet(dve, MEET["ssd", 0])
                normed(2, lambda t: mz[:, t, :], None, 1, MIX)
                meet(dve, MEET["br_in", 0])
                branches(l)
                down(l, KC, U_OUT // 4, 4)
                meet(dve, MEET["out", 0])
                layer_norm(1)
                ffn(l, 1, UF2)
                layer_norm(2)
                meet(dve, MEET["end", 0])
                layer_over(dve, l, "dve")


def constants():
    i = np.arange(P)
    s, t = i[:, None], i[None, :]
    neg = np.stack([np.where(s <= t, 0.0, NEG), np.where(s >= t, 0.0, NEG)], 1).astype(np.float32)
    hm = np.zeros((P, 2, len(LEVELS) + 1, P), np.float32)
    for n, h in enumerate(LEVELS):
        same = s // (2 * h) == t // (2 * h)
        sf, tf = s % (2 * h) < h, t % (2 * h) < h
        hm[:, 0, n], hm[:, 1, n] = same & sf & ~tf, same & ~sf & tf
    hm[:, 0, -1] = hm[:, 1, -1] = s == t
    keep = np.ones((P, NT, C1), np.float32)
    keep[:, :, 0] = 0.0
    sgn = np.where(i < 64, -1.0, 1.0).astype(np.float32)[:, None]
    width, quarter = 64, D // 4
    n = np.arange(NL_TOK)
    freq = np.exp(-math.log(10000.0) * np.arange(quarter, dtype=np.float32) / quarter).astype(np.float32)
    ar = (n // width).astype(np.float32)[:, None] * freq
    ac = (n % width).astype(np.float32)[:, None] * freq
    pos = np.concatenate([np.sin(ar), np.cos(ar), np.sin(ac), np.cos(ac)], -1).astype(np.float32)
    return {"ident": np.eye(P, dtype=np.float32), "mean_w": np.full((P, P), 1.0 / D, np.float32), "neg": neg,
            "hmask": hm, "keep": keep.reshape(P, -1), "sgn": sgn, "pos": pos.T.reshape(KC, P, NL_TOK)
            .transpose(1, 0, 2).copy(), "pick": (i[:, None] % 2 == np.arange(2)).astype(np.float32)}


def laid_out(a):
    a = {k: np.asarray(v) for k, v in a.items()}
    f = np.ascontiguousarray

    def units(w, n):
        lead = w.shape[:-2]
        K, N = w.shape[-2:]
        w = w.reshape(*lead, K // P, P, N // n, n)
        return np.moveaxis(w, (-2, -3, -4, -1), (-4, -3, -2, -1)).reshape(*lead, N // n, P, K // P * n)

    r = {}
    xt = np.concatenate([a["x_prompt"][0], a["x_sample"][0]], 0).T.reshape(KC, P, T)
    r["x"] = f(xt.transpose(1, 0, 2))
    r["cond"] = f(np.stack([a["c_ctx"], a["c"][0]], -1).reshape(KC, P, 2).transpose(1, 0, 2))
    r["hg_lb"] = f(a["hg_lb"].reshape(L, 8, P).transpose(2, 0, 1))
    def rows_units(m):
        n, K, N = m.shape
        return m.reshape(n, 4, 2, P, N // MIX, MIX).transpose(0, 4, 1, 3, 2, 5).reshape(n, N // MIX, 4, P, KC * P)

    wm = rows_units(a["w_mod"]).reshape(L, 9, KC, P, KC * P)
    bm = a["b_mod"].reshape(L, 9, KC, P)

    def streamed(m):
        return np.concatenate([m[:, list(MOD_ORDER[:4])], np.roll(m, -1, 0)[:, list(MOD_ORDER[4:])]], 1).reshape(
            L, U_MOD, *m.shape[3:])

    r["w_mod"] = f(wm[0, :5].reshape(U_MOD0, P, KC * P))
    r["bmod0"] = f(bm[0, :5].reshape(U_MOD0, P).T)
    wm = streamed(wm)
    gu = units(a["ffn_w_gu"], P)
    gu = gu.reshape(L, 2, 2, NF, P, KC * P)
    r["w_gu"] = f(gu.transpose(0, 1, 3, 2, 4, 5).reshape(L, 2, U_GU, P, KC * P))
    dn = np.zeros((L, 2, KC, P, KTHIRDS * UW), np.float32)
    dn[..., :NF * P] = units(a["ffn_w_down"], P)
    dn = dn.reshape(L, 2, KC, P, KTHIRDS, UW)
    r["w_down"] = f(dn.transpose(0, 1, 2, 4, 3, 5).reshape(L, 2, U_DOWN, P, UW))
    w, at, seg = a["w_in"], 0, {}
    for name, size in (("hq", 512), ("hi", 512), ("hg", 512), ("hf", 1024), ("mq", 512), ("mk", 512), ("mv", 512),
                       ("mo", 512), ("mi", 8), ("mf", 8), ("mz", 512), ("xbc", 768), ("dt", 16), ("bg", 3072)):
        seg[name] = w[..., at:at + size]
        at += size
    fm = lambda m: units(m, P)
    tm = lambda m: f(m.reshape(L, 4, 2, P, MIX).transpose(0, 1, 3, 2, 4)).reshape(L, 4, P, KC * P)

    def rows(parts):
        m = np.zeros((L, D, P), w.dtype)
        for at_, p in parts:
            m[..., at_:at_ + p.shape[-1]] = p
        return fm(m)

    mf, mi, dt = seg["mf"], seg["mi"], seg["dt"]
    gr = [rows([(0, mf[..., 0:4]), (32, mf[..., 4:8]), (64, dt[..., 0:8]), (96, dt[..., 8:16])]),
          rows([(0, mi[..., 0:4]), (32, mi[..., 4:8])])]
    bg, wg = fm(seg["bg"]).reshape(L, 6, 4, P, KC * P), wm.reshape(L, 6, 3, 4, P, KC * P)
    b1 = lambda n: bg[:, :, n:n + 1]
    bg = np.concatenate([b1(0), wg[:, :, 0], b1(1), wg[:, :, 1], b1(2), wg[:, :, 2], b1(3)], 2).reshape(
        L, 96, P, KC * P)
    n1, n2 = (sum(GATE_UNITS[w] for w, _ in GATE_SEQ[:n]) for n in (HG_ITEMS, HG_ITEMS + ROW_ITEMS))
    r["w_in"] = f(np.concatenate([fm(seg["hf"]), fm(seg["hq"]), tm(seg["hi"]), tm(seg["hg"]), bg[:, :n1],
                                  fm(seg["mq"]), fm(seg["mk"]), *gr, tm(seg["mv"]), tm(seg["mo"]), bg[:, n1:n2],
                                  fm(seg["xbc"]), tm(seg["mz"]), bg[:, n2:]], 1))
    br = units(a["w_branch"], 2 * P)
    r["w_branch"] = f(br.transpose(0, 2, 1, 3, 4).reshape(L, U_BR, P, KC * P))
    r["w_out"] = f(units(a["w_out"], P))
    par = np.zeros((L, P, NPAR), np.float32)

    def put(name, m):
        par[:, :, PAR[name]:PAR[name] + m.shape[1]] = m.transpose(0, 2, 1)

    put("bmod", streamed(bm))
    put("ln", np.stack([a["ln_g"], a["ln_b"]], 2).reshape(L, 48, P))
    put("normg", np.stack([a["hg_norm_g"], a["ml_norm_g"], a["mb_norm_g"]], 1).reshape(L, 12, P))
    put("convw", a["mb_conv_w"].reshape(L, 3, 6, P).transpose(0, 2, 1, 3).reshape(L, 18, P))
    put("convb", a["mb_conv_b"].reshape(L, 6, P))
    row = np.zeros((L, 4, P), np.float32)
    gb, sm = a["ml_gate_b"], a["state_mlstm_m"][0]
    for d in range(2):
        row[:, 0, 32 * d:32 * d + 4] = gb[:, 1, d]
        row[:, 0, 64 + 32 * d:72 + 32 * d] = a["mb_dt_bias"][:, d]
        row[:, 1, 64 + 32 * d:72 + 32 * d] = a["mb_a_log"][:, d]
        row[:, 2, 32 * d:32 * d + 4] = gb[:, 0, d]
        row[:, 3, 32 * d:32 * d + 4] = sm[:, d]
    put("row", row)
    par[:, :, PAR["mbd"]:PAR["mbd"] + 8] = a["mb_d"][:, None, :]
    r["par"] = par
    r["hgrn"] = f(a["state_hgrn"][0].transpose(0, 3, 1, 2, 4))
    cn = np.concatenate([a["state_mlstm_C"][0], a["state_mlstm_n"][0][..., None]], -1)
    r["mlstm"] = f(cn.transpose(0, 3, 1, 2, 4))
    ss = a["state_ssd"][0].reshape(L, 2, 2, 4, SP_, 64)
    r["ssd"] = f(ss.transpose(0, 2, 5, 1, 3, 4).reshape(L, P, 2, 4, SP_))
    return r


OUTS = {"y": (P, KC, T), "hgrn": (L, 2, P, NH, P), "mlstm": (L, 2, NH, P, C1), "m": (L, 2, NH, 1),
        "ssd": (L, 2, P, 4, SP_)}


def returned(o):
    y = o["y"].transpose(2, 1, 0).reshape(T, D)
    hg = o["hgrn"].transpose(0, 1, 3, 2, 4)[None]
    ml = o["mlstm"][None]
    ssd = o["ssd"].reshape(L, 2, 2, 64, 4, SP_).transpose(0, 1, 2, 4, 5, 3).reshape(1, L, 2, SH, SP_, 64)
    return (y[None, :NC_TOK], y[None, NC_TOK:], hg, ml[..., :P], ml[..., P], o["m"].reshape(1, L, 2, NH), ssd)


def kernel(**inputs):
    import concourse.bacc as bacc
    from concourse.bass_utils import run_bass_kernel_spmd

    arrays = {**laid_out(inputs), **constants()}
    nc = bacc.Bacc("TRN2", target_bir_lowering=False, num_devices=1)
    ins = {n: nc.dram_tensor(f"in_{n}", a.shape, mybir.dt.from_np(a.dtype), kind="ExternalInput").ap()
           for n, a in arrays.items()}
    outs = {n: nc.dram_tensor(f"out_{n}", s, F32, kind="ExternalOutput").ap() for n, s in OUTS.items()}
    build(nc, ins, outs)
    r = run_bass_kernel_spmd(nc, [{f"in_{n}": a for n, a in arrays.items()}], core_ids=[0])
    got = returned({n: r.results[0][f"out_{n}"] for n in OUTS})
    return tuple(np.ascontiguousarray(g) for g in got)
```
